# Optimizing a Trainium2 kernel written in Bass

```python
import math
import jax
import jax.numpy as jnp
from jax import lax
import numpy as np

D_MODEL = 4096
BATCH = 1
SEQ = 256
DEPTH = 1

D_MIX = D_MODEL
MLSTM_WIDTH = D_MIX // 2
MLSTM_HEADS = 4
MLSTM_V_DIM = MLSTM_WIDTH // MLSTM_HEADS
MLSTM_QK_DIM = MLSTM_V_DIM // 2
MLSTM_QK_WIDTH = MLSTM_HEADS * MLSTM_QK_DIM
MLSTM_CHUNK = 64
CONV_WIDTH = 4
NSA_WIDTH = D_MIX - MLSTM_WIDTH
NSA_HEAD_DIM = 128
NSA_HEADS = NSA_WIDTH // NSA_HEAD_DIM
NSA_KV_GROUPS = 4
NSA_HPG = NSA_HEADS // NSA_KV_GROUPS
NSA_KV_WIDTH = NSA_KV_GROUPS * NSA_HEAD_DIM
CMP_BLOCK = 32
CMP_STRIDE = 16
SLC_BLOCK = 64
SLC_TOP_N = 16
WINDOW = 512
QUERY_BLOCK = 64
FORCE_BONUS = 1000.0
REL_BUCKETS = 32
REL_MAX_EXACT = REL_BUCKETS // 2
REL_MAX_DISTANCE = 1024
RMS_EPS = 1e-6
NEG_LOGIT = -1e30

SPLIT_SIZES = (
    MLSTM_QK_WIDTH, MLSTM_QK_WIDTH, MLSTM_WIDTH, MLSTM_WIDTH, MLSTM_WIDTH,
    MLSTM_HEADS, MLSTM_HEADS,
    NSA_WIDTH,
    NSA_KV_WIDTH, NSA_KV_WIDTH,
    NSA_KV_WIDTH, NSA_KV_WIDTH,
    NSA_KV_WIDTH, NSA_KV_WIDTH,
    3 * NSA_HEADS,
    NSA_WIDTH,
)
IN_COLS = sum(SPLIT_SIZES)

kernel_name = "hymba_mlstm_nsa_layer"

def _rmsnorm(x, gain):
    xf = x.astype(jnp.float32)
    y = xf * lax.rsqrt(jnp.mean(xf * xf, axis=-1, keepdims=True) + RMS_EPS)
    return (y * gain.astype(jnp.float32)).astype(x.dtype)

def _rel_bucket(dist):
    n = jnp.maximum(dist, 0)
    nf = jnp.maximum(n, REL_MAX_EXACT).astype(jnp.float32)
    large = REL_MAX_EXACT + (jnp.log(nf / REL_MAX_EXACT) / math.log(REL_MAX_DISTANCE / REL_MAX_EXACT)
                             * (REL_BUCKETS - REL_MAX_EXACT)).astype(jnp.int32)
    large = jnp.minimum(large, REL_BUCKETS - 1)
    return jnp.where(n < REL_MAX_EXACT, n, large)

def _causal_conv(u, w):
    c = u.shape[-1]
    return lax.conv_general_dilated(
        u, w[:, None, :].astype(u.dtype), window_strides=(1,), padding=[(CONV_WIDTH - 1, 0)],
        dimension_numbers=("NWC", "WIO", "NWC"), feature_group_count=c)

def _mlstm(q, k, v, i_pre, f_pre):
    b_, t_, nh, dqk = q.shape
    dv = v.shape[-1]
    L = MLSTM_CHUNK
    nc = t_ // L
    k = k * (dqk ** -0.5)
    log_f = jax.nn.log_sigmoid(f_pre)

    def to_chunks(a):
        return a.reshape(b_, nc, L, nh, a.shape[-1]).transpose(1, 0, 3, 2, 4)

    def gate_chunks(a):
        return a.reshape(b_, nc, L, nh).transpose(1, 0, 3, 2)

    causal = jnp.tril(jnp.ones((L, L), dtype=bool))

    def step(carry, inp):
        c_st, n_st, m_st = carry
        qc, kc, vc, ic, lfc = inp
        bcum = jnp.cumsum(lfc, axis=-1)
        g = bcum[..., -1]
        dlog = jnp.where(causal, bcum[..., :, None] - bcum[..., None, :] + ic[..., None, :], -jnp.inf)
        m_inter = bcum + m_st[..., None]
        m_t = jnp.maximum(m_inter, jnp.max(dlog, axis=-1))
        s = jnp.einsum('bhld,bhsd->bhls', qc, kc) * jnp.exp(dlog - m_t[..., None])
        inter = jnp.exp(m_inter - m_t)
        num = jnp.einsum('bhls,bhsv->bhlv', s, vc) + inter[..., None] * jnp.einsum('bhld,bhdv->bhlv', qc, c_st)
        qn = jnp.sum(s, axis=-1) + inter * jnp.einsum('bhld,bhd->bhl', qc, n_st)
        h = num / jnp.maximum(jnp.abs(qn), jnp.exp(-m_t))[..., None]
        w_log = g[..., None] - bcum + ic
        m_next = jnp.maximum(g + m_st, jnp.max(w_log, axis=-1))
        wts = jnp.exp(w_log - m_next[..., None])
        keep = jnp.exp(g + m_st - m_next)
        c_new = keep[..., None, None] * c_st + jnp.einsum('bhl,bhld,bhlv->bhdv', wts, kc, vc)
        n_new = keep[..., None] * n_st + jnp.einsum('bhl,bhld->bhd', wts, kc)
        return (c_new, n_new, m_next), h

    init = (jnp.zeros((b_, nh, dqk, dv), jnp.float32),
            jnp.zeros((b_, nh, dqk), jnp.float32),
            jnp.zeros((b_, nh), jnp.float32))
    xs = (to_chunks(q), to_chunks(k), to_chunks(v), gate_chunks(i_pre), gate_chunks(log_f))
    _, hs = lax.scan(step, init, xs)
    return hs.transpose(1, 0, 3, 2, 4).reshape(b_, t_, nh, dv)

def _compress(blocks, pos, w1, w2):
    hid = jax.nn.silu(jnp.einsum('bnlgd,lde->bnge', blocks + pos[None, None, :, None, :], w1))
    return jnp.einsum('bnge,ef->bngf', hid, w2)

def _nsa(q, ck, cv, sk, sv, wk, wv, gate_pre,
         cmp_k_pos, cmp_k_w1, cmp_k_w2, cmp_v_pos, cmp_v_w1, cmp_v_w2, rel_bias):
    b_, t_, _ = q.shape
    G, HPG, DH = NSA_KV_GROUPS, NSA_HPG, NSA_HEAD_DIM
    scale = DH ** -0.5
    q = q.reshape(b_, t_, G, HPG, DH)
    ck, cv, sk, sv, wk, wv = [a.reshape(b_, t_, G, DH) for a in (ck, cv, sk, sv, wk, wv)]
    tpos = jnp.arange(t_, dtype=jnp.int32)

    n_cmp = (t_ - CMP_BLOCK) // CMP_STRIDE + 1
    blk_idx = np.arange(n_cmp)[:, None] * CMP_STRIDE + np.arange(CMP_BLOCK)[None, :]
    k_cmp = _compress(ck[:, blk_idx], cmp_k_pos, cmp_k_w1, cmp_k_w2)
    v_cmp = _compress(cv[:, blk_idx], cmp_v_pos, cmp_v_w1, cmp_v_w2)
    blk_end = jnp.asarray(np.arange(n_cmp) * CMP_STRIDE + CMP_BLOCK - 1, dtype=jnp.int32)
    dist_c = tpos[:, None] - blk_end[None, :]
    mask_c = dist_c >= 0
    bias_c = rel_bias[_rel_bucket(dist_c)].transpose(2, 0, 1).reshape(G, HPG, t_, n_cmp)
    logit_c = jnp.einsum('btghd,bngd->bghtn', q, k_cmp, preferred_element_type=jnp.float32) * scale + bias_c
    p_c = jax.nn.softmax(jnp.where(mask_c, logit_c, NEG_LOGIT), axis=-1) * mask_c
    o_cmp = jnp.einsum('bghtn,bngd->btghd', p_c.astype(v_cmp.dtype), v_cmp)

    n_slc = t_ // SLC_BLOCK
    cs = np.arange(n_cmp) * CMP_STRIDE
    ss = np.arange(n_slc) * SLC_BLOCK
    cover = np.clip(np.minimum(cs[:, None] + CMP_BLOCK, ss[None, :] + SLC_BLOCK)
                    - np.maximum(cs[:, None], ss[None, :]), 0, None) / CMP_BLOCK
    cover = jnp.asarray(cover, dtype=jnp.float32)
    p_slc = jnp.einsum('bghtn,nj->bgtj', p_c, cover)
    cur = tpos // SLC_BLOCK
    jb = jnp.arange(n_slc, dtype=jnp.int32)
    valid = jb[None, :] <= cur[:, None]
    forced = (jb[None, :] == 0) | (jb[None, :] == cur[:, None]) | (jb[None, :] == cur[:, None] - 1)
    score = jnp.where(valid, p_slc + jnp.where(forced, FORCE_BONUS, 0.0), -1.0)
    n_sel = min(SLC_TOP_N, n_slc)
    _, sel_idx = lax.top_k(score, n_sel)

    ks = sk.reshape(b_, n_slc, SLC_BLOCK, G, DH).transpose(0, 3, 1, 2, 4)
    vs = sv.reshape(b_, n_slc, SLC_BLOCK, G, DH).transpose(0, 3, 1, 2, 4)
    wk_pad = jnp.pad(wk, ((0, 0), (WINDOW, 0), (0, 0), (0, 0)))
    wv_pad = jnp.pad(wv, ((0, 0), (WINDOW, 0), (0, 0), (0, 0)))
    rb = rel_bias.T.reshape(G, HPG, REL_BUCKETS)
    bi = jnp.arange(b_)[:, None, None, None]
    gi = jnp.arange(G)[None, :, None, None]
    gi5 = jnp.arange(G)[None, :, None, None, None]
    hi5 = jnp.arange(HPG)[None, None, :, None, None]
    in_blk = jnp.arange(SLC_BLOCK, dtype=jnp.int32)
    win_off = jnp.arange(QUERY_BLOCK + WINDOW, dtype=jnp.int32)

    def block_fn(qb):
        t0 = qb * QUERY_BLOCK
        q_blk = lax.dynamic_slice_in_dim(q, t0, QUERY_BLOCK, axis=1)
        t_blk = t0 + jnp.arange(QUERY_BLOCK, dtype=jnp.int32)
        sel = lax.dynamic_slice_in_dim(sel_idx, t0, QUERY_BLOCK, axis=2)
        k_sel = ks[bi, gi, sel].reshape(b_, G, QUERY_BLOCK, n_sel * SLC_BLOCK, DH)
        v_sel = vs[bi, gi, sel].reshape(b_, G, QUERY_BLOCK, n_sel * SLC_BLOCK, DH)
        s_pos = (sel[..., None] * SLC_BLOCK + in_blk).reshape(b_, G, QUERY_BLOCK, n_sel * SLC_BLOCK)
        dist_s = t_blk[None, None, :, None] - s_pos
        bias_s = rb[gi5, hi5, _rel_bucket(dist_s)[:, :, None]]
        logit_s = jnp.einsum('bqghd,bgqkd->bghqk', q_blk, k_sel, preferred_element_type=jnp.float32) * scale + bias_s
        p_s = jax.nn.softmax(jnp.where((dist_s >= 0)[:, :, None], logit_s, NEG_LOGIT), axis=-1)
        o_s = jnp.einsum('bghqk,bgqkd->bqghd', p_s.astype(v_sel.dtype), v_sel)
        k_win = lax.dynamic_slice_in_dim(wk_pad, t0, QUERY_BLOCK + WINDOW, axis=1)
        v_win = lax.dynamic_slice_in_dim(wv_pad, t0, QUERY_BLOCK + WINDOW, axis=1)
        w_pos = t0 - WINDOW + win_off
        dist_w = t_blk[:, None] - w_pos[None, :]
        mask_w = (dist_w >= 0) & (dist_w < WINDOW) & (w_pos[None, :] >= 0)
        bias_w = rel_bias[_rel_bucket(dist_w)].transpose(2, 0, 1).reshape(G, HPG, QUERY_BLOCK, QUERY_BLOCK + WINDOW)
        logit_w = jnp.einsum('bqghd,bkgd->bghqk', q_blk, k_win, preferred_element_type=jnp.float32) * scale + bias_w
        p_w = jax.nn.softmax(jnp.where(mask_w, logit_w, NEG_LOGIT), axis=-1)
        o_w = jnp.einsum('bghqk,bkgd->bqghd', p_w.astype(v_win.dtype), v_win)
        return o_s, o_w

    o_slc, o_win = lax.map(block_fn, jnp.arange(t_ // QUERY_BLOCK, dtype=jnp.int32))
    o_slc = o_slc.transpose(1, 0, 2, 3, 4, 5).reshape(b_, t_, G, HPG, DH)
    o_win = o_win.transpose(1, 0, 2, 3, 4, 5).reshape(b_, t_, G, HPG, DH)

    gates = jax.nn.sigmoid(gate_pre.astype(jnp.float32)).reshape(b_, t_, G, HPG, 3)
    o = gates[..., 0:1] * o_cmp + gates[..., 1:2] * o_slc + gates[..., 2:3] * o_win
    return o.reshape(b_, t_, NSA_WIDTH)

def setup_inputs(seed: int = 0) -> dict:
    key = jax.random.key(seed)
    ks = jax.random.split(key, 16)
    nrm = jax.random.normal
    f32 = jnp.float32
    return {
        "x": nrm(ks[0], (BATCH, SEQ, D_MODEL), f32),
        "norm_gain": 1.0 + 0.02 * nrm(ks[1], (D_MODEL,), f32),
        "w_in": nrm(ks[2], (D_MODEL, IN_COLS), f32) * D_MODEL ** -0.5,
        "w_conv": nrm(ks[3], (CONV_WIDTH, 2 * MLSTM_QK_WIDTH), f32) * CONV_WIDTH ** -0.5,
        "b_igate": 0.1 * nrm(ks[4], (MLSTM_HEADS,), f32),
        "b_fgate": 3.0 + 0.5 * nrm(ks[5], (MLSTM_HEADS,), f32),
        "mlstm_norm_gain": 1.0 + 0.02 * nrm(ks[6], (MLSTM_WIDTH,), f32),
        "cmp_k_pos": 0.1 * nrm(ks[7], (CMP_BLOCK, NSA_HEAD_DIM), f32),
        "cmp_k_w1": nrm(ks[8], (CMP_BLOCK, NSA_HEAD_DIM, NSA_HEAD_DIM), f32) * (CMP_BLOCK * NSA_HEAD_DIM) ** -0.5,
        "cmp_k_w2": nrm(ks[9], (NSA_HEAD_DIM, NSA_HEAD_DIM), f32) * NSA_HEAD_DIM ** -0.5,
        "cmp_v_pos": 0.1 * nrm(ks[10], (CMP_BLOCK, NSA_HEAD_DIM), f32),
        "cmp_v_w1": nrm(ks[11], (CMP_BLOCK, NSA_HEAD_DIM, NSA_HEAD_DIM), f32) * (CMP_BLOCK * NSA_HEAD_DIM) ** -0.5,
        "cmp_v_w2": nrm(ks[12], (NSA_HEAD_DIM, NSA_HEAD_DIM), f32) * NSA_HEAD_DIM ** -0.5,
        "rel_bias": 0.5 * nrm(ks[13], (REL_BUCKETS, NSA_HEADS), f32),
        "w_out": nrm(ks[14], (D_MIX, D_MODEL), f32) * D_MIX ** -0.5,
        "final_norm_gain": 1.0 + 0.02 * nrm(ks[15], (D_MODEL,), f32),
    }

def reference(x, norm_gain, w_in, w_conv, b_igate, b_fgate, mlstm_norm_gain,
              cmp_k_pos, cmp_k_w1, cmp_k_w2, cmp_v_pos, cmp_v_w1, cmp_v_w2,
              rel_bias, w_out, final_norm_gain):
    b_, t_, _ = x.shape
    f32 = jnp.float32
    split_points = [int(s) for s in np.cumsum(SPLIT_SIZES)[:-1]]
    for _layer in range(DEPTH):
        h = _rmsnorm(x, norm_gain)
        proj = h @ w_in
        (m_q, m_k, m_v, m_o, m_z, m_i, m_f, a_q, ck, cv, sk, sv, wk, wv, a_gate, a_z) = \
            jnp.split(proj, split_points, axis=-1)

        qk = jax.nn.silu(_causal_conv(jnp.concatenate([m_q, m_k], axis=-1), w_conv))
        mq, mk = jnp.split(qk.astype(f32), 2, axis=-1)
        mq = mq.reshape(b_, t_, MLSTM_HEADS, MLSTM_QK_DIM)
        mk = mk.reshape(b_, t_, MLSTM_HEADS, MLSTM_QK_DIM)
        mv = m_v.astype(f32).reshape(b_, t_, MLSTM_HEADS, MLSTM_V_DIM)
        i_pre = m_i.astype(f32) + b_igate.astype(f32)
        f_pre = m_f.astype(f32) + b_fgate.astype(f32)
        h_m = _mlstm(mq, mk, mv, i_pre, f_pre)
        h_m = jax.nn.sigmoid(m_o.astype(f32)).reshape(b_, t_, MLSTM_HEADS, MLSTM_V_DIM) * h_m
        h_m = h_m * lax.rsqrt(jnp.mean(h_m * h_m, axis=-1, keepdims=True) + RMS_EPS)
        h_m = h_m * mlstm_norm_gain.astype(f32).reshape(MLSTM_HEADS, MLSTM_V_DIM)
        y_m = h_m.reshape(b_, t_, MLSTM_WIDTH) * jax.nn.silu(m_z.astype(f32))

        o_a = _nsa(a_q, ck, cv, sk, sv, wk, wv, a_gate,
                   cmp_k_pos, cmp_k_w1, cmp_k_w2, cmp_v_pos, cmp_v_w1, cmp_v_w2, rel_bias)
        y_a = o_a.astype(f32) * jax.nn.silu(a_z.astype(f32))

        mix = jnp.concatenate([y_m, y_a], axis=-1).astype(x.dtype)
        x = x + mix @ w_out
    return _rmsnorm(x, final_norm_gain)


_drawn_inputs = setup_inputs


def setup_inputs(seed=0):
    import zlib

    import numpy as np

    out = dict(_drawn_inputs(seed))
    spreads = {}
    factors = {'norm_gain': 3.787,
     'b_igate': 8.0,
     'mlstm_norm_gain': 7.184,
     'cmp_k_pos': 8.0,
     'cmp_k_w1': 2.716,
     'cmp_k_w2': 2.771,
     'cmp_v_pos': 5.289,
     'final_norm_gain': 2.826}
    for name, (base, spread) in spreads.items():
        noise = np.random.default_rng([zlib.crc32(name.encode()), seed]).standard_normal(out[name].shape)
        drawn = base * np.exp(spread * noise) if base else spread * noise
        out[name] = jnp.asarray(drawn.astype(out[name].dtype))
    for name, factor in factors.items():
        out[name] = (out[name] * factor).astype(out[name].dtype)
    return out
```

```python
import math
from contextlib import ExitStack

import numpy as np
import concourse.bass as bass
from concourse import mybir

F32 = mybir.dt.float32
F32R = mybir.dt.float32r
ALU = mybir.AluOpType
ACT = mybir.ActivationFunctionType
AX = mybir.AxisListType.X

P = 128
T = 256
TT = T // P
D = 4096
KT_IN = D // P
BW = 512
PAIRS = KT_IN // 2
RING = 4
LOADED = 32
LOOKAHEAD = 3
HEADS_M, QK_M, V_M = 4, 256, 512
GROUPS, HPG, DH = 4, 4, 128
HEADS_A = GROUPS * HPG
N_CMP, CMP_L, CMP_S = 15, 32, 16
BUCKETS = 32
EPS = 1e-6
NEG = -1e30

C_MQ, C_MK, C_MV, C_MO, C_MZ = 0, 1024, 2048, 4096, 6144
C_IF = 8192
C_AQ = 8200
C_KV = 10248
C_GATE = 13320
C_AZ = 13368
N_IF, N_GATE = 2 * HEADS_M, 3 * HEADS_A
N_SMALL = N_IF + N_GATE

B_KV, B_NSA, B_MLSTM, B_OUT = 0, 6, 18, 30
N_OUT = D // BW

UNIT0, UNIT_STEP, UNITS = 19, 3, HPG * TT
TOE = 383


class Count:

    def __init__(self):
        self.base, self.n, self.i, self.per = 0, 0, None, 0

    def enter(self, i, per):
        self.base, self.n, self.i, self.per = self.base + self.n, 0, i, per

    def leave(self, turns):
        assert self.n == self.per, (self.n, self.per)
        self.base, self.n, self.i = self.base + self.per * turns, 0, None

    def value(self):
        v = self.base + self.n
        return v if self.i is None else self.i * self.per + v


def hybrid_layer(nc, x, norm_gain, w_in, w_conv, b_igate, b_fgate, mlstm_norm_gain,
                 cmp_k_pos, cmp_k_w1, cmp_k_w2, cmp_v_pos, cmp_v_w1, cmp_v_w2,
                 rel_bias, w_out, final_norm_gain, const128, const32, const16, out):
    ctx = ExitStack()
    with ctx:
        def sb(name, cols, dt=F32, parts=P):
            return ctx.enter_context(nc.sbuf_tensor(name, [parts, cols], dt))

        def sem(name):
            return ctx.enter_context(nc.semaphore(name))

        def bank(name):
            return ctx.enter_context(nc.psum_tensor(name, [P, 512], F32))

        lhs_hi = sb("lhs_hi", KT_IN * T, F32R)[:, :].rearrange("p (k t) -> p k t", t=T)
        lhs_lo = sb("lhs_lo", KT_IN * T, F32R)[:, :].rearrange("p (k t) -> p k t", t=T)
        w_raw = sb("w_raw", RING * 2 * BW)
        w_hi = sb("w_hi", RING * 2 * BW, F32R)
        w_lo = sb("w_lo", RING * 2 * BW, F32R)

        wide = sb("wide", TT * D)
        x_nat = wide[:, :].rearrange("p (a d) -> p a d", a=TT)
        w1k = wide[:, 0:D].rearrange("p (l e) -> p l e", l=CMP_L)
        w1v = wide[:, D:2 * D].rearrange("p (l e) -> p l e", l=CMP_L)
        mix_a = wide[:, 0:D].rearrange("p (a c) -> p a c", a=TT)
        mix_m = wide[:, D:2 * D].rearrange("p (a c) -> p a c", a=TT)
        res = x_nat

        v_nat = sb("v_nat", 3 * TT * BW)[:, :].rearrange("p (j a c) -> p j a c", j=3, a=TT)
        k_all = sb("k_t", 3 * GROUPS * T)
        k_t = k_all[:, :].rearrange("p (j g t) -> p j g t", j=3, g=GROUPS)
        q_t = k_t[:, 0]
        az = v_nat[:, 0]
        neg_m = k_t[:, 1]
        neg_m_diag = k_t[:, 2]
        qk = v_nat[:, 1].rearrange("p a c -> p (a c)").rearrange("p (c t) -> p c t", t=T)
        qk_sig = v_nat[:, 2].rearrange("p a c -> p (a c)").rearrange("p (c t) -> p c t", t=T)

        multi = sb("multi", D)
        w_small = multi[:, 0:KT_IN * N_SMALL].rearrange("p (k n) -> p k n", n=N_SMALL)
        toe = multi[:, :].rearrange("p (h s) -> p h s", h=HEADS_A)
        mv = multi[:, 0:1024].rearrange("p (a c) -> p a c", a=TT)
        hm = multi[:, 1024:2048].rearrange("p (a c) -> p a c", a=TT)
        PADT = T + 3
        conv_in = multi[:, 2048:2048 + 4 * PADT].rearrange("p (c t) -> p c t", t=PADT)
        wexp = multi[:, 3104:3104 + 384]
        sw = multi[:, 3488:3488 + 384]
        gain_f = multi

        stage = sb("stage", TT * BW)[:, :].rearrange("p (a c) -> p a c", a=TT)
        ebuf_t = sb("ebuf", TT * BW)
        ebuf = ebuf_t[:, :].rearrange("p (a c) -> p a c", a=TT)
        cv_t = ebuf_t[:, :].rearrange("p (g t) -> p g t", t=T)
        lg = sb("lg", 512 + 16)
        lg2 = lg[:, 0:512].rearrange("p (b s) -> p b s", b=2)
        pt = sb("pt", 512)
        pt2 = pt[:, :].rearrange("p (b s) -> p b s", b=2)
        pct = sb("pct", P)
        xres = k_all[:, 0:2 * TT * BW].rearrange("p (n a c) -> p n a c", n=2, a=TT)

        c128 = sb("c128", const128.shape[1])
        ident = c128[:, 0:P]
        tri = c128[:, P:2 * P]
        diag_mask = c128[:, 2 * P:3 * P]
        o = 3 * P
        cmp_neg = c128[:, o:o + TT * N_CMP].rearrange("p (a n) -> p a n", a=TT)
        cmp_01 = c128[:, o + TT * N_CMP:o + 2 * TT * N_CMP].rearrange("p (a n) -> p a n", a=TT)
        hot_up = ebuf_t[0:BUCKETS, 0:511]
        hot_down = ebuf_t[0:BUCKETS, 512:512 + TOE]
        toe_mask = lg[0:HEADS_A, 0:TOE]
        toe_row = pt[0:HEADS_A, 0:TOE]
        rb = sb("rb", HEADS_A, parts=BUCKETS)
        ones = sb("ones", P)
        gain_rows = k_all[0:KT_IN, 16 * P:17 * P]
        gain_t = sb("gain_t", KT_IN)
        pos_rows = k_all[0:CMP_L, 17 * P:19 * P]
        gain_m_rows = k_all[0:KT_IN // 2, 19 * P:20 * P]
        gain_mix = sb("gain_mix", KT_IN)
        pos_t = sb("pos_t", 2 * CMP_L)
        conv_rows = k_all[0:4, 0:16 * P]
        conv_w = sb("conv_w", 16 * 4)[:, :].rearrange("p (c j) -> p c j", j=4)
        w2 = sb("w2", 2 * P)
        b_if = sb("b_if", N_IF)
        ss = sb("ss", TT)
        rstd = sb("rstd", TT)
        nrstd = sb("nrstd", TT)
        m_half = sb("m_half", TT)
        eps_m = sb("eps_m", TT)
        inv_m = sb("inv_m", TT)
        small = sb("small", TT * N_SMALL)[:, :].rearrange("p (a n) -> p a n", a=TT)
        g_sig = sb("g_sig", TT * N_GATE)[:, :].rearrange("p (a n) -> p a n", a=TT)
        hid = pt[:, 384:512]
        hid_e = pct
        hid_b = sb("hid_b", 2)
        k_cmp = sb("k_cmp", GROUPS * N_CMP)[:, :].rearrange("p (g n) -> p g n", n=N_CMP)
        v_cmp = sb("v_cmp", GROUPS * P, parts=N_CMP)[:, :].rearrange("p (g f) -> p g f", f=P)
        bias_c = sb("bias_c", TT * N_CMP * HEADS_A)[:, :].rearrange(
            "p (a n h) -> p a n h", a=TT, h=HEADS_A)
        nmax = sb("nmax", 3)
        rsum = sb("rsum", 3)
        coef = sb("coef", 3)
        f_abs = sb("f_abs", TT * HEADS_M)[:, :].rearrange("p (a h) -> p a h", a=TT)
        log_f = sb("log_f", TT * HEADS_M)[:, :].rearrange("p (a h) -> p a h", a=TT)
        f_cum = sb("f_cum", TT * HEADS_M)[:, :].rearrange("p (a h) -> p a h", a=TT)
        a_col = sb("a_col", TT * HEADS_M)[:, :].rearrange("p (a h) -> p a h", a=TT)
        e_neg_m = sb("e_neg_m", TT * HEADS_M)[:, :].rearrange("p (a h) -> p a h", a=TT)
        a_row = lg[0:4, 0:T]
        m_row = lg[0:4, T:2 * T]
        m_neg = sb("m_neg", TT * HEADS_M)[:, :].rearrange("p (h a) -> p h a", a=TT)
        m_wide = multi[:, 0:8 * P].rearrange("p (i m) -> p i m", m=P)
        den = sb("den", TT)
        ssm = sb("ssm", TT)
        hr = sb("hr", TT)
        ssf = sb("ssf", TT * N_OUT)[:, :].rearrange("p (a n) -> p a n", a=TT)
        fr = sb("fr", TT)
        spare = sb("spare", 8)
        pool_spare = sb("pool_spare", 1)

        acc = [[bank("acc_a0"), bank("acc_a1")], [bank("acc_b0"), bank("acc_b1")]]
        bx, by, bz, bv = bank("bank_x"), bank("bank_y"), bank("bank_z"), bank("bank_v")
        bx2 = bx[:, :].rearrange("p (b s) -> p b s", b=2)
        bz2 = bz[:, :].rearrange("p (b s) -> p b s", b=2)

        toe_dram = nc.dram_tensor("toe_dram", (HEADS_A, P, TOE), F32, kind="Internal")

        x_in = [sem(f"x_in{i}") for i in range(4)]
        consts_in = sem("consts_in")
        w_loaded = [sem(f"w_loaded{i}") for i in range(RING)]
        hi_done = sem("hi_done")
        lo_done = sem("lo_done")
        pe_used = sem("pe_used")
        acc0_full = sem("acc0_full")
        acc0_free = sem("acc0_free")
        acc1_free = sem("acc1_free")
        act_chain = sem("act_chain")
        dve_chain = sem("dve_chain")
        pool_chain = sem("pool_chain")
        ones_set = sem("ones_set")
        pre_pe = sem("pre_pe")
        pre_dve = sem("pre_dve")
        pre_act = sem("pre_act")
        pre_pool = sem("pre_pool")
        ht_ready = sem("ht_ready")
        ht_hi = sem("ht_hi")
        ht_lo = sem("ht_lo")
        toe_out = sem("toe_out")
        toe_in = sem("toe_in")
        w1_in = sem("w1_in")
        ws_in = sem("ws_in")
        tr_v = sem("tr_v")
        tr_x = sem("tr_x")
        tr_v_read = sem("tr_v_read")
        tr_x_read = sem("tr_x_read")
        s_ready = sem("s_ready")
        l_done = sem("l_done")
        e_done = sem("e_done")
        p_done = sem("p_done")
        pt_ready = sem("pt_ready")
        pt_read = sem("pt_read")
        o_ready = sem("o_ready")
        o_done = sem("o_done")
        az_e = sem("az_e")
        az_r = sem("az_r")
        az_mul = sem("az_mul")
        az_free = sem("az_free")
        mz_e = sem("mz_e")
        mz_r = sem("mz_r")
        mz_free = sem("mz_free")
        m_spread = sem("m_spread")
        nm_ready = sem("nm_ready")
        nm_done = sem("nm_done")
        conv_done = sem("conv_done")
        conv_e = sem("conv_e")
        conv_r = sem("conv_r")
        qk_done = sem("qk_done")
        wexp_done = sem("wexp_done")
        st_ready = sem("st_ready")
        sw_done = sem("sw_done")
        num_ready = sem("num_ready")
        hm_done = sem("hm_done")
        mo_e = sem("mo_e")
        ho_done = sem("ho_done")
        ssm_done = sem("ssm_done")
        hr_done = sem("hr_done")
        ym_done = sem("ym_done")
        mt_ready = sem("mt_ready")
        mt_hi = sem("mt_hi")
        mt_lo = sem("mt_lo")
        xr_in = [sem("xr_in0"), sem("xr_in1")]
        out0_free = sem("out0_free")
        out1_free = sem("out1_free")
        sq_done = sem("sq_done")
        gained = sem("gained")
        gf_in = sem("gf_in")
        ssf_sum = sem("ssf_sum")
        fr_done = sem("fr_done")
        y0_done = sem("y0_done")
        y1_done = sem("y1_done")
        stored = sem("stored")

        block = ctx.enter_context(nc.Block())

        N_CONST = 13
        T_CV, T_AQ, T_MQK = 3, 4, 8
        w_small_dram = w_in.rearrange("(k p) n -> p k n", p=P)
        FETCH = 1024

        @block.sync
        def _(sp):
            def fetch_pair(q, c, src):
                if not isinstance(q, int) or q >= RING:
                    sp.wait_ge(lo_done, q - RING + 1)
                s = c % RING
                if isinstance(src, list):
                    for k in range(2):
                        sp.dma_start(w_raw[:, (2 * s + k) * BW:(2 * s + k + 1) * BW], src[k]
                                     ).then_inc(w_loaded[s], LOADED // 2)
                else:
                    sp.dma_start(w_raw[:, s * 2 * BW:(s + 1) * 2 * BW], src
                                 ).then_inc(w_loaded[s], LOADED)

            def rows(w, c):
                return w[c * 2 * P:(c + 1) * 2 * P, :].rearrange("(k p) n -> p k n", p=P)

            def columns(b, col):
                for c in range(PAIRS):
                    fetch_pair(b * PAIRS + c, c, rows(w_in, c)[:, :, bass.ds(col, BW)])

            def fetch_x(i):
                sp.dma_start(x_nat[:, :, i * FETCH:(i + 1) * FETCH],
                             x[0, :, i * FETCH:(i + 1) * FETCH].rearrange("(a p) d -> p a d", p=P)
                             ).then_inc(x_in[i], 16)

            fetch_x(0)
            fetch_x(1)
            for c in range(RING):
                fetch_pair(c, c, rows(w_in, c)[:, :, C_KV:C_KV + BW])
            fetch_x(2)
            fetch_x(3)
            for c in range(RING, PAIRS):
                fetch_pair(c, c, rows(w_in, c)[:, :, C_KV:C_KV + BW])
            columns(1, C_KV + BW)
            with sp.Fori(1, 3) as j:
                columns(2 * j, j * (2 * BW) + C_KV)
                columns(2 * j + 1, j * (2 * BW) + C_KV + BW)
            with sp.Fori(0, GROUPS) as g:
                columns(3 * g + B_NSA, g * BW + C_AQ)
                columns(3 * g + B_NSA + 1, g * BW + C_AZ)
                columns(3 * g + B_NSA + 2, g * BW + C_MZ)
            with sp.Fori(0, HEADS_M) as h:
                for c in range(PAIRS):
                    src = [w_in[(2 * c + k) * P:(2 * c + k + 1) * P, C_MQ:C_MV].rearrange(
                        "p (s n) -> p s n", s=2)[:, :, bass.ds(h * QK_M, QK_M)]
                        for k in range(2)]
                    fetch_pair((3 * h + B_MLSTM) * PAIRS + c, c, src)
                columns(3 * h + B_MLSTM + 1, h * BW + C_MV)
                columns(3 * h + B_MLSTM + 2, h * BW + C_MO)
            with sp.Fori(1, N_OUT + 1) as n:
                for c in range(PAIRS):
                    fetch_pair((n + B_OUT - 1) * PAIRS + c, c,
                               rows(w_out, (c + PAIRS // 2) % PAIRS)[
                                   :, :, bass.ds(n * BW - BW, BW)])
            y_dram = out[0].rearrange("(a p) d -> p a d", p=P)
            for i in range(4):
                cols = slice(i * FETCH, (i + 1) * FETCH)
                sp.wait_ge(y0_done, i + 1)
                sp.dma_start(y_dram[:, 0, cols], res[:, 0, cols]).then_inc(stored, 16)
                sp.wait_ge(y1_done, i + 1)
                sp.dma_start(y_dram[:, 1, cols], res[:, 1, cols]).then_inc(stored, 16)
            sp.wait_ge(stored, 8 * 16)

        @block.tensor
        def _(pe):
            def pair(b, c, banks, before0=None, before1=None):
                q = b * PAIRS + c
                s = c % RING
                pe.wait_ge(lo_done, q + 1)
                for t in range(TT):
                    wait = (before0, before1)[t]
                    if c == 0 and wait is not None:
                        pe.wait_ge(*wait)
                    for k in range(2):
                        kk = 2 * c + k
                        hi = lhs_hi[:, kk, t * P:(t + 1) * P]
                        lo = lhs_lo[:, kk, t * P:(t + 1) * P]
                        cols = slice((2 * s + k) * BW, (2 * s + k + 1) * BW)
                        pe.matmul(banks[t][:, :], hi, w_hi[:, cols], start=(kk == 0), stop=False)
                        pe.matmul(banks[t][:, :], hi, w_lo[:, cols], start=False, stop=False)
                        last = pe.matmul(banks[t][:, :], lo, w_hi[:, cols], start=False,
                                         stop=(kk == KT_IN - 1))
                    if c == PAIRS - 1 and t == 0:
                        last.then_inc(acc0_full, 1)
                last.then_inc(pe_used, 1)

            def stream(b, banks, pieces, since):
                for c in range(PAIRS):
                    for piece in pieces.get(c, ()):
                        piece()
                    if since is None:
                        pair(b, c, banks)
                    else:
                        pair(b, c, banks, (acc0_free, since + 1), (acc1_free, since + 1))

            def transpose_stage(event, b, src=None):
                src = stage if src is None else src
                pe.wait_ge(acc0_free, b + 2)
                pe.wait_ge(acc1_free, b + 2)
                for half, (bk, read, done) in enumerate(((bv, tr_v_read, tr_v),
                                                         (bx, tr_x_read, tr_x))):
                    pe.wait_ge(read, event + 1)
                    for c in range(2):
                        for t in range(TT):
                            cc = 2 * half + c
                            last = pe.transpose(bk[:, c * T + t * P:c * T + (t + 1) * P],
                                                src[:, t, cc * P:(cc + 1) * P], ident)
                    last.then_inc(done, 1)

            pe.wait_ge(consts_in, 16 * N_CONST)
            pe.transpose(bx[:, 0:KT_IN], gain_rows, ident[0:KT_IN, 0:KT_IN])
            for i in range(2):
                last = pe.transpose(bx[:, (1 + i) * CMP_L:(2 + i) * CMP_L],
                                    pos_rows[:, i * P:(i + 1) * P], ident[0:CMP_L, 0:CMP_L])
            pe.transpose(bx[:, 192:192 + KT_IN // 2], gain_m_rows, ident[0:KT_IN // 2, 0:KT_IN // 2])
            for c in range(16):
                last = pe.transpose(bx[:, 128 + 4 * c:132 + 4 * c],
                                    conv_rows[:, c * P:(c + 1) * P], ident[0:4, 0:4])
            last.then_inc(pre_pe, 1)
            pe.matmul(by[0:HEADS_A, 0:TOE], rb[:, :], hot_down, start=True,
                      stop=True).then_inc(pre_pe, 1)
            for t in range(TT):
                bk = (bz, bv)[t]
                for n in range(N_CMP):
                    at = 255 + t * P - (CMP_S * n + CMP_L - 1)
                    last = pe.matmul(bk[:, n * HEADS_A:(n + 1) * HEADS_A],
                                     hot_up[:, at:at + P], rb[:, :], start=True, stop=True)
            last.then_inc(pre_pe, 1)
            pe.wait_ge(pre_act, 1)
            pe.transpose(bx[0:P, 0:P], ident, ident).then_inc(tr_x, 1)

            def x_t(c):
                bk = acc[1][c % 2]
                if c % 4 == 0:
                    pe.wait_ge(x_in[c // 4], 16)
                if c >= 2:
                    pe.wait_ge(ht_lo, c - 1)
                for k in range(2):
                    for t in range(TT):
                        last = pe.transpose(bk[:, k * T + t * P:k * T + (t + 1) * P],
                                            x_nat[:, t, (2 * c + k) * P:(2 * c + k + 1) * P], ident)
                last.then_inc(ht_ready, 1)

            def kv(j, b):
                if j is not None:
                    stream(b, acc[0], {}, b)
                stream(b + 1, acc[1], {1: [lambda: transpose_stage(0 if j is None else j, b)]}, b)

            x_t(0)
            x_t(1)
            for c in range(PAIRS):
                pe.wait_ge(ht_lo, c + 1)
                pair(0, c, acc[0])
                if c + 2 < PAIRS:
                    x_t(c + 2)
            kv(None, 0)
            with pe.Fori(1, 3) as j:
                kv(j, 2 * j)

            transpose_stage(T_CV, 5, v_nat[:, 0])
            pe.wait_ge(w1_in, 32)
            pe.wait_ge(tr_v_read, 5)
            pe.wait_ge(tr_x_read, 5)
            for i, (bk, w1, src) in enumerate(((by, w1k, k_t[:, 0]), (bz, w1v, cv_t))):
                for l in range(CMP_L):
                    pe.matmul(bk[:, 0:GROUPS * N_CMP], w1[:, l, :],
                              src[:, :, l:l + CMP_S * (N_CMP - 1) + 1:CMP_S],
                              start=(l == 0), stop=(l == CMP_L - 1))
                for l in range(CMP_L):
                    last = pe.matmul(bk[:, 64:65], w1[:, l, :],
                                     pos_t[:, i * CMP_L + l:i * CMP_L + l + 1],
                                     start=(l == 0), stop=(l == CMP_L - 1))
                last.then_inc(pre_pe, 1)
            pe.wait_ge(ws_in, 32)
            for t in range(TT):
                for k in range(KT_IN):
                    for part in (lhs_hi, lhs_lo):
                        last = pe.matmul(bv[:, t * 64:t * 64 + N_SMALL],
                                         part[:, k, t * P:(t + 1) * P].bitcast(F32),
                                         w_small[:, k, :], start=(k == 0 and part is lhs_hi),
                                         stop=(k == KT_IN - 1 and part is lhs_lo))
            last.then_inc(pre_pe, 1)
            pe.wait_ge(pre_pool, 4)
            pe.matmul(by[:, 128:128 + GROUPS * N_CMP], w2[:, 0:P], hid[:, 0:GROUPS * N_CMP],
                      start=True, stop=True)
            for g in range(GROUPS):
                last = pe.matmul(bx[0:N_CMP, g * P:(g + 1) * P],
                                 hid[:, 64 + g * N_CMP:64 + (g + 1) * N_CMP], w2[:, P:2 * P],
                                 start=True, stop=True)
            last.then_inc(pre_pe, 1)
            pe.wait_ge(pre_dve, 8)
            pe.matmul(bz[:, 0:4], tri, log_f[:, 0, :], start=True, stop=True)
            pe.matmul(bz[:, 4:8], ones[:, :], log_f[:, 0, :], start=True, stop=False)
            pe.matmul(bz[:, 4:8], tri, log_f[:, 1, :], start=False,
                      stop=True).then_inc(pre_pe, 1)
            pe.wait_ge(pre_dve, 9)
            for t in range(TT):
                last = pe.transpose(bz[0:4, 128 + t * P:128 + (t + 1) * P], a_col[:, t, :], ident)
            last.then_inc(pre_pe, 1)
            pe.wait_ge(pre_dve, 10)
            for t in range(TT):
                last = pe.transpose(bz[:, 8 + 4 * t:12 + 4 * t], m_row[:, t * P:(t + 1) * P],
                                    ident[0:4, 0:4])
            last.then_inc(pre_pe, 1)

            with pe.Fori(0, GROUPS) as g:
                def logits(u):
                    hh, t = divmod(u, TT)
                    n = P * (t + 1)
                    q = q_t[:, hh, t * P:(t + 1) * P]
                    if u == 0:
                        pe.wait_ge(tr_v_read, g + T_AQ + 2)
                        pe.wait_ge(tr_x_read, g + T_AQ + 2)
                    else:
                        pe.wait_ge(l_done, g * UNITS + u)
                    for b in range(2):
                        pe.matmul(bx2[:, b, 0:n], q, k_t[:, 1 + b, :, :].rearrange(
                            "p g t -> p (g t)")[:, bass.ds(g * T, n)], start=True, stop=True)
                    pe.matmul(by[:, 0:N_CMP], q, k_cmp[:, :, :].rearrange("p g n -> p (g n)")[
                        :, bass.ds(g * N_CMP, N_CMP)], start=True, stop=True).then_inc(s_ready, 1)

                def weights_t(u):
                    t = u % TT
                    pe.wait_ge(p_done, g * UNITS + u + 1)
                    for b in range(2):
                        for s in range(t + 1):
                            pe.transpose(bz[:, (2 * b + s) * P:(2 * b + s + 1) * P],
                                         lg2[:, b, s * P:(s + 1) * P], ident)
                    pe.transpose(by[0:N_CMP, P:2 * P], lg[:, 512:512 + N_CMP],
                                 ident).then_inc(pt_ready, 1)

                def values(u):
                    t = u % TT
                    pe.wait_ge(pt_read, g * UNITS + u + 1)
                    for b in range(2):
                        for s in range(t + 1):
                            pe.matmul(bv[:, 0:P], pt[:, (2 * b + s) * P:(2 * b + s + 1) * P],
                                      v_nat[:, 1 + b, s, bass.ds(g * P, P)],
                                      start=(b == 0 and s == 0), stop=False)
                    pe.matmul(bv[:, 0:P], pct[0:N_CMP, :],
                              v_cmp[:, :, :].rearrange("p g f -> p (g f)")[:, bass.ds(g * P, P)],
                              start=False, stop=True).then_inc(o_ready, 1)

                at = {17: [lambda: transpose_stage(g + T_AQ, 3 * g + B_NSA)]}
                for u in range(UNITS):
                    s = UNIT0 + UNIT_STEP * u
                    at.setdefault(s, []).append(lambda u=u: logits(u))
                    at.setdefault(s + 2, []).append(lambda u=u: weights_t(u))
                    at.setdefault(s + 3, []).insert(0, lambda u=u: values(u))
                b = 3 * g + B_NSA
                for n in range(3):
                    pieces = {s - n * PAIRS: f for s, f in at.items()
                              if n * PAIRS <= s < (n + 1) * PAIRS}
                    stream(b + n, acc[n % 2], pieces, b + n - (0 if n == 0 else 1))

            pe.wait_ge(o_done, GROUPS * UNITS)
            pe.wait_ge(m_spread, 1)
            for i in range(HEADS_M * TT):
                last = pe.matmul((by, bz)[i // 4][:, (i % 4) * P:(i % 4 + 1) * P], m_wide[:, i, :],
                                 ident, start=True, stop=True)
            last.then_inc(nm_ready, 1)

            with pe.Fori(0, HEADS_M) as h:
                b = 3 * h + B_MLSTM

                def scores():
                    pe.wait_ge(qk_done, h + 1)
                    pe.wait_ge(tr_x_read, h + T_MQK + 2)
                    for s in range(TT):
                        o0 = 2 * P * s
                        for d in range(2):
                            last = pe.matmul(bx[:, o0:o0 + T - s * P],
                                             qk[:, 2 + d, s * P:(s + 1) * P], qk[:, d, s * P:T],
                                             start=(d == 0), stop=(d == 1))
                    last.then_inc(st_ready, 1)

                def numerator():
                    pe.wait_ge(sw_done, h + 1)
                    pe.wait_ge(acc0_free, b + 3)
                    pe.wait_ge(acc1_free, b + 3)
                    parts = ((0, 0, 0), (1, 0, 1), (1, 1, 2))
                    for t, s, i in parts:
                        pe.matmul((by, bz)[t][:, :], sw[:, i * P:(i + 1) * P], mv[:, s, :],
                                  start=(s == 0), stop=(s == t))
                    for t, s, i in parts:
                        last = pe.matmul(bv[:, t:t + 1], sw[:, i * P:(i + 1) * P], ones[:, 0:1],
                                         start=(s == 0), stop=(s == t))
                    last.then_inc(num_ready, 1)

                stream(b, acc[0], {}, b)
                stream(b + 1, acc[1], {1: [lambda: transpose_stage(h + T_MQK, b)], 11: [scores]}, b)
                stream(b + 2, acc[0], {1: [numerator]}, b + 1)

            def mix_t(c):
                if c < PAIRS // 2:
                    src, col = mix_a, c * 2 * P
                    pe.wait_ge(az_free, GROUPS + 1)
                else:
                    src, col = mix_m, (c - PAIRS // 2) * 2 * P
                    pe.wait_ge(ym_done, (c - PAIRS // 2) // 2 + 1)
                if c >= 2:
                    pe.wait_ge(mt_lo, c - 1)
                for k in range(2):
                    for t in range(TT):
                        last = pe.transpose((by, bz)[c % 2][:, k * T + t * P:k * T + (t + 1) * P],
                                            src[:, t, col + k * P:col + (k + 1) * P], ident)
                last.then_inc(mt_ready, 1)

            pe.wait_ge(hm_done, HEADS_M)
            mix_t(0)
            mix_t(1)
            for c in range(PAIRS):
                pe.wait_ge(mt_lo, c + 1)
                pair(B_OUT, c, acc[1], (acc0_free, B_OUT), (acc1_free, B_OUT))
                if c + 2 < PAIRS:
                    mix_t(c + 2)
            pe.wait_ge(acc0_free, B_OUT + 1)
            pe.wait_ge(acc1_free, B_OUT + 1)
            with pe.Fori(0, 3) as i:
                for n in range(2):
                    for c in range(PAIRS):
                        pair(2 * i + n + B_OUT + 1, c, acc[n], (out0_free, 2 * i + n + 1),
                             (out1_free, 2 * i + n + 1))
            for c in range(PAIRS):
                pair(B_OUT + 7, c, acc[0], (out0_free, 7), (out1_free, 7))

        @block.scalar
        def _(act):
            chain = Count()

            def link(ins):
                chain.n += 1
                ins.then_inc(act_chain, 1)
                act.wait_ge(act_chain, chain.value())

            def slot(b, c):
                s = (c + LOOKAHEAD) % RING
                if isinstance(b, int) and b * PAIRS + c + LOOKAHEAD < RING:
                    pass
                else:
                    act.wait_ge(pe_used, b * PAIRS + (c + LOOKAHEAD - RING + 1))
                act.wait_ge(w_loaded[s], b * (PAIRS // RING * LOADED)
                            + LOADED * ((c + LOOKAHEAD) // RING + 1))
                act.activation(w_hi[:, s * 2 * BW:(s + 1) * 2 * BW],
                               w_raw[:, s * 2 * BW:(s + 1) * 2 * BW], ACT.Copy).then_inc(hi_done, 1)

            def first_split(q):
                act.wait_ge(w_loaded[q], LOADED)
                act.activation(w_hi[:, q * 2 * BW:(q + 1) * 2 * BW],
                               w_raw[:, q * 2 * BW:(q + 1) * 2 * BW], ACT.Copy).then_inc(hi_done, 1)

            loads = [
                (c128[:, :], const128), (ebuf_t[0:BUCKETS, :], const32), (toe_mask, const16),
                (rb[:, :], rel_bias), (gain_m_rows, mlstm_norm_gain.rearrange("(k p) -> k p", p=P)),
                (gain_rows, norm_gain.rearrange("(k p) -> k p", p=P)),
                (pos_rows[:, 0:P], cmp_k_pos), (pos_rows[:, P:2 * P], cmp_v_pos),
                (conv_rows, w_conv), (w2[:, 0:P], cmp_k_w2), (w2[:, P:2 * P], cmp_v_w2),
            ]
            for dst, src in loads:
                act.dma_start(dst, src).then_inc(consts_in, 16)
            for i, src in enumerate((b_igate, b_fgate)):
                act.dma_start(b_if[:, i * HEADS_M:(i + 1) * HEADS_M],
                              src.rearrange("(o n) -> o n", o=1).broadcast_to([P, HEADS_M])
                              ).then_inc(consts_in, 16)
            act.wait_ge(pre_pe, 1)
            act.activation(gain_t[:, :], bx[:, 0:KT_IN], ACT.Copy)
            act.activation(gain_mix[:, KT_IN // 2:KT_IN], bx[:, 192:192 + KT_IN // 2], ACT.Copy)
            act.activation(pos_t[:, :], bx[:, KT_IN:KT_IN + 2 * CMP_L], ACT.Copy)
            act.activation(conv_w.rearrange("p c j -> p (c j)"), bx[:, 128:192],
                           ACT.Copy).then_inc(pre_act, 1)
            act.wait_ge(pre_act, 1)
            def x_hi(c):
                act.wait_ge(ht_ready, c + 1)
                for k in range(2):
                    last = act.activation(lhs_hi[:, 2 * c + k, :],
                                          acc[1][c % 2][:, k * T:(k + 1) * T], ACT.Copy,
                                          scale=gain_t[:, 2 * c + k:2 * c + k + 1])
                last.then_inc(ht_hi, 1)

            act.wait_ge(pre_dve, 2)
            act.dma_start(toe_dram.ap(), toe_row.unsqueeze(1).broadcast_to([HEADS_A, P, TOE])
                          ).then_inc(toe_out, 16)
            act.activation(spare[:, 0:1], gain_t[:, 0:1], ACT.Copy).then_inc(tr_v_read, 1)
            act.activation(spare[:, 1:2], gain_t[:, 0:1], ACT.Copy).then_inc(acc0_free, 1)
            x_hi(0)
            first_split(0)
            x_hi(1)
            first_split(1)
            first_split(2)
            for c in range(PAIRS):
                if c + 2 < PAIRS:
                    x_hi(c + 2)
                slot(0, c)
                if c in (12, 14):
                    t = (c - 12) // 2
                    for i in range(4):
                        act.wait_ge(x_in[i], 16)
                    link(act.activation(multi[:, :], x_nat[:, t, :], ACT.Square,
                                        accum_out=ss[:, t:t + 1]))
            act.activation(spare[:, 2:3], gain_t[:, 0:1], ACT.Copy).then_inc(pre_act, 1)

            for t in range(2):
                src = (cmp_k_w1, cmp_v_w1)[t]
                act.wait_ge(ht_lo, PAIRS)
                act.dma_start((w1k, w1v)[t], src.rearrange("l d e -> d l e")).then_inc(w1_in, 16)
            act.dma_start(w_small[:, :, 0:N_IF], w_small_dram[:, :, C_IF:C_IF + N_IF]
                          ).then_inc(ws_in, 16)
            act.dma_start(w_small[:, :, N_IF:N_SMALL], w_small_dram[:, :, C_GATE:C_GATE + N_GATE]
                          ).then_inc(ws_in, 16)

            def kv(j, b):
                if not isinstance(j, int):
                    for c in range(PAIRS):
                        slot(b, c)
                act.wait_ge(tr_x, j + 1)
                act.wait_ge(pre_pool, 1)
                act.wait_ge(acc0_full, b + 1)
                act.activation(stage[:, 0, :], acc[0][0][:, :], ACT.Copy,
                               scale=rstd[:, 0:1]).then_inc(acc0_free, 1)
                for c in range(PAIRS):
                    slot(b + 1, c)
                    if c == 1:
                        act.wait_ge(tr_v, j + 1)
                        act.activation(k_t[:, bass.ds(j, 1), 0:2, :].rearrange("p o g t -> p (o g t)"),
                                       bv[:, :], ACT.Copy).then_inc(tr_v_read, 1)
                act.wait_ge(acc0_full, b + 2)
                act.activation(v_nat[:, bass.ds(j, 1), 0, :].rearrange("p o c -> p (o c)"),
                               acc[1][0][:, :], ACT.Copy, scale=rstd[:, 0:1]).then_inc(acc0_free, 1)

            kv(0, 0)
            with act.Fori(1, 3) as j:
                kv(j, 2 * j)

            act.wait_ge(tr_v, 4)
            act.activation(cv_t[:, 0:2, :], bv[:, :].rearrange("p (g t) -> p g t", t=T),
                           ACT.Copy).then_inc(tr_v_read, 1)
            act.wait_ge(pre_dve, 3)
            act.activation(hid_e[:, 0:60], hid[:, 0:60], ACT.Exp, scale=-1.0)
            act.activation(hid_e[:, 64:124], hid[:, 64:124], ACT.Exp,
                           scale=-1.0).then_inc(pre_act, 1)
            act.wait_ge(pre_dve, 5)
            act.activation(g_sig[:, :, :], small[:, :, N_IF:], ACT.Exp, scale=-1.0
                           ).then_inc(pre_act, 1)
            link(act.activation(log_f[:, :, :], f_abs[:, :, :], ACT.Exp, scale=-1.0))
            act.activation(log_f[:, :, :], log_f[:, :, :], ACT.Ln, bias=1.0
                           ).then_inc(pre_act, 1)
            act.wait_ge(pre_pe, 6)
            act.wait_ge(toe_out, 16)
            act.dma_start(toe, bass.AP(toe_dram, P - 1, [[TOE - 1, P], [P * TOE, HEADS_A], [1, T]])
                          ).then_inc(toe_in, 16)
            act.wait_ge(pre_dve, 11)
            act.activation(e_neg_m[:, :, :], e_neg_m[:, :, :], ACT.Exp, scale=-1.0
                           ).then_inc(pre_act, 1)

            with act.Fori(0, GROUPS) as g:
                def queries():
                    act.wait_ge(tr_v, g + T_AQ + 1)
                    act.activation(q_t[:, 0:2, :], bv[:, :].rearrange("p (g t) -> p g t", t=T),
                                   ACT.Copy).then_inc(tr_v_read, 1)

                def exponentials(u):
                    n = P * (u % TT + 1)
                    act.wait_ge(l_done, g * UNITS + u + 1)
                    for b in range(2):
                        act.activation(lg2[:, b, 0:n], lg2[:, b, 0:n], ACT.Exp,
                                       bias=nmax[:, 1 + b:2 + b], accum_out=rsum[:, 1 + b:2 + b])
                    act.activation(lg[:, 512:512 + N_CMP], lg[:, 512:512 + N_CMP], ACT.Exp,
                                   bias=nmax[:, 0:1], accum_out=rsum[:, 0:1]).then_inc(e_done, 1)

                def weights_t(u):
                    n = P * (u % TT + 1)
                    act.wait_ge(pt_ready, g * UNITS + u + 1)
                    act.activation(pt2[:, :, 0:n], bz2[:, :, 0:n], ACT.Copy)
                    act.activation(pct[0:N_CMP, :], by[0:N_CMP, P:2 * P],
                                   ACT.Copy).then_inc(pt_read, 1)

                def gate_exp():
                    act.wait_ge(acc1_free, 3 * g + B_NSA + 3)
                    act.wait_ge(acc0_free, 3 * g + B_NSA + 3)
                    act.wait_ge(mz_free, g + 1)
                    act.activation(ebuf[:, :, :], az[:, :, :], ACT.Exp, scale=-1.0
                                   ).then_inc(az_e, 1)

                at = {17: [queries], 32: [gate_exp]}
                for u in range(UNITS):
                    s = UNIT0 + UNIT_STEP * u
                    at.setdefault(s + 1, []).append(lambda u=u: exponentials(u))
                    at.setdefault(s + 2, []).append(lambda u=u: weights_t(u))
                b = 3 * g + B_NSA
                for n in range(3):
                    for c in range(PAIRS):
                        slot(b + n, c)
                        for piece in at.get(n * PAIRS + c, ()):
                            piece()
                    act.wait_ge(acc0_full, b + n + 1)
                    if n == 0:
                        act.wait_ge(tr_x, g + T_AQ + 1)
                        act.wait_ge(mz_free, g + 1)
                        dst = stage[:, 0, :]
                    elif n == 1:
                        act.wait_ge(az_free, g + 1)
                        dst = az[:, 0, :]
                    else:
                        dst = stage[:, 0, :]
                        act.wait_ge(tr_x, g + T_AQ + 2)
                    act.activation(dst, acc[n % 2][0][:, :], ACT.Copy,
                                   scale=rstd[:, 0:1]).then_inc(acc0_free, 1)
                act.wait_ge(acc1_free, b + 4)
                act.wait_ge(acc0_free, b + 4)
                act.wait_ge(az_mul, g + 1)
                act.activation(ebuf[:, :, :], stage[:, :, :], ACT.Exp, scale=-1.0
                               ).then_inc(mz_e, 1)

            with act.Fori(0, HEADS_M) as h:
                b = 3 * h + B_MLSTM

                def conv_inputs():
                    act.wait_ge(tr_v, h + T_MQK + 1)
                    act.activation(conv_in[:, 0:2, 3:PADT], bv[:, :].rearrange(
                        "p (g t) -> p g t", t=T), ACT.Copy).then_inc(tr_v_read, 1)

                def conv_exp():
                    act.wait_ge(conv_done, h + 1)
                    act.activation(qk_sig[:, :, :], qk[:, :, :], ACT.Exp, scale=-1.0
                                   ).then_inc(conv_e, 1)

                def decay():
                    act.wait_ge(nm_done, 1)
                    for i, (s, src) in enumerate(((0, neg_m_diag), (0, neg_m), (1, neg_m_diag))):
                        t = (0, 1, 1)[i]
                        flat = src.rearrange("p h t -> p (h t)")
                        last = act.activation(
                            wexp[:, i * P:(i + 1) * P], flat[:, bass.ds(h * T + t * P, P)], ACT.Exp,
                            bias=a_col.rearrange("p a h -> p (a h)")[
                                :, bass.ds(h + s * HEADS_M, 1)])
                    last.then_inc(wexp_done, 1)

                at = {17: [conv_inputs], 22: [conv_exp], 24: [decay]}
                for n in range(3):
                    for c in range(PAIRS):
                        slot(b + n, c)
                        for piece in at.get(n * PAIRS + c, ()):
                            piece()
                    act.wait_ge(acc0_full, b + n + 1)
                    if n == 0:
                        act.wait_ge(tr_x, h + T_MQK + 1)
                        act.wait_ge(mz_free, GROUPS + 1)
                        act.activation(stage[:, 0, :], acc[0][0][:, :], ACT.Copy,
                                       scale=rstd[:, 0:1]).then_inc(acc0_free, 1)
                    elif n == 1:
                        act.activation(mv[:, 0, :], acc[1][0][:, :], ACT.Copy,
                                       scale=rstd[:, 0:1]).then_inc(acc0_free, 1)
                    else:
                        act.activation(ebuf[:, 0, :], acc[0][0][:, :], ACT.Exp,
                                       scale=nrstd[:, 0:1]).then_inc(acc0_free, 1)
                        act.wait_ge(acc1_free, b + 4)
                        act.activation(ebuf[:, 1, :], stage[:, 1, :], ACT.Exp, scale=-1.0
                                       ).then_inc(mo_e, 1)
                act.wait_ge(ho_done, h + 1)
                for t in range(TT):
                    last = act.activation(ebuf[:, t, :], hm[:, t, :], ACT.Square,
                                          accum_out=ssm[:, t:t + 1])
                last.then_inc(ssm_done, 1)

            x_cols = x[0].rearrange("(a p) d -> p a d", p=P)

            def fetch_residual(n, i):
                act.dma_start(xres[:, i], x_cols[:, :, bass.ds(n * BW, BW)]).then_inc(xr_in[i], 16)

            def squares(n, banks_i):
                act.wait_ge(out1_free, n + 2)
                for t in range(TT):
                    last = act.activation(
                        ebuf[:, t, :], res[:, t, bass.ds(n * BW, BW)], ACT.Square,
                        accum_out=ssf[:, t, bass.ds(n, 1)])
                last.then_inc(sq_done, 1)

            fetch_residual(0, 0)
            fetch_residual(1, 1)
            act.wait_ge(pe_used, B_OUT * PAIRS)
            for c in range(PAIRS):
                act.wait_ge(mt_ready, c + 1)
                for k in range(2):
                    last = act.activation(lhs_hi[:, 2 * c + k, :],
                                          (by, bz)[c % 2][:, k * T:(k + 1) * T], ACT.Copy,
                                          scale=gain_mix[:, 2 * c + k:2 * c + k + 1])
                last.then_inc(mt_hi, 1)
                slot(B_OUT, c)
                if c == 8:
                    act.wait_ge(ym_done, HEADS_M)
                    act.dma_start(gain_f[:, :], final_norm_gain.rearrange("(o n) -> o n", o=1)
                                  .broadcast_to([P, D])).then_inc(gf_in, 16)
            with act.Fori(0, 3) as i:
                for k in range(2):
                    n = 2 * i + k
                    for c in range(PAIRS):
                        slot(n + (B_OUT + 1), c)
                        if c == 2:
                            squares(n, k)
                        if c == 4:
                            fetch_residual(n + 2, k)
            for c in range(PAIRS - LOOKAHEAD):
                slot(B_OUT + 7, c)
                if c == 2:
                    squares(6, 0)
            squares(7, 1)
            act.wait_ge(fr_done, 1)
            act.wait_ge(gained, N_OUT)
            for i in range(4):
                cols = slice(i * FETCH, (i + 1) * FETCH)
                act.activation(res[:, 0, cols], res[:, 0, cols], ACT.Copy,
                               scale=fr[:, 0:1]).then_inc(y0_done, 1)

        @block.vector
        def _(dve):
            chain = Count()

            def link(ins):
                chain.n += 1
                ins.then_inc(dve_chain, 1)
                dve.wait_ge(dve_chain, chain.value())

            def lo(q, s):
                dve.wait_ge(hi_done, q + 1)
                cols = slice(s * 2 * BW, (s + 1) * 2 * BW)
                dve.tensor_tensor(w_lo[:, cols], w_raw[:, cols], w_hi[:, cols].bitcast(F32),
                                  ALU.subtract).then_inc(lo_done, 1)

            def slot(b, c):
                lo(b * PAIRS + (c + LOOKAHEAD), (c + LOOKAHEAD) % RING)

            dve.memset(m_half[:, :], -0.5)
            dve.memset(eps_m[:, :], V_M * EPS)
            dve.memset(inv_m[:, :], 1.0 / V_M)
            dve.memset(gain_mix[:, 0:KT_IN // 2], 1.0)
            dve.memset(ones[:, :], 1.0).then_inc(ones_set, 1)
            dve.wait_ge(pre_pe, 2)
            dve.tensor_tensor(toe_row, by[0:HEADS_A, 0:TOE], toe_mask, ALU.add
                              ).then_inc(pre_dve, 1)
            dve.wait_ge(pre_pe, 3)
            for t in range(TT):
                last = dve.tensor_tensor(
                    bias_c[:, t], (bz, bv)[t][:, 0:N_CMP * HEADS_A].rearrange(
                        "p (n h) -> p n h", h=HEADS_A),
                    cmp_neg[:, t, :].unsqueeze(2).broadcast_to([P, N_CMP, HEADS_A]), ALU.add)
            last.then_inc(pre_dve, 1)
            dve.memset(spare[:, 4:5], 0.0).then_inc(acc1_free, 1)
            dve.memset(spare[:, 5:6], 0.0).then_inc(tr_x_read, 1)

            def x_lo(c):
                dve.wait_ge(ht_hi, c + 1)
                for k in range(2):
                    last = dve.scalar_tensor_tensor(
                        lhs_lo[:, 2 * c + k, :], acc[1][c % 2][:, k * T:(k + 1) * T],
                        gain_t[:, 2 * c + k:2 * c + k + 1], lhs_hi[:, 2 * c + k, :].bitcast(F32),
                        ALU.mult, ALU.subtract)
                last.then_inc(ht_lo, 1)

            x_lo(0)
            lo(0, 0)
            x_lo(1)
            lo(1, 1)
            lo(2, 2)
            for c in range(PAIRS):
                if c + 2 < PAIRS:
                    x_lo(c + 2)
                slot(0, c)

            def kv(j, b):
                if not isinstance(j, int):
                    for c in range(PAIRS):
                        slot(b, c)
                dve.wait_ge(tr_x, j + 1)
                dve.wait_ge(pre_pool, 1)
                dve.wait_ge(pe_used, b * PAIRS + PAIRS)
                dve.tensor_scalar(stage[:, 1, :], acc[0][1][:, :], rstd[:, 1:2], None,
                                  ALU.mult).then_inc(acc1_free, 1)
                for c in range(PAIRS):
                    slot(b + 1, c)
                    if c == 1:
                        dve.wait_ge(tr_x, j + 2)
                        dve.tensor_copy(k_t[:, bass.ds(j, 1), 2:4, :].rearrange(
                            "p o g t -> p (o g t)"), bx[:, :]).then_inc(tr_x_read, 1)
                dve.wait_ge(pe_used, b * PAIRS + 2 * PAIRS)
                dve.tensor_scalar(v_nat[:, bass.ds(j, 1), 1, :].rearrange("p o c -> p (o c)"),
                                  acc[1][1][:, :], rstd[:, 1:2], None,
                                  ALU.mult).then_inc(acc1_free, 1)

            kv(0, 0)
            with dve.Fori(1, 3) as j:
                kv(j, 2 * j)

            dve.wait_ge(tr_x, 5)
            dve.tensor_copy(cv_t[:, 2:4, :], bx[:, :].rearrange("p (g t) -> p g t", t=T)
                            ).then_inc(tr_x_read, 1)
            dve.wait_ge(pre_pe, 5)
            link(dve.tensor_copy(hid_b[:, 0:1], by[:, 64:65]))
            link(dve.tensor_copy(hid_b[:, 1:2], bz[:, 64:65]))
            dve.tensor_scalar(hid[:, 0:60], by[:, 0:60], hid_b[:, 0:1], None, ALU.add)
            dve.tensor_scalar(hid[:, 64:124], bz[:, 0:60], hid_b[:, 1:2], None,
                              ALU.add).then_inc(pre_dve, 1)
            dve.wait_ge(pre_pool, 2)
            dve.reciprocal(hid_e[:, 0:60], hid_e[:, 0:60])
            dve.reciprocal(hid_e[:, 64:124], hid_e[:, 64:124]).then_inc(pre_dve, 1)
            dve.wait_ge(pre_pe, 6)
            for t in range(TT):
                last = dve.tensor_scalar(small[:, t, :], bv[:, t * 64:t * 64 + N_SMALL],
                                         rstd[:, t:t + 1], None, ALU.mult)
            link(last)
            for t in range(TT):
                last = dve.tensor_tensor(small[:, t, 0:N_IF], small[:, t, 0:N_IF], b_if[:, :],
                                         ALU.add)
            link(last)
            dve.scalar_tensor_tensor(f_abs[:, :, :], small[:, :, HEADS_M:N_IF], -1.0,
                                     small[:, :, HEADS_M:N_IF], ALU.mult, ALU.max
                                     ).then_inc(pre_dve, 1)
            dve.wait_ge(pre_act, 4)
            link(dve.tensor_scalar(g_sig[:, :, :], g_sig[:, :, :], 1.0, None, ALU.add))
            dve.reciprocal(g_sig[:, :, :], g_sig[:, :, :]).then_inc(pre_dve, 1)
            dve.wait_ge(pre_pe, 7)
            dve.tensor_copy(k_cmp[:, :, :], by[:, 128:128 + 60].rearrange(
                "p (g n) -> p g n", n=N_CMP))
            dve.tensor_copy(v_cmp[:, :, :], bx[0:N_CMP, :].rearrange("p (g f) -> p g f", f=P)
                            ).then_inc(pre_dve, 1)
            dve.wait_ge(pre_act, 5)
            dve.scalar_tensor_tensor(log_f[:, :, :], small[:, :, HEADS_M:N_IF], 0.0,
                                     log_f[:, :, :], ALU.min, ALU.subtract
                                     ).then_inc(pre_dve, 1)
            dve.wait_ge(pre_pe, 8)
            link(dve.tensor_copy(f_cum[:, :, :], bz[:, 0:8].rearrange("p (a h) -> p a h", a=TT)))
            dve.tensor_tensor(a_col[:, :, :], small[:, :, 0:HEADS_M], f_cum[:, :, :],
                              ALU.subtract).then_inc(pre_dve, 1)
            dve.wait_ge(pre_pe, 9)
            link(dve.tensor_copy(a_row[:, :], bz[0:4, 128:128 + T]))
            dve.tensor_tensor_scan(m_row[:, :], a_row[:, :], a_row[:, :], 0.0, ALU.max,
                                   ALU.max).then_inc(pre_dve, 1)
            dve.wait_ge(pre_pe, 10)
            dve.tensor_scalar(m_neg.rearrange("p h a -> p a h"),
                              bz[:, 8:16].rearrange("p (a h) -> p a h", a=TT), -1.0, None,
                              ALU.mult)
            dve.tensor_tensor(e_neg_m[:, :, :], f_cum[:, :, :],
                              bz[:, 8:16].rearrange("p (a h) -> p a h", a=TT),
                              ALU.add).then_inc(pre_dve, 1)

            with dve.Fori(0, GROUPS) as g:
                chain.enter(g, NSA_LINKS)
                toe_flat = toe.rearrange("p h s -> p (h s)")

                def queries():
                    dve.wait_ge(tr_x, g + T_AQ + 2)
                    dve.tensor_copy(q_t[:, 2:4, :], bx[:, :].rearrange("p (g t) -> p g t", t=T)
                                    ).then_inc(tr_x_read, 1)

                def logits(u):
                    hh, t = divmod(u, TT)
                    n = P * (t + 1)
                    if u == 0:
                        dve.wait_ge(toe_in, 16)
                    dve.wait_ge(s_ready, g * UNITS + u + 1)
                    dve.scalar_tensor_tensor(
                        lg2[:, :, 0:n], bx2[:, :, 0:n], DH ** -0.5,
                        toe_flat[:, bass.ds((g * HPG + hh) * T + (T - n), n)].unsqueeze(1)
                        .broadcast_to([P, 2, n]), ALU.mult, ALU.add)
                    link(dve.scalar_tensor_tensor(
                        lg[:, 512:512 + N_CMP], by[:, 0:N_CMP], DH ** -0.5,
                        bias_c[:, t, :, bass.ds(g * HPG + hh, 1)].rearrange("p n o -> p (n o)"),
                        ALU.mult, ALU.add))
                    dve.tensor_reduce(nmax[:, 1:3], lg2[:, :, 0:n], AX, ALU.max, negate=True)
                    dve.tensor_reduce(nmax[:, 0:1], lg[:, 512:512 + N_CMP], AX, ALU.max,
                                      negate=True).then_inc(l_done, 1)

                def weights(u):
                    hh, t = divmod(u, TT)
                    n = P * (t + 1)
                    dve.wait_ge(e_done, g * UNITS + u + 1)
                    link(dve.reciprocal(coef[:, :], rsum[:, :]))
                    link(dve.tensor_tensor(coef[:, :], coef[:, :], g_sig.rearrange(
                        "p a n -> p (a n)")[:, bass.ds(3 * (g * HPG + hh) + t * N_GATE, 3)],
                        ALU.mult))
                    for b in range(2):
                        dve.tensor_scalar(lg2[:, b, 0:n], lg2[:, b, 0:n], coef[:, 1 + b:2 + b],
                                          None, ALU.mult)
                    dve.scalar_tensor_tensor(lg[:, 512:512 + N_CMP], lg[:, 512:512 + N_CMP],
                                             coef[:, 0:1], cmp_01[:, t, :], ALU.mult, ALU.mult
                                             ).then_inc(p_done, 1)

                def outputs(u):
                    hh, t = divmod(u, TT)
                    dve.wait_ge(o_ready, g * UNITS + u + 1)
                    dve.tensor_copy(mix_a[:, t, bass.ds(g * BW + hh * P, P)],
                                    bv[:, 0:P]).then_inc(o_done, 1)

                def gate():
                    dve.wait_ge(az_e, g + 1)
                    link(dve.tensor_scalar(ebuf[:, :, :], ebuf[:, :, :], 1.0, None, ALU.add))
                    dve.reciprocal(ebuf[:, :, :], ebuf[:, :, :]).then_inc(az_r, 1)

                at = {17: [queries], 33: [gate]}
                for u in range(UNITS):
                    s = UNIT0 + UNIT_STEP * u
                    at.setdefault(s, []).append(lambda u=u: logits(u))
                    at.setdefault(s + 1, []).append(lambda u=u: weights(u))
                    at.setdefault(s + 3, []).insert(0, lambda u=u: outputs(u))
                b = 3 * g + B_NSA
                for n in range(3):
                    for c in range(PAIRS):
                        slot(b + n, c)
                        for piece in at.get(n * PAIRS + c, ()):
                            piece()
                    dve.wait_ge(pe_used, (b + n + 1) * PAIRS)
                    if n == 0:
                        dve.wait_ge(tr_x, g + T_AQ + 1)
                        dve.wait_ge(mz_free, g + 1)
                        dst = stage[:, 1, :]
                    elif n == 1:
                        dve.wait_ge(az_free, g + 1)
                        dst = az[:, 1, :]
                    else:
                        dst = stage[:, 1, :]
                    dve.tensor_scalar(dst, acc[n % 2][1][:, :], rstd[:, 1:2], None,
                                      ALU.mult).then_inc(acc1_free, 1)
                dve.wait_ge(mz_e, g + 1)
                link(dve.tensor_scalar(ebuf[:, :, :], ebuf[:, :, :], 1.0, None, ALU.add))
                dve.reciprocal(ebuf[:, :, :], ebuf[:, :, :]).then_inc(mz_r, 1)
            chain.leave(GROUPS)

            dve.wait_ge(o_ready, GROUPS * UNITS)
            dve.tensor_copy(m_wide, m_neg.rearrange("p h a -> p (h a)").unsqueeze(2)
                            .broadcast_to([P, HEADS_M * TT, P])).then_inc(m_spread, 1)
            dve.wait_ge(nm_ready, 1)
            for i, bk in enumerate((by, bz)):
                v = bk[:, :].rearrange("p (h t) -> p h t", t=T)
                dve.tensor_copy(neg_m[:, 2 * i:2 * i + 2, :], v)
                for hh in range(2):
                    last = dve.tensor_tensor(
                        neg_m_diag[:, 2 * i + hh, :].rearrange("p (a t) -> p a t", a=TT),
                        v[:, hh, :].rearrange("p (a t) -> p a t", a=TT),
                        diag_mask.unsqueeze(1).broadcast_to([P, TT, P]), ALU.add)
            last.then_inc(nm_done, 1)
            link(dve.memset(conv_in[:, :, 0:3], 0.0))

            with dve.Fori(0, HEADS_M) as h:
                chain.enter(h, MLSTM_LINKS)
                b = 3 * h + B_MLSTM

                def conv_inputs():
                    dve.wait_ge(tr_x, h + T_MQK + 2)
                    dve.tensor_copy(conv_in[:, 2:4, 3:PADT], bx[:, :].rearrange(
                        "p (g t) -> p g t", t=T)).then_inc(tr_x_read, 1)

                def conv(j):
                    if j == 0:
                        dve.wait_ge(tr_v_read, h + T_MQK + 2)
                        dve.wait_ge(tr_x_read, h + T_MQK + 2)
                    for c in range(4):
                        w = conv_w.rearrange("p c j -> p (c j)")[
                            :, bass.ds(h * 8 + ((c // 2) * 8 + c % 2) * 4 + j, 1)]
                        if j == 0:
                            last = dve.tensor_scalar(qk[:, c, :], conv_in[:, c, 0:T], w, None,
                                                     ALU.mult)
                        else:
                            last = dve.scalar_tensor_tensor(
                                qk[:, c, :], conv_in[:, c, j:j + T], w, qk[:, c, :], ALU.mult,
                                ALU.add)
                    if j < 3:
                        link(last)
                    else:
                        last.then_inc(conv_done, 1)

                def conv_sigmoid():
                    dve.wait_ge(conv_e, h + 1)
                    link(dve.tensor_scalar(qk_sig[:, :, :], qk_sig[:, :, :], 1.0, None, ALU.add))
                    dve.reciprocal(qk_sig[:, :, :], qk_sig[:, :, :]).then_inc(conv_r, 1)

                def scores():
                    dve.wait_ge(st_ready, h + 1)
                    dve.wait_ge(wexp_done, h + 1)
                    dve.scalar_tensor_tensor(sw, bx[:, 0:384], QK_M ** -0.5, wexp, ALU.mult,
                                             ALU.mult).then_inc(sw_done, 1)

                def normalise(t):
                    if t == 0:
                        dve.wait_ge(num_ready, h + 1)
                        link(dve.tensor_copy(den[:, :], bv[:, 0:TT]))
                        link(dve.scalar_tensor_tensor(den[:, :], den[:, :], -1.0, den[:, :],
                                                      ALU.mult, ALU.max))
                        link(dve.tensor_tensor(den[:, :], den[:, :], e_neg_m[
                            :, :, bass.ds(h, 1)].rearrange("p a o -> p (a o)"), ALU.max))
                        link(dve.reciprocal(den[:, :], den[:, :]))
                    last = dve.tensor_scalar(hm[:, t, :], (by, bz)[t][:, :], den[:, t:t + 1], None,
                                             ALU.mult)
                    if t == 1:
                        last.then_inc(hm_done, 1)

                at = {17: [conv_inputs], 23: [conv_sigmoid], 27: [scores],
                      34: [lambda: normalise(0)], 35: [lambda: normalise(1)]}
                for j in range(4):
                    at[18 + j] = [lambda j=j: conv(j)]
                for n in range(3):
                    for c in range(PAIRS):
                        slot(b + n, c)
                        for piece in at.get(n * PAIRS + c, ()):
                            piece()
                    dve.wait_ge(pe_used, (b + n + 1) * PAIRS)
                    if n == 0:
                        dve.wait_ge(tr_x, h + T_MQK + 1)
                        dve.wait_ge(mz_free, GROUPS + 1)
                        dst = stage[:, 1, :]
                    elif n == 1:
                        dst = mv[:, 1, :]
                    else:
                        dst = stage[:, 1, :]
                    dve.tensor_scalar(dst, acc[n % 2][1][:, :], rstd[:, 1:2], None,
                                      ALU.mult).then_inc(acc1_free, 1)
                dve.wait_ge(mo_e, h + 1)
                link(dve.tensor_scalar(ebuf[:, :, :], ebuf[:, :, :], 1.0, None, ALU.add))
                link(dve.reciprocal(ebuf[:, :, :], ebuf[:, :, :]))
                dve.wait_ge(hm_done, h + 1)
                dve.tensor_tensor(hm[:, :, :], hm[:, :, :], ebuf[:, :, :],
                                  ALU.mult).then_inc(ho_done, 1)
                dve.wait_ge(hr_done, h + 1)
                for t in range(TT):
                    dst = mix_m[:, t, bass.ds(h * BW, BW)]
                    last = dve.scalar_tensor_tensor(dst, hm[:, t, :], hr[:, t:t + 1], dst,
                                                    ALU.mult, ALU.mult)
                last.then_inc(ym_done, 1)
            chain.leave(HEADS_M)

            dve.memset(spare[:, 6:7], 0.0).then_inc(out0_free, 1)
            dve.memset(spare[:, 7:8], 0.0).then_inc(out1_free, 1)
            for c in range(PAIRS):
                dve.wait_ge(mt_hi, c + 1)
                for k in range(2):
                    last = dve.scalar_tensor_tensor(
                        lhs_lo[:, 2 * c + k, :], (by, bz)[c % 2][:, k * T:(k + 1) * T],
                        gain_mix[:, 2 * c + k:2 * c + k + 1], lhs_hi[:, 2 * c + k, :].bitcast(F32),
                        ALU.mult, ALU.subtract)
                last.then_inc(mt_lo, 1)
                slot(B_OUT, c)

            def add_residual(n, i, turn):
                cols = bass.ds(n * BW, BW)
                dve.wait_ge(acc0_full, n + (B_OUT + 1))
                dve.wait_ge(xr_in[i], turn)
                dve.tensor_tensor(res[:, 0, cols], banks[0][:, :], xres[:, i, 0, :],
                                  ALU.add).then_inc(out0_free, 1)
                dve.wait_ge(pe_used, (n + (B_OUT + 1)) * PAIRS)
                dve.tensor_tensor(res[:, 1, cols], banks[1][:, :], xres[:, i, 1, :],
                                  ALU.add).then_inc(out1_free, 1)

            banks = acc[1]
            add_residual(0, 0, 16)
            with dve.Fori(0, 3) as i:
                for k in range(2):
                    for c in range(PAIRS):
                        slot(2 * i + k + (B_OUT + 1), c)
                    banks = acc[k]
                    add_residual(2 * i + k + 1, 1 - k, i * 16 + 16 * (1 + k))
            for c in range(PAIRS - LOOKAHEAD):
                slot(B_OUT + 7, c)
            banks = acc[0]
            add_residual(7, 1, 64)
            dve.wait_ge(sq_done, N_OUT)
            dve.tensor_reduce(ss[:, :], ssf[:, :, :], AX, ALU.add).then_inc(ssf_sum, 1)
            dve.wait_ge(fr_done, 1)
            dve.wait_ge(gained, N_OUT)
            for i in range(4):
                cols = slice(i * FETCH, (i + 1) * FETCH)
                dve.tensor_scalar(res[:, 1, cols], res[:, 1, cols], fr[:, 1:2], None,
                                  ALU.mult).then_inc(y1_done, 1)

        @block.gpsimd
        def _(pool):
            chain = Count()

            def link(ins):
                chain.n += 1
                ins.then_inc(pool_chain, 1)
                pool.wait_ge(pool_chain, chain.value())

            def rsqrt_mean(dst, src, n):
                link(pool.tensor_scalar(dst[:, :], src[:, :], 1.0 / n, EPS, ALU.mult, ALU.add))
                return pool.tensor_tensor(dst[:, :], dst[:, :], m_half[:, :], ALU.pow)

            pool.memset(spare[:, 3:4], 0.0).then_inc(az_free, 1)
            pool.memset(pool_spare[:, :], 0.0).then_inc(mz_free, 1)
            pool.wait_ge(ones_set, 1)
            pool.wait_ge(pre_act, 2)
            link(rsqrt_mean(rstd, ss, D))
            pool.tensor_scalar(nrstd[:, :], rstd[:, :], -1.0, None, ALU.mult
                               ).then_inc(pre_pool, 1)
            pool.wait_ge(pre_act, 3)
            pool.tensor_scalar(hid_e[:, 0:60], hid_e[:, 0:60], 1.0, None, ALU.add)
            pool.tensor_scalar(hid_e[:, 64:124], hid_e[:, 64:124], 1.0, None, ALU.add
                               ).then_inc(pre_pool, 1)
            pool.wait_ge(pre_dve, 4)
            pool.tensor_tensor(hid[:, 0:60], hid[:, 0:60], hid_e[:, 0:60], ALU.mult
                               ).then_inc(pre_pool, 1)
            pool.tensor_tensor(hid[:, 64:124], hid[:, 64:124], hid_e[:, 64:124], ALU.mult
                               ).then_inc(pre_pool, 1)

            with pool.Fori(0, GROUPS) as g:
                pool.wait_ge(az_r, g + 1)
                pool.tensor_tensor(az[:, :, :], az[:, :, :], ebuf[:, :, :], ALU.mult
                                   ).then_inc(az_mul, 1)
                pool.wait_ge(az_mul, g + 1)
                pool.wait_ge(o_done, g * UNITS + UNITS)
                dst = mix_a[:, :, bass.ds(g * BW, BW)]
                pool.tensor_tensor(dst, dst, az[:, :, :], ALU.mult).then_inc(az_free, 1)
                pool.wait_ge(mz_r, g + 1)
                dst = mix_m[:, :, bass.ds(g * BW, BW)]
                pool.tensor_tensor(dst, stage[:, :, :], ebuf[:, :, :], ALU.mult
                                   ).then_inc(mz_free, 1)

            with pool.Fori(0, HEADS_M) as h:
                chain.enter(h, 2)
                pool.wait_ge(conv_r, h + 1)
                pool.tensor_tensor(qk[:, :, :], qk[:, :, :], qk_sig[:, :, :], ALU.mult
                                   ).then_inc(qk_done, 1)
                pool.wait_ge(ssm_done, h + 1)
                link(pool.tensor_tensor(hr[:, :], ssm[:, :], eps_m[:, :], ALU.add))
                link(pool.tensor_tensor(hr[:, :], hr[:, :], inv_m[:, :], ALU.mult))
                pool.tensor_tensor(hr[:, :], hr[:, :], m_half[:, :], ALU.pow).then_inc(hr_done, 1)
            chain.leave(HEADS_M)

            pool.wait_ge(gf_in, 16)
            with pool.Fori(0, N_OUT) as n:
                pool.wait_ge(sq_done, n + 1)
                for t in range(TT):
                    dst = res[:, t, bass.ds(n * BW, BW)]
                    last = pool.tensor_tensor(dst, dst, gain_f[:, bass.ds(n * BW, BW)], ALU.mult)
                last.then_inc(gained, 1)
            pool.wait_ge(ssf_sum, 1)
            rsqrt_mean(fr, ss, D).then_inc(fr_done, 1)


NSA_LINKS = 3 * UNITS + 2
MLSTM_LINKS = 3 + 1 + 4 + 2


def shape_constants():
    s, t = np.arange(P)[:, None], np.arange(P)[None, :]
    tri = (s <= t).astype(np.float32)
    end = np.arange(N_CMP) * CMP_S + CMP_L - 1
    seen = (np.arange(T)[:, None] >= end[None, :]).astype(np.float32)
    seen = seen.reshape(TT, P, N_CMP).transpose(1, 0, 2).reshape(P, TT * N_CMP)
    const128 = np.concatenate([np.eye(P, dtype=np.float32), tri,
                               np.where(tri > 0, np.float32(0), np.float32(NEG)),
                               np.where(seen > 0, np.float32(0), np.float32(NEG)), seen], axis=1)
    n = np.arange(T)
    exact = BUCKETS // 2
    nf = np.maximum(n, exact).astype(np.float32)
    large = exact + (np.log(nf / np.float32(exact)) / np.float32(math.log(1024 / exact))
                     * np.float32(BUCKETS - exact)).astype(np.int32)
    bucket = np.where(n < exact, n, np.minimum(large, BUCKETS - 1))
    const32 = np.zeros((BUCKETS, 1024), np.float32)
    const32[bucket, 255 + n] = 1
    const32[bucket, 512 + 255 - n] = 1
    const16 = np.zeros((HEADS_A, TOE), np.float32)
    const16[:, T:] = NEG
    return const128.astype(np.float32), const32, const16


def kernel(x, norm_gain, w_in, w_conv, b_igate, b_fgate, mlstm_norm_gain,
           cmp_k_pos, cmp_k_w1, cmp_k_w2, cmp_v_pos, cmp_v_w1, cmp_v_w2,
           rel_bias, w_out, final_norm_gain):
    import concourse.bacc as bacc
    from concourse.bass_utils import run_bass_kernel_spmd

    const128, const32, const16 = shape_constants()
    arrays = dict(x=x, norm_gain=norm_gain, w_in=w_in, w_conv=w_conv, b_igate=b_igate,
                  b_fgate=b_fgate, mlstm_norm_gain=mlstm_norm_gain, cmp_k_pos=cmp_k_pos,
                  cmp_k_w1=cmp_k_w1, cmp_k_w2=cmp_k_w2, cmp_v_pos=cmp_v_pos, cmp_v_w1=cmp_v_w1,
                  cmp_v_w2=cmp_v_w2, rel_bias=rel_bias, w_out=w_out,
                  final_norm_gain=final_norm_gain, const128=const128, const32=const32,
                  const16=const16)
    nc = bacc.Bacc("TRN2", target_bir_lowering=False, num_devices=1)
    feed, args = {}, []
    for name, a in arrays.items():
        a = np.ascontiguousarray(a)
        feed[f"in_{name}"] = a
        args.append(nc.dram_tensor(f"in_{name}", a.shape, mybir.dt.from_np(a.dtype),
                                   kind="ExternalInput").ap())
    out = nc.dram_tensor("out_y", (1, T, D), F32, kind="ExternalOutput").ap()
    hybrid_layer(nc, *args, out)
    r = run_bass_kernel_spmd(nc, [feed], core_ids=[0])
    return r.results[0]["out_y"]
```

```python
import math
from contextlib import ExitStack

import numpy as np
import concourse.bass as bass
from concourse import mybir

F32 = mybir.dt.float32
F32R = mybir.dt.float32r
ALU = mybir.AluOpType
ACT = mybir.ActivationFunctionType
AX = mybir.AxisListType.X

P = 128
T = 256
TT = T // P
D = 4096
KT_IN = D // P
BW = 512
PAIRS = KT_IN // 2
RING = 4
LOADED = 32
LOOKAHEAD = 3
HEADS_M, QK_M, V_M = 4, 256, 512
GROUPS, HPG, DH = 4, 4, 128
HEADS_A = GROUPS * HPG
N_CMP, CMP_L, CMP_S = 15, 32, 16
BUCKETS = 32
EPS = 1e-6
NEG = -1e30

C_MQ, C_MK, C_MV, C_MO, C_MZ = 0, 1024, 2048, 4096, 6144
C_IF = 8192
C_AQ = 8200
C_KV = 10248
C_GATE = 13320
C_AZ = 13368
N_IF, N_GATE = 2 * HEADS_M, 3 * HEADS_A
N_SMALL = N_IF + N_GATE

B_KV, B_Q0, B_NSA, B_MLSTM, B_OUT = 0, 6, 7, 15, 30
N_OUT = D // BW
SMALL_PAIRS, CMP_PAIRS = 4, 4
EXTRA = SMALL_PAIRS + 2 * CMP_PAIRS
SMALL_K = KT_IN // SMALL_PAIRS
CMP_PL = CMP_L // CMP_PAIRS
MIXED = 2


def mixed_block():
    steps = []
    for c in range(PAIRS):
        if c < EXTRA:
            steps.append((c, None))
        steps.append((None, c))
    return [(MIXED * PAIRS + j, *step) for j, step in enumerate(steps)]

UNIT0, UNIT_STEP, UNITS = 3, 3, HPG * TT
TOE = 383
NP16 = 16
CPAD = T + NP16


MIX_EARLY, MIX_LATE = PAIRS - 2, 11


class Count:

    def __init__(self):
        self.base, self.n, self.i, self.per = 0, 0, None, 0

    def enter(self, i, per):
        self.base, self.n, self.i, self.per = self.base + self.n, 0, i, per

    def leave(self, turns):
        assert self.n == self.per, (self.n, self.per)
        self.base, self.n, self.i = self.base + self.per * turns, 0, None

    def value(self):
        v = self.base + self.n
        return v if self.i is None else self.i * self.per + v


def flat(ap):
    return ap.rearrange("p a b -> p (a b)")


def hybrid_layer(nc, x, norm_gain, w_in, w_conv, b_igate, b_fgate, mlstm_norm_gain,
                 cmp_k_pos, cmp_k_w1, cmp_k_w2, cmp_v_pos, cmp_v_w1, cmp_v_w2,
                 rel_bias, w_out, final_norm_gain, const128, const32, const16, out):
    ctx = ExitStack()
    with ctx:
        def sb(name, cols, dt=F32, parts=P):
            return ctx.enter_context(nc.sbuf_tensor(name, [parts, cols], dt))

        def sem(name):
            return ctx.enter_context(nc.semaphore(name))

        def bank(name):
            return ctx.enter_context(nc.psum_tensor(name, [P, 512], F32))

        lhs_hi = sb("lhs_hi", KT_IN * T, F32R)[:, :].rearrange("p (k t) -> p k t", t=T)
        lhs_lo = sb("lhs_lo", KT_IN * T, F32R)[:, :].rearrange("p (k t) -> p k t", t=T)
        w_raw = sb("w_raw", RING * 2 * BW)
        w_hi = sb("w_hi", RING * 2 * BW, F32R)
        w_lo = sb("w_lo", RING * 2 * BW, F32R)

        KIB = 1024
        arena_start = (nc.sbuf_base + 31) // 32 * 32
        sb("arena", (32 * KIB + 55552) // 4)

        def at(name, kib, cols, dt=F32, parts=P):
            return nc.alloc_sbuf_tensor_at(name, [parts, cols], dt,
                                           offset=arena_start + int(kib * KIB))

        wide = at("wide", 0, TT * D)
        x_nat = wide[:, :].rearrange("p (a d) -> p a d", a=TT)
        mix_a = wide[:, 0:D].rearrange("p (a c) -> p a c", a=TT)
        mix_m = wide[:, D:2 * D].rearrange("p (a c) -> p a c", a=TT)
        res = x_nat
        cin = []
        for i, kind in enumerate("kv"):
            cin.append([at(f"cmp_{kind}_{part}", (2 * i + j) * 5.5, 5 * CPAD, F32R)[:, :].rearrange(
                "p (g t) -> p g t", t=CPAD) for j, part in enumerate(("hi", "lo"))])
        k_hi, k_lo = [at(n, 16 + 8 * i, 2 * GROUPS * T, F32R)[:, :].rearrange(
            "p (j g t) -> p j g t", j=2, g=GROUPS) for i, n in enumerate(("k_hi", "k_lo"))]

        Z = 32
        stage = at("stage", Z, TT * BW)[:, :].rearrange("p (a c) -> p a c", a=TT)
        ebuf = at("ebuf", Z + 4, TT * BW)[:, :].rearrange("p (a c) -> p a c", a=TT)
        gate_buf = at("gate_buf", Z + 8, TT * BW)[:, :].rearrange("p (a c) -> p a c", a=TT)
        toe = at("toe", Z + 12, HPG * T)
        v_hi, v_lo = [at(n, Z + 16 + 8 * i, 2 * TT * BW, F32R)[:, :].rearrange(
            "p (j a c) -> p j a c", j=2, a=TT) for i, n in enumerate(("v_hi", "v_lo"))]
        q_hi, q_lo = [at(n, Z + 32 + 4 * i, HPG * T, F32R)[:, :].rearrange(
            "p (h t) -> p h t", t=T) for i, n in enumerate(("q_hi", "q_lo"))]
        lgs = [at(f"lg{i}", Z + 40 + 2.0625 * i, 512 + NP16) for i in range(2)]
        pt_hi, pt_lo = [at(n, Z + 44.25 + 2 * i, 512, F32R) for i, n in enumerate(("pt_hi", "pt_lo"))]
        pct_hi, pct_lo = [at(n, Z + 48.25 + 0.5 * i, P, F32R)
                          for i, n in enumerate(("pct_hi", "pct_lo"))]
        vc_hi, vc_lo = [at(n, Z + 49.25 + 2 * i, GROUPS * P, F32R)
                        for i, n in enumerate(("vc_hi", "vc_lo"))]
        hm = at("hm", Z + 12, TT * BW)[:, :].rearrange("p (a c) -> p a c", a=TT)
        m_wide = at("m_wide", Z + 12, 8 * P)[:, :].rearrange("p (i m) -> p i m", m=P)
        PADT = T + 3
        conv_in = at("conv_in", Z + 16, 4 * PADT)[:, :].rearrange("p (c t) -> p c t", t=PADT)
        qk = at("qk", Z + 20.25, 4 * T)[:, :].rearrange("p (c t) -> p c t", t=T)
        qk_sig = flat(ebuf).rearrange("p (c t) -> p c t", t=T)
        qk_hi, qk_lo = [at(n, Z + 24.25 + 4 * i, 4 * T, F32R)[:, :].rearrange(
            "p (c t) -> p c t", t=T) for i, n in enumerate(("qk_hi", "qk_lo"))]
        mv_hi, mv_lo = [at(n, Z + 32.25 + 4 * i, TT * BW, F32R)[:, :].rearrange(
            "p (a c) -> p a c", a=TT) for i, n in enumerate(("mv_hi", "mv_lo"))]
        neg_m = at("neg_m", Z + 40.25, HEADS_M * T)[:, :].rearrange("p (h t) -> p h t", t=T)
        neg_m_diag = at("neg_m_diag", Z + 44.25, HEADS_M * T)[:, :].rearrange(
            "p (h t) -> p h t", t=T)
        wexp = at("wexp", Z + 48.25, 384)
        sw = at("sw", Z + 49.75, 384)
        sw_hi, sw_lo = [at(n, Z + 51.25 + 1.5 * i, 384, F32R) for i, n in enumerate(("sw_hi", "sw_lo"))]
        gain_f = at("gain_f", Z + 16, D)
        xres = at("xres", Z + 32, 2 * TT * BW)[:, :].rearrange("p (n a c) -> p n a c", n=2, a=TT)
        hot = at("hot", Z + 16, 1024, parts=BUCKETS)
        hot_up, hot_down = hot[:, 0:511], hot[:, 512:512 + TOE]
        toe_mask = at("toe_mask", Z + 20, TOE, parts=HEADS_A)
        toe_row = at("toe_row", Z + 22, TOE, parts=HEADS_A)
        conv_rows = at("conv_rows", Z + 24, 16 * P, parts=4)
        gain_rows = at("gain_rows", Z + 32, P, parts=KT_IN)
        pos_rows = at("pos_rows", Z + 32.5, 2 * P, parts=CMP_L)
        gain_m_rows = at("gain_m_rows", Z + 33.5, P, parts=KT_IN // 2)
        junk = at("junk", Z + 36, 1024)
        hid = at("hid", Z + 40, 2 * 64)
        hid_e = at("hid_e", Z + 40.5, 2 * 64)
        a_row = at("a_row", Z + 41, T, parts=4)
        m_row = at("m_row", Z + 42, T, parts=4)

        c128 = sb("c128", const128.shape[1])
        ident = c128[:, 0:P]
        tri = c128[:, P:2 * P]
        diag_mask = c128[:, 2 * P:3 * P]
        o = 3 * P
        cmp_neg = c128[:, o:o + TT * N_CMP].rearrange("p (a n) -> p a n", a=TT)
        cmp_01 = c128[:, o + TT * N_CMP:o + 2 * TT * N_CMP].rearrange("p (a n) -> p a n", a=TT)
        rb = sb("rb", HEADS_A, parts=BUCKETS)
        ones = sb("ones", P)
        ones_r = sb("ones_r", 2, F32R)
        gain_t = sb("gain_t", KT_IN)
        gain_mix = sb("gain_mix", KT_IN)
        pos_t = sb("pos_t", 2 * CMP_L)
        conv_w = sb("conv_w", 16 * 4)
        w2 = sb("w2", 2 * P)
        b_if = sb("b_if", N_IF)
        ss8 = sb("ss8", TT * 4)[:, :].rearrange("p (a n) -> p a n", a=TT)
        ss = sb("ss", TT)
        rstd = sb("rstd", TT)
        m_half = sb("m_half", TT)
        eps_m = sb("eps_m", TT)
        inv_m = sb("inv_m", TT)

        def by_head(name, n=HEADS_M):
            return sb(name, TT * n)[:, :].rearrange("p (a n) -> p a n", a=TT)

        small = by_head("small", N_SMALL)
        g_sig = by_head("g_sig", N_GATE)
        f_abs, log_f, f_cum = by_head("f_abs"), by_head("log_f"), by_head("f_cum")
        a_col, e_neg_m = by_head("a_col"), by_head("e_neg_m")
        m_neg = sb("m_neg", TT * HEADS_M)[:, :].rearrange("p (h a) -> p h a", a=TT)
        hid_b = sb("hid_b", 2)
        kc_hi, kc_lo = [sb(n, GROUPS * NP16, F32R) for n in ("kc_hi", "kc_lo")]
        bias_c = sb("bias_c", TT * N_CMP * HEADS_A)[:, :].rearrange(
            "p (a n h) -> p a n h", a=TT, h=HEADS_A)
        nmax = sb("nmax", 3)
        rsum = sb("rsum", 3)
        coef = sb("coef", 3)
        den = sb("den", TT)
        ssm = sb("ssm", TT)
        hr = sb("hr", TT)
        ssf = by_head("ssf", N_OUT)
        fr = sb("fr", TT)
        spare = sb("spare", 3)

        acc = [[bank("acc_a0"), bank("acc_a1")], [bank("acc_b0"), bank("acc_b1")]]
        bx, by, bz, bv = bank("bank_x"), bank("bank_y"), bank("bank_z"), bank("bank_v")

        def halves(t):
            return t[:, 0:512].rearrange("p (b s) -> p b s", b=2)

        toe_dram = nc.dram_tensor("toe_dram", (HEADS_A, P, TOE), F32, kind="Internal")

        x_in = [sem(f"x_in{i}") for i in range(8)]
        first_in = sem("first_in")
        consts_in = sem("consts_in")
        w_loaded = [sem(f"w_loaded{i}") for i in range(RING)]
        hi_done = sem("hi_done")
        lo_done = sem("lo_done")
        pe_used = sem("pe_used")
        acc0_full = sem("acc0_full")
        acc0_free = sem("acc0_free")
        acc1_free = sem("acc1_free")
        act_chain = sem("act_chain")
        dve_chain = sem("dve_chain")
        pool_chain = sem("pool_chain")
        pre_pe, pre_dve, pre_act, pre_pool = [sem(f"pre_{e}") for e in ("pe", "dve", "act", "pool")]
        ht_ready = sem("ht_ready")
        ht_hi = sem("ht_hi")
        ht_lo = sem("ht_lo")
        toe_out = sem("toe_out")
        toe_in = sem("toe_in")
        tr_done = sem("tr_done")
        tr_hi = sem("tr_hi")
        tr_lo = sem("tr_lo")
        v_split_hi = sem("v_split_hi")
        v_split_lo = sem("v_split_lo")
        s_ready = sem("s_ready")
        l_done = sem("l_done")
        e_done = sem("e_done")
        p_done = sem("p_done")
        pt_ready = sem("pt_ready")
        pt_hi_done = sem("pt_hi_done")
        pt_lo_done = sem("pt_lo_done")
        o_ready = sem("o_ready")
        o_done = sem("o_done")
        az_e = sem("az_e")
        az_r = sem("az_r")
        az_mul = sem("az_mul")
        az_free = sem("az_free")
        m_spread = sem("m_spread")
        nm_ready = sem("nm_ready")
        nm_done = sem("nm_done")
        conv_done = sem("conv_done")
        conv_e = sem("conv_e")
        conv_r = sem("conv_r")
        qk_done = sem("qk_done")
        qk_hi_done = sem("qk_hi_done")
        qk_lo_done = sem("qk_lo_done")
        wexp_done = sem("wexp_done")
        st_ready = sem("st_ready")
        sw_done = sem("sw_done")
        sw_hi_done = sem("sw_hi_done")
        sw_lo_done = sem("sw_lo_done")
        num_ready = sem("num_ready")
        hm_done = sem("hm_done")
        mo_e = sem("mo_e")
        mo_r = sem("mo_r")
        ho_done = sem("ho_done")
        ssm_done = sem("ssm_done")
        hr_done = sem("hr_done")
        mz_e = sem("mz_e")
        mz_r = sem("mz_r")
        mz_done = sem("mz_done")
        ym_done = sem("ym_done")
        xr_in = [sem("xr_in0"), sem("xr_in1")]
        out0_free = sem("out0_free")
        out1_free = sem("out1_free")
        sq_done = sem("sq_done")
        gained = sem("gained")
        gf_in = sem("gf_in")
        ssf_sum = sem("ssf_sum")
        fr_done = sem("fr_done")
        y0_done = sem("y0_done")
        y1_done = sem("y1_done")
        stored = sem("stored")

        block = ctx.enter_context(nc.Block())

        N_CONST = 11
        XC = 512
        T_CK, T_CV, T_SK, T_WK, T_AQ, T_MQK = 0, 1, 2, 3, 4, 8

        def piece_map(*entries):
            found = {}
            for slot, piece in entries:
                found.setdefault(slot, []).append(piece)
            return found

        @block.sync
        def _(sp):
            extra = 0

            def fetch(q, s, parts):
                if not isinstance(q, int) or q >= RING:
                    sp.wait_ge(lo_done, q - RING + 1)
                for dst, src in parts:
                    sp.dma_start(dst, src).then_inc(w_loaded[s], LOADED // len(parts))

            def slot_of(s, k=0, n=2):
                return w_raw[:, (2 * s + k) * BW:(2 * s + k + n) * BW]

            def rows(w, c):
                return w[c * 2 * P:(c + 1) * 2 * P, :].rearrange("(k p) n -> p k n", p=P)

            def columns(b, col, pairs=range(PAIRS)):
                for c in pairs:
                    fetch(b * PAIRS + (c + extra), c % RING,
                          [(slot_of(c % RING), rows(w_in, c)[:, :, bass.ds(col, BW)])])

            def mlstm_qk(b, h):
                for c in range(PAIRS):
                    fetch(b * PAIRS + (c + extra), c % RING,
                          [(slot_of(c % RING, k, 1), w_in[
                              (2 * c + k) * P:(2 * c + k + 1) * P, C_MQ:C_MV].rearrange(
                              "p (s n) -> p s n", s=2)[:, :, bass.ds(h * QK_M, QK_M)])
                           for k in range(2)])

            def fetch_x(i):
                sp.dma_start(x_nat[:, :, i * XC:(i + 1) * XC],
                             x[0, :, i * XC:(i + 1) * XC].rearrange("(a p) d -> p a d", p=P)
                             ).then_inc(x_in[i], 16)

            fetch_x(0)
            columns(0, C_KV, [0])
            fetch_x(1)
            columns(0, C_KV, [1])
            fetch_x(2)
            columns(0, C_KV, [2])
            fetch_x(3)
            columns(0, C_KV, [3])
            for i in range(4, 8):
                fetch_x(i)
            columns(0, C_KV, range(RING, PAIRS))
            columns(1, C_KV + BW)

            def extra_pair(q, i):
                s = q % RING
                if i < SMALL_PAIRS:
                    dst = slot_of(s)[:, 0:SMALL_K * N_SMALL].rearrange(
                        "p (k n) -> p k n", n=N_SMALL)
                    src = w_in[i * SMALL_K * P:(i + 1) * SMALL_K * P, :].rearrange(
                        "(k p) n -> p k n", p=P)
                    fetch(q, s, [(dst[:, :, 0:N_IF], src[:, :, C_IF:C_IF + N_IF]),
                                 (dst[:, :, N_IF:], src[:, :, C_GATE:C_GATE + N_GATE])])
                else:
                    j, i = divmod(i - SMALL_PAIRS, CMP_PAIRS)
                    fetch(q, s, [(slot_of(s).rearrange("p (l e) -> p l e", e=P),
                                  (cmp_k_w1, cmp_v_w1)[j][i * CMP_PL:(i + 1) * CMP_PL].rearrange(
                                      "l d e -> d l e"))])

            for q, i, c in mixed_block():
                if i is not None:
                    extra_pair(q, i)
                else:
                    fetch(q, q % RING, [(slot_of(q % RING), rows(w_in, c)[
                        :, :, C_KV + MIXED * BW:C_KV + (MIXED + 1) * BW])])
            extra = EXTRA
            for b in range(MIXED + 1, 6):
                columns(b, C_KV + b * BW)
            columns(B_Q0, C_AQ)
            with sp.Fori(0, GROUPS - 1) as g:
                columns(2 * g + B_NSA, g * BW + C_AZ)
                columns(2 * g + B_NSA + 1, g * BW + C_AQ + BW)
            columns(B_MLSTM - 2, C_AZ + 3 * BW)
            mlstm_qk(B_MLSTM - 1, 0)
            with sp.Fori(1, HEADS_M) as h:
                columns(4 * h + B_MLSTM - 4, h * BW + C_MV - BW)
                columns(4 * h + B_MLSTM - 3, h * BW + C_MO - BW)
                columns(4 * h + B_MLSTM - 2, h * BW + C_MZ - BW)
                mlstm_qk(4 * h + B_MLSTM - 1, h)
            for n, col in enumerate((C_MV, C_MO, C_MZ)):
                columns(B_OUT - 3 + n, col + 3 * BW)
            with sp.Fori(1, N_OUT + 1) as n:
                for c in range(PAIRS):
                    fetch((n + B_OUT - 1) * PAIRS + (c + extra), c % RING,
                          [(slot_of(c % RING), rows(w_out, (c + PAIRS // 2) % PAIRS)[
                              :, :, bass.ds(n * BW - BW, BW)])])
            y_dram = out[0].rearrange("(a p) d -> p a d", p=P)
            for i in range(4):
                cols = slice(i * 1024, (i + 1) * 1024)
                sp.wait_ge(y0_done, i + 1)
                sp.dma_start(y_dram[:, 0, cols], res[:, 0, cols]).then_inc(stored, 16)
                sp.wait_ge(y1_done, i + 1)
                sp.dma_start(y_dram[:, 1, cols], res[:, 1, cols]).then_inc(stored, 16)
            sp.wait_ge(stored, 8 * 16)

        @block.tensor
        def _(pe):
            extra = 0

            def passes(dst, a, b, start, stop):
                pe.matmul(dst, a[0], b[0], start=start, stop=False)
                pe.matmul(dst, a[0], b[1], start=False, stop=False)
                return pe.matmul(dst, a[1], b[0], start=False, stop=stop)

            def pair(b, c, parity, free=None, q=None):
                s = c % RING if q is None else q % RING
                pe.wait_ge(lo_done, b * PAIRS + (c + extra + 1) if q is None else q + 1)
                for t in range(TT):
                    if c == 0 and free is not None:
                        pe.wait_ge(*free[t])
                    for k in range(2):
                        kk = 2 * c + k
                        cols = slice((2 * s + k) * BW, (2 * s + k + 1) * BW)
                        toks = slice(t * P, (t + 1) * P)
                        last = passes(acc[parity][t][:, :],
                                      (lhs_hi[:, kk, toks], lhs_lo[:, kk, toks]),
                                      (w_hi[:, cols], w_lo[:, cols]), kk == 0, kk == KT_IN - 1)
                    if c == PAIRS - 1 and t == 0:
                        last.then_inc(acc0_full, 1)
                last.then_inc(pe_used, 1)

            def stream(b, parity, pieces=None):
                free = None
                if not isinstance(b, int) or b >= 2:
                    free = ((acc0_free, b - 1), (acc1_free, b - 1))
                for c in range(PAIRS):
                    for piece in (pieces or {}).get(c, ()):
                        piece()
                    pair(b, c, parity, free)

            def transpose_stage(event, b):
                pe.wait_ge(acc0_free, b + 1)
                pe.wait_ge(acc1_free, b + 1)
                if not isinstance(event, int) or event > 0:
                    pe.wait_ge(tr_lo, event)
                for cc in range(4):
                    for t in range(TT):
                        o = (cc % 2) * T + t * P
                        last = pe.transpose((bv, bx)[cc // 2][:, o:o + P],
                                            stage[:, t, cc * P:(cc + 1) * P], ident)
                last.then_inc(tr_done, 1)

            def x_t(c):
                if c % 2 == 0:
                    pe.wait_ge(x_in[c // 2], 16)
                if c >= 2:
                    pe.wait_ge(ht_lo, c - 1)
                for k in range(2):
                    for t in range(TT):
                        last = pe.transpose(acc[1][c % 2][:, k * T + t * P:k * T + (t + 1) * P],
                                            x_nat[:, t, (2 * c + k) * P:(2 * c + k + 1) * P], ident)
                last.then_inc(ht_ready, 1)

            def prepare_rows():
                pe.wait_ge(consts_in, 16 * N_CONST)
                for i in range(2):
                    pe.transpose(bx[:, i * CMP_L:(i + 1) * CMP_L], pos_rows[:, i * P:(i + 1) * P],
                                 ident[0:CMP_L, 0:CMP_L])
                pe.transpose(bx[:, 192:192 + KT_IN // 2], gain_m_rows[:, :],
                             ident[0:KT_IN // 2, 0:KT_IN // 2])
                for c in range(16):
                    last = pe.transpose(bx[:, 128 + 4 * c:132 + 4 * c],
                                        conv_rows[:, c * P:(c + 1) * P], ident[0:4, 0:4])
                last.then_inc(pre_pe, 1)
                pe.matmul(by[0:HEADS_A, 0:TOE], rb[:, :], hot_down, start=True,
                          stop=True).then_inc(pre_pe, 1)

            def prepare_bias(t):
                for n in range(N_CMP):
                    start = 255 + t * P - (CMP_S * n + CMP_L - 1)
                    last = pe.matmul((bz, bv)[t][:, n * HEADS_A:(n + 1) * HEADS_A],
                                     hot_up[:, start:start + P], rb[:, :], start=True, stop=True)
                last.then_inc(pre_pe, 1)

            pe.wait_ge(first_in, 32)
            pe.transpose(bx[:, 0:KT_IN], gain_rows[:, :], ident[0:KT_IN, 0:KT_IN]
                         ).then_inc(pre_pe, 1)
            x_t(0)
            x_t(1)
            pe.wait_ge(pre_act, 1)
            for c in range(PAIRS):
                pe.wait_ge(ht_lo, c + 1)
                pair(0, c, 0)
                if c + 2 < PAIRS:
                    x_t(c + 2)
                if c == 5:
                    prepare_rows()
                if c in (7, 8):
                    prepare_bias(c - 7)
            pe.wait_ge(pre_dve, 2)
            pe.wait_ge(pre_act, 2)
            stream(1, 1, {1: [lambda: transpose_stage(T_CK, 0)]})

            def small_pair(q, i):
                pe.wait_ge(lo_done, q + 1)
                for t in range(TT):
                    for k in range(SMALL_K):
                        kk = i * SMALL_K + k
                        col = (q % RING) * 2 * BW + k * N_SMALL
                        toks = slice(t * P, (t + 1) * P)
                        last = passes((by, bz)[t][:, 0:N_SMALL],
                                      (lhs_hi[:, kk, toks], lhs_lo[:, kk, toks]),
                                      [m[:, col:col + N_SMALL] for m in (w_hi, w_lo)],
                                      kk == 0, kk == KT_IN - 1)
                last.then_inc(pe_used, 1)

            def compressor_pair(q, j, i):
                if (j, i) == (0, 0):
                    pe.wait_ge(tr_lo, T_CV + 1)
                    pe.wait_ge(pre_dve, 4)
                pe.wait_ge(lo_done, q + 1)
                for m in range(CMP_PL):
                    l = i * CMP_PL + m
                    col = (q % RING) * 2 * BW + m * P
                    ins = slice(l, l + CMP_S * (NP16 - 1) + 1, CMP_S)
                    last = passes((bx, bv)[j][:, 0:5 * NP16],
                                  [w[:, col:col + P] for w in (w_hi, w_lo)],
                                  [part[:, :, ins] for part in cin[j]],
                                  l == 0, l == CMP_L - 1)
                last.then_inc(pe_used, 1)

            transpose_stage(T_CV, 1)
            for q, i, c in mixed_block():
                if i is None:
                    pair(MIXED, c, 0, ((acc0_free, MIXED - 1), (acc1_free, MIXED - 1)), q)
                elif i < SMALL_PAIRS:
                    small_pair(q, i)
                else:
                    compressor_pair(q, *divmod(i - SMALL_PAIRS, CMP_PAIRS))
            extra = EXTRA

            def compressed():
                pe.wait_ge(pre_pool, 3)
                pe.wait_ge(tr_lo, T_SK + 1)
                pe.matmul(by[:, 0:GROUPS * NP16], w2[:, 0:P], hid[:, 0:GROUPS * NP16],
                          start=True, stop=True)
                for g in range(GROUPS):
                    last = pe.matmul(bz[0:N_CMP, g * P:(g + 1) * P],
                                     hid[:, 64 + g * NP16:64 + g * NP16 + N_CMP], w2[:, P:2 * P],
                                     start=True, stop=True)
                last.then_inc(pre_pe, 1)

            def running_sum():
                pe.wait_ge(pre_dve, 8)
                pe.matmul(bx[:, 0:4], tri, log_f[:, 0, :], start=True, stop=True)
                pe.matmul(bx[:, 4:8], ones[:, :], log_f[:, 0, :], start=True, stop=False)
                pe.matmul(bx[:, 4:8], tri, log_f[:, 1, :], start=False,
                          stop=True).then_inc(pre_pe, 1)

            def a_rows():
                pe.wait_ge(pre_dve, 9)
                for t in range(TT):
                    last = pe.transpose(bx[0:4, 128 + t * P:128 + (t + 1) * P], a_col[:, t, :],
                                        ident)
                last.then_inc(pre_pe, 1)

            def m_columns():
                pe.wait_ge(pre_dve, 10)
                for t in range(TT):
                    last = pe.transpose(bx[:, 8 + 4 * t:12 + 4 * t], m_row[:, t * P:(t + 1) * P],
                                        ident[0:4, 0:4])
                last.then_inc(pre_pe, 1)

            def key_block():
                pe.wait_ge(pre_dve, 5)
                transpose_stage(T_SK, 2)

            def window_key_block():
                pe.wait_ge(pre_dve, 11)
                transpose_stage(T_WK, 4)

            stream(3, 1, {1: [key_block], 5: [compressed, running_sum], 8: [a_rows],
                          11: [m_columns]})
            stream(4, 0)
            stream(5, 1, {1: [window_key_block]})
            stream(B_Q0, 0)

            def group_pieces(g):
                def logits(u):
                    hh, t = divmod(u, TT)
                    n = P * (t + 1)
                    q = [m[:, hh, t * P:(t + 1) * P] for m in (q_hi, q_lo)]
                    if u == 0:
                        pe.wait_ge(tr_lo, g + (T_AQ + 1))
                    else:
                        pe.wait_ge(l_done, g * UNITS + u)
                    keys = [m.rearrange("p j g t -> p j (g t)")[:, :, bass.ds(g * T, n)]
                            for m in (k_hi, k_lo)]
                    passes(halves(bx)[:, :, 0:n], q, keys, True, True)
                    passes(by[:, 0:NP16], q, [m[:, bass.ds(g * NP16, NP16)]
                                              for m in (kc_hi, kc_lo)],
                           True, True).then_inc(s_ready, 1)

                def weights_t(u):
                    t = u % TT
                    lg = lgs[u % 2]
                    pe.wait_ge(p_done, g * UNITS + u + 1)
                    for b in range(2):
                        for s in range(t + 1):
                            pe.transpose(bz[:, (2 * b + s) * P:(2 * b + s + 1) * P],
                                         halves(lg)[:, b, s * P:(s + 1) * P], ident)
                    if u:
                        pe.wait_ge(o_done, g * UNITS + u)
                    pe.transpose(bv[0:N_CMP, P:2 * P], lg[:, 512:512 + N_CMP],
                                 ident).then_inc(pt_ready, 1)

                def values(u):
                    t = u % TT
                    pe.wait_ge(pt_lo_done, g * UNITS + u + 1)
                    for b in range(2):
                        for s in range(t + 1):
                            cols = slice((2 * b + s) * P, (2 * b + s + 1) * P)
                            passes(bv[:, 0:P], (pt_hi[:, cols], pt_lo[:, cols]),
                                   [m[:, b, s, bass.ds(g * P, P)] for m in (v_hi, v_lo)],
                                   b == 0 and s == 0, False)
                    passes(bv[:, 0:P], (pct_hi[0:N_CMP, :], pct_lo[0:N_CMP, :]),
                           [m[0:N_CMP, bass.ds(g * P, P)] for m in (vc_hi, vc_lo)],
                           False, True).then_inc(o_ready, 1)

                entries = [(1, lambda: transpose_stage(g + T_AQ, 2 * g + B_Q0))]
                for u in range(UNITS):
                    s = UNIT0 + UNIT_STEP * u
                    entries += [(s + 3, lambda u=u: weights_t(u)), (s + 4, lambda u=u: values(u))]
                entries += [(UNIT0 + UNIT_STEP * u, lambda u=u: logits(u)) for u in range(UNITS)]
                return piece_map(*entries)

            def group(g):
                b, pieces = 2 * g + B_NSA, group_pieces(g)
                for n in range(2):
                    stream(b + n, 1 - n, {s - n * PAIRS: f for s, f in pieces.items()
                                          if n * PAIRS <= s < (n + 1) * PAIRS})

            with pe.Fori(0, GROUPS - 1) as g:
                group(g)
            group(GROUPS - 1)

            def spread_m():
                pe.wait_ge(m_spread, 1)
                for i in range(HEADS_M * TT):
                    last = pe.matmul((by, bz)[i // 4][:, (i % 4) * P:(i % 4 + 1) * P],
                                     m_wide[:, i, :], ident, start=True, stop=True)
                last.then_inc(nm_ready, 1)

            def head_pieces(h):
                def scores():
                    pe.wait_ge(qk_lo_done, h + 1)
                    for s in range(TT):
                        o0 = 2 * P * s
                        for d in range(2):
                            last = passes(bx[:, o0:o0 + T - s * P],
                                          [m[:, 2 + d, s * P:(s + 1) * P] for m in (qk_hi, qk_lo)],
                                          [m[:, d, s * P:T] for m in (qk_hi, qk_lo)],
                                          d == 0, d == 1)
                    last.then_inc(st_ready, 1)

                def numerator():
                    pe.wait_ge(sw_lo_done, h + 1)
                    pe.wait_ge(v_split_lo, h + 3)
                    parts = ((0, 0, 0), (1, 0, 1), (1, 1, 2))
                    for t, s, i in parts:
                        cols = slice(i * P, (i + 1) * P)
                        passes((by, bz)[t][:, :], (sw_hi[:, cols], sw_lo[:, cols]),
                               (mv_hi[:, s, :], mv_lo[:, s, :]), s == 0, s == t)
                    for t, s, i in parts:
                        for m in (sw_hi, sw_lo):
                            last = pe.matmul(bv[:, 2 * t:2 * t + 2], m[:, i * P:(i + 1) * P],
                                             ones_r[:, :], start=(s == 0 and m is sw_hi),
                                             stop=(s == t and m is sw_lo))
                    last.then_inc(num_ready, 1)

                return {0: {1: [lambda: transpose_stage(h + T_MQK, 4 * h + B_MLSTM - 1)],
                            },
                        1: {0: [scores], 3: [numerator]}}

            def head(h, blocks, last={}):
                pieces = head_pieces(h)
                pieces[2] = last
                for n in range(blocks):
                    stream(4 * h + B_MLSTM + n, 1 - n % 2, pieces.get(n))

            def mix_t(c):
                if c == 0:
                    pe.wait_ge(hm_done, HEADS_M)
                if c < PAIRS // 2:
                    src, col = mix_a, c * 2 * P
                    pe.wait_ge(az_free, GROUPS + 1)
                else:
                    src, col = mix_m, (c - PAIRS // 2) * 2 * P
                    pe.wait_ge(ym_done, (c - PAIRS // 2) // 2 + 1)
                if c >= 2:
                    pe.wait_ge(ht_lo, PAIRS + c - 1)
                for k in range(2):
                    for t in range(TT):
                        last = pe.transpose((by, bz)[c % 2][:, k * T + t * P:k * T + (t + 1) * P],
                                            src[:, t, col + k * P:col + (k + 1) * P], ident)
                last.then_inc(ht_ready, 1)

            spread_m()
            with pe.Fori(0, HEADS_M - 1) as h:
                head(h, 4)
            head(HEADS_M - 1, 3, {c + 2: [lambda c=c: mix_t(c)] for c in range(MIX_EARLY)})

            for c in range(PAIRS):
                if MIX_LATE <= c < MIX_LATE + PAIRS - MIX_EARLY:
                    mix_t(MIX_EARLY + c - MIX_LATE)
                pe.wait_ge(ht_lo, PAIRS + c + 1)
                pair(B_OUT, c, 0, ((acc0_free, B_OUT - 1), (acc1_free, B_OUT - 1)))
            for c in range(PAIRS):
                pair(B_OUT + 1, c, 1, ((acc0_free, B_OUT), (acc1_free, B_OUT)))
            with pe.Fori(0, 3) as i:
                for n in range(2):
                    for c in range(PAIRS):
                        pair(2 * i + (n + B_OUT + 2), c, n,
                             ((out0_free, 2 * i + n + 1), (out1_free, 2 * i + n + 1)))

        @block.scalar
        def _(act):
            chain = Count()
            extra = 0

            def link(ins):
                chain.n += 1
                ins.then_inc(act_chain, 1)
                act.wait_ge(act_chain, chain.value())

            def split(q, s, turn):
                if not isinstance(q, int) or q >= RING:
                    act.wait_ge(pe_used, q - RING + 1)
                act.wait_ge(w_loaded[s], turn)
                cols = slice(s * 2 * BW, (s + 1) * 2 * BW)
                act.activation(w_hi[:, cols], w_raw[:, cols], ACT.Copy).then_inc(hi_done, 1)

            def slot(b, c):
                n = c + LOOKAHEAD + extra
                split(b * PAIRS + n, n % RING,
                      b * (PAIRS // RING * LOADED) + LOADED * (n // RING + 1))

            def take(b, parity, dst):
                act.wait_ge(acc0_full, b + 1)
                act.activation(dst, acc[parity][0][:, :], ACT.Copy,
                               scale=rstd[:, 0:1]).then_inc(acc0_free, 1)

            def stream(b, pieces=None, first=False):
                for c in range(PAIRS):
                    if not first:
                        slot(b, c)
                    for piece in (pieces or {}).get(c, ()):
                        piece()
                    if first:
                        slot(b, c)

            def tiles(t):
                return t.rearrange("p (g t) -> p g t", t=T)

            def transposed(event, dst):
                act.wait_ge(tr_done, event + 1)
                act.activation(dst(0), tiles(bv[:, :]), ACT.Copy)
                act.activation(dst(1), tiles(bx[:, :]), ACT.Copy).then_inc(tr_hi, 1)

            def staged_values(b, dst):
                act.wait_ge(acc1_free, b + 1)
                act.wait_ge(acc0_free, b + 1)
                act.activation(dst, stage[:, :, :], ACT.Copy).then_inc(v_split_hi, 1)

            act.dma_start(c128[:, :], const128).then_inc(first_in, 16)
            act.dma_start(gain_rows[:, :], norm_gain.rearrange("(k p) -> k p", p=P)
                          ).then_inc(first_in, 16)
            loads = [
                (hot[:, :], const32), (toe_mask[:, :], const16), (rb[:, :], rel_bias),
                (gain_m_rows[:, :], mlstm_norm_gain.rearrange("(k p) -> k p", p=P)),
                (pos_rows[:, 0:P], cmp_k_pos), (pos_rows[:, P:2 * P], cmp_v_pos),
                (conv_rows[:, :], w_conv), (w2[:, 0:P], cmp_k_w2), (w2[:, P:2 * P], cmp_v_w2),
            ] + [(b_if[:, i * HEADS_M:(i + 1) * HEADS_M],
                  src.rearrange("(o n) -> o n", o=1).broadcast_to([P, HEADS_M]))
                 for i, src in enumerate((b_igate, b_fgate))]
            assert len(loads) == N_CONST

            def x_hi(c, gain=gain_t, banks=acc[1]):
                act.wait_ge(ht_ready, c + 1)
                if c >= PAIRS:
                    act.wait_ge(pe_used, (B_OUT - 1) * PAIRS + (EXTRA + 1) + c - PAIRS)
                for k in range(2):
                    kk = (2 * c + k) % KT_IN
                    last = act.activation(lhs_hi[:, kk, :], banks[c % 2][:, k * T:(k + 1) * T],
                                          ACT.Copy, scale=gain[:, kk:kk + 1])
                last.then_inc(ht_hi, 1)

            act.wait_ge(pre_pe, 1)
            link(act.activation(gain_t[:, :], bx[:, 0:KT_IN], ACT.Copy))
            act.activation(spare[:, 0:1], gain_t[:, 0:1], ACT.Copy).then_inc(pre_act, 1)
            x_hi(0)
            split(0, 0, LOADED)
            x_hi(1)
            for dst, src in loads:
                act.dma_start(dst, src).then_inc(consts_in, 16)
            split(1, 1, LOADED)
            split(2, 2, LOADED)
            for c in range(PAIRS):
                if c + 2 < PAIRS:
                    x_hi(c + 2)
                slot(0, c)
                if c == 7:
                    act.wait_ge(pre_pe, 2)
                    act.activation(gain_mix[:, KT_IN // 2:KT_IN], bx[:, 192:192 + KT_IN // 2],
                                   ACT.Copy)
                    act.activation(pos_t[:, :], bx[:, 0:2 * CMP_L], ACT.Copy)
                    act.activation(conv_w[:, :], bx[:, 128:192], ACT.Copy).then_inc(pre_act, 1)
                if c == 12:
                    act.wait_ge(pre_dve, 1)
                    act.dma_start(toe_dram.ap(), toe_row[:, :].unsqueeze(1).broadcast_to(
                        [HEADS_A, P, TOE])).then_inc(toe_out, 16)
                if c % 2 == 1:
                    t, i = divmod(c // 2, 4)
                    act.wait_ge(x_in[2 * i], 16)
                    act.wait_ge(x_in[2 * i + 1], 16)
                    link(act.activation(junk[:, :], x_nat[:, t, i * 1024:(i + 1) * 1024],
                                        ACT.Square, accum_out=ss8[:, t, i:i + 1]))
            act.activation(spare[:, 1:2], gain_t[:, 0:1], ACT.Copy).then_inc(pre_act, 1)
            act.wait_ge(pre_pool, 1)
            take(0, 0, stage[:, 0, :])

            def first_bias():
                act.wait_ge(toe_out, 16)
                act.dma_start(toe[:, :].rearrange("p (h s) -> p h s", s=T), toe_rows[:, 0:HPG, :]
                              ).then_inc(toe_in, 16)

            toe_rows = bass.AP(toe_dram, P - 1, [[TOE - 1, P], [P * TOE, HEADS_A], [1, T]])

            def positions_hi():
                act.wait_ge(pre_pool, 2)
                act.activation(cin[0][0][:, 4, 0:CMP_L], pos_t[:, 0:CMP_L], ACT.Copy)
                act.activation(cin[1][0][:, 4, 0:CMP_L], pos_t[:, CMP_L:2 * CMP_L], ACT.Copy
                               ).then_inc(pre_act, 1)

            stream(1, {2: [lambda: transposed(T_CK, lambda i: cin[0][0][:, 2 * i:2 * i + 2, 0:T])],
                       5: [positions_hi], 8: [first_bias]})
            act.wait_ge(tr_done, T_CK + 1)
            take(1, 1, stage[:, 0, :])

            def exponentials_1():
                act.wait_ge(pre_dve, 5)
                act.activation(hid_e[:, :], hid[:, :], ACT.Exp, scale=-1.0).then_inc(pre_act, 1)
                act.wait_ge(pre_dve, 6)
                act.activation(g_sig[:, :, :], small[:, :, N_IF:], ACT.Exp, scale=-1.0
                               ).then_inc(pre_act, 1)
                link(act.activation(log_f[:, :, :], f_abs[:, :, :], ACT.Exp, scale=-1.0))
                act.activation(log_f[:, :, :], log_f[:, :, :], ACT.Ln, bias=1.0
                               ).then_inc(pre_act, 1)

            def compressed_hi():
                act.wait_ge(pre_pe, 6)
                act.activation(kc_hi[:, :], by[:, 0:GROUPS * NP16], ACT.Copy)
                act.activation(vc_hi[0:N_CMP, :], bz[0:N_CMP, :], ACT.Copy).then_inc(pre_act, 1)

            def e_neg_m_exp():
                act.wait_ge(pre_dve, 11)
                act.activation(e_neg_m[:, :, :], e_neg_m[:, :, :], ACT.Exp, scale=-1.0
                               ).then_inc(pre_act, 1)

            for j, (q, _, _) in enumerate(mixed_block()):
                q += LOOKAHEAD
                split(q, q % RING, LOADED * (q // RING + 1))
                if j == 1:
                    transposed(T_CV, lambda i: cin[1][0][:, 2 * i:2 * i + 2, 0:T])
                if j == 2 * EXTRA + 2:
                    exponentials_1()
            extra = EXTRA
            act.wait_ge(tr_done, T_CV + 1)
            take(2, 0, stage[:, 0, :])
            stream(3, {2: [lambda: transposed(T_SK, lambda i: k_hi[:, 0, 2 * i:2 * i + 2, :])],
                       6: [compressed_hi], 14: [e_neg_m_exp]})
            act.wait_ge(tr_done, T_SK + 1)
            take(3, 1, stage[:, 0, :])
            stream(4, {1: [lambda: staged_values(3, v_hi[:, 0])]})
            act.wait_ge(v_split_lo, 1)
            take(4, 0, stage[:, 0, :])
            stream(5, {2: [lambda: transposed(T_WK, lambda i: k_hi[:, 1, 2 * i:2 * i + 2, :])]})
            act.wait_ge(tr_done, T_WK + 1)
            take(5, 1, stage[:, 0, :])
            stream(B_Q0, {1: [lambda: staged_values(5, v_hi[:, 1])]})
            act.wait_ge(v_split_lo, 2)
            take(B_Q0, 0, stage[:, 0, :])

            def group_pieces(g, last):
                def exponentials(u):
                    n = P * (u % TT + 1)
                    lg = lgs[u % 2]
                    act.wait_ge(l_done, g * UNITS + u + 1)
                    for b in range(2):
                        act.activation(halves(lg)[:, b, 0:n], halves(lg)[:, b, 0:n], ACT.Exp,
                                       bias=nmax[:, 1 + b:2 + b], accum_out=rsum[:, 1 + b:2 + b])
                    act.activation(lg[:, 512:512 + N_CMP], lg[:, 512:512 + N_CMP], ACT.Exp,
                                   bias=nmax[:, 0:1], accum_out=rsum[:, 0:1]).then_inc(e_done, 1)

                def weights_hi(u):
                    n = P * (u % TT + 1)
                    act.wait_ge(pt_ready, g * UNITS + u + 1)
                    act.activation(halves(pt_hi)[:, :, 0:n], halves(bz)[:, :, 0:n], ACT.Copy)
                    act.activation(pct_hi[0:N_CMP, :], bv[0:N_CMP, P:2 * P],
                                   ACT.Copy).then_inc(pt_hi_done, 1)

                def outputs(u):
                    hh, t = divmod(u, TT)
                    act.wait_ge(o_ready, g * UNITS + u + 1)
                    act.activation(mix_a[:, t, bass.ds(g * BW + hh * P, P)], bv[:, 0:P], ACT.Copy
                                   ).then_inc(o_done, 1)

                def take_gate():
                    act.wait_ge(az_free, g + 1)
                    take(2 * g + B_NSA, 1, gate_buf[:, 0, :])

                def gate_exp():
                    act.wait_ge(acc1_free, 2 * g + (B_NSA + 1))
                    act.wait_ge(acc0_free, 2 * g + (B_NSA + 1))
                    act.activation(ebuf[:, :, :], gate_buf[:, :, :], ACT.Exp, scale=-1.0
                                   ).then_inc(az_e, 1)

                def next_bias():
                    act.wait_ge(l_done, g * UNITS + UNITS)
                    act.dma_start(toe[:, :].rearrange("p (h s) -> p h s", s=T),
                                  toe_rows[:, bass.ds(g * HPG + HPG, HPG), :]).then_inc(toe_in, 16)

                entries = [(2, lambda: transposed(g + T_AQ, lambda i: q_hi[:, 2 * i:2 * i + 2, :])),
                           (16, take_gate), (17, gate_exp)]
                for u in range(UNITS):
                    s = UNIT0 + UNIT_STEP * u
                    entries += [(s + 1, lambda u=u: exponentials(u)),
                                (s + 3, lambda u=u: weights_hi(u)),
                                (s + 5, lambda u=u: outputs(u))]
                if not last:
                    entries.append((28, next_bias))
                return piece_map(*entries)

            def group(g, last=False):
                b, pieces = 2 * g + B_NSA, group_pieces(g, last)
                for n in range(2):
                    stream(b + n, {s - n * PAIRS: f for s, f in pieces.items()
                                   if n * PAIRS <= s < (n + 1) * PAIRS}, first=True)
                act.wait_ge(tr_done, g + (T_AQ + 1))
                take(b + 1, 0, stage[:, 0, :])

            with act.Fori(0, GROUPS - 1) as g:
                group(g)
            group(GROUPS - 1, last=True)

            def head_pieces(h):
                b = 4 * h + B_MLSTM

                def conv_inputs():
                    act.wait_ge(tr_done, h + (T_MQK + 1))
                    act.activation(conv_in[:, 0:2, 3:PADT], tiles(bv[:, :]),
                                   ACT.Copy).then_inc(tr_hi, 1)

                def conv_exp():
                    act.wait_ge(conv_done, h + 1)
                    act.wait_ge(az_free, GROUPS + 1)
                    act.activation(qk_sig, qk[:, :, :], ACT.Exp, scale=-1.0).then_inc(conv_e, 1)

                def decay():
                    act.wait_ge(nm_done, 1)
                    for i, (s, src) in enumerate(((0, neg_m_diag), (0, neg_m), (1, neg_m_diag))):
                        t = (0, 1, 1)[i]
                        last = act.activation(
                            wexp[:, i * P:(i + 1) * P], flat(src)[:, bass.ds(h * T + t * P, P)],
                            ACT.Exp, bias=flat(a_col)[:, bass.ds(h + s * HEADS_M, 1)])
                    last.then_inc(wexp_done, 1)

                def qk_hi_part():
                    act.wait_ge(qk_done, h + 1)
                    act.activation(qk_hi[:, :, :], qk[:, :, :], ACT.Copy).then_inc(qk_hi_done, 1)

                def sw_hi_part():
                    act.wait_ge(sw_done, h + 1)
                    act.activation(sw_hi[:, :], sw[:, :], ACT.Copy).then_inc(sw_hi_done, 1)

                def output_gate():
                    act.wait_ge(acc1_free, b + 2)
                    act.wait_ge(acc0_free, b + 2)
                    act.activation(ebuf[:, :, :], stage[:, :, :], ACT.Exp, scale=-1.0
                                   ).then_inc(mo_e, 1)

                def squares():
                    act.wait_ge(ho_done, h + 1)
                    for t in range(TT):
                        last = act.activation(ebuf[:, t, :], hm[:, t, :], ACT.Square,
                                              accum_out=ssm[:, t:t + 1])
                    last.then_inc(ssm_done, 1)

                return {0: piece_map((2, conv_inputs), (7, conv_exp), (9, decay),
                                     (13, qk_hi_part)),
                        1: piece_map((1, sw_hi_part),
                                     (1, lambda: staged_values(b, mv_hi[:, :, :]))),
                        2: piece_map((1, output_gate), (7, squares))}

            def silu_gate(h):
                act.wait_ge(hr_done, h + 1)
                act.wait_ge(acc1_free, 4 * h + (B_MLSTM + 3))
                act.wait_ge(acc0_free, 4 * h + (B_MLSTM + 3))
                act.activation(ebuf[:, :, :], stage[:, :, :], ACT.Exp, scale=-1.0
                               ).then_inc(mz_e, 1)

            def head(h, blocks, last={}):
                b, pieces = 4 * h + B_MLSTM, head_pieces(h)
                pieces[3] = {1: [lambda: silu_gate(h)]}
                for c, late in last.items():
                    pieces[2].setdefault(c, []).extend(late)
                stage_free = ((tr_done, h + (T_MQK + 1)), (v_split_lo, h + 3), None,
                              (mz_done, h + 1))
                for n in range(blocks):
                    stream(b + n, pieces.get(n))
                    if stage_free[n] is not None:
                        act.wait_ge(*stage_free[n])
                    take(b + n, 1 - n % 2, stage[:, 0, :])

            def mix_hi(c):
                x_hi(PAIRS + c, gain_mix, (by, bz))

            with act.Fori(0, HEADS_M - 1) as h:
                head(h, 4)
            head(HEADS_M - 1, 3, {c + 2: [lambda c=c: mix_hi(c)] for c in range(MIX_EARLY)})

            x_cols = x[0].rearrange("(a p) d -> p a d", p=P)

            def fetch_residual(n, i):
                act.dma_start(xres[:, i], x_cols[:, :, bass.ds(n * BW, BW)]).then_inc(xr_in[i], 16)

            def squares(n):
                act.wait_ge(out1_free, n + 1)
                for t in range(TT):
                    last = act.activation(
                        ebuf[:, t, :], res[:, t, bass.ds(n * BW, BW)], ACT.Square,
                        accum_out=ssf[:, t, bass.ds(n, 1)])
                last.then_inc(sq_done, 1)

            for c in range(PAIRS):
                if MIX_LATE <= c < MIX_LATE + PAIRS - MIX_EARLY:
                    mix_hi(MIX_EARLY + c - MIX_LATE)
                slot(B_OUT, c)
                if c == 1:
                    silu_gate(HEADS_M - 1)
                if c == 9:
                    act.wait_ge(ym_done, HEADS_M)
                    fetch_residual(0, 0)
                    fetch_residual(1, 1)
                    act.dma_start(gain_f[:, :], final_norm_gain.rearrange("(o n) -> o n", o=1)
                                  .broadcast_to([P, D])).then_inc(gf_in, 16)

            def out_block(n, i, last=False):
                for c in range(PAIRS - LOOKAHEAD if last else PAIRS):
                    slot(n + B_OUT, c)
                    if c == 2:
                        squares(n - 1)
                    if c == 4 and not last:
                        fetch_residual(n + 1, i)

            out_block(1, 0)
            with act.Fori(1, 3) as i:
                out_block(2 * i, 1)
                out_block(2 * i + 1, 0)
            out_block(6, 1)
            out_block(7, 0, last=True)
            squares(7)
            act.wait_ge(fr_done, 1)
            act.wait_ge(gained, N_OUT)
            for i in range(4):
                cols = slice(i * 1024, (i + 1) * 1024)
                act.activation(res[:, 0, cols], res[:, 0, cols], ACT.Copy,
                               scale=fr[:, 0:1]).then_inc(y0_done, 1)

        @block.vector
        def _(dve):
            chain = Count()
            extra = 0

            def link(ins):
                chain.n += 1
                ins.then_inc(dve_chain, 1)
                dve.wait_ge(dve_chain, chain.value())

            def lo(q, s):
                dve.wait_ge(hi_done, q + 1)
                cols = slice(s * 2 * BW, (s + 1) * 2 * BW)
                dve.tensor_tensor(w_lo[:, cols], w_raw[:, cols], w_hi[:, cols].bitcast(F32),
                                  ALU.subtract).then_inc(lo_done, 1)

            def slot(b, c):
                n = c + LOOKAHEAD + extra
                lo(b * PAIRS + n, n % RING)

            def take(b, parity, dst):
                dve.wait_ge(pe_used, b * PAIRS + (PAIRS + extra))
                dve.tensor_scalar(dst, acc[parity][1][:, :], rstd[:, 1:2], None,
                                  ALU.mult).then_inc(acc1_free, 1)

            def stream(b, pieces=None, first=False):
                for c in range(PAIRS):
                    if not first:
                        slot(b, c)
                    for piece in (pieces or {}).get(c, ()):
                        piece()
                    if first:
                        slot(b, c)

            def tiles(t):
                return t.rearrange("p (g t) -> p g t", t=T)

            def transposed(event, hi, dst):
                dve.wait_ge(tr_hi, event + 1)
                for i, bk in enumerate((bv, bx)):
                    last = dve.tensor_tensor(dst(i), tiles(bk[:, :]), hi(i).bitcast(F32),
                                             ALU.subtract)
                last.then_inc(tr_lo, 1)

            def two(m, lead):
                return (lambda i: lead(m[0])[:, 2 * i:2 * i + 2, 0:T],
                        lambda i: lead(m[1])[:, 2 * i:2 * i + 2, 0:T])

            def staged_values(event, hi, dst):
                dve.wait_ge(v_split_hi, event + 1)
                dve.tensor_tensor(dst, stage[:, :, :], hi.bitcast(F32), ALU.subtract
                                  ).then_inc(v_split_lo, 1)

            def sigmoid(ready, buf, done, slots):
                flat_buf = flat(buf)

                def piece(i):
                    if i == 0:
                        dve.wait_ge(*ready)
                        link(dve.tensor_scalar(flat_buf, flat_buf, 1.0, None, ALU.add))
                    part = flat_buf[:, i * 256:(i + 1) * 256]
                    last = dve.reciprocal(part, part)
                    if i == 3:
                        last.then_inc(done, 1)
                return [(n, lambda i=i: piece(i)) for i, n in enumerate(slots)]

            dve.memset(m_half[:, :], -0.5)
            dve.memset(gain_mix[:, 0:KT_IN // 2], 1.0)
            dve.memset(eps_m[:, :], V_M * EPS)
            dve.memset(inv_m[:, :], 1.0 / V_M)
            dve.memset(ones_r[:, :].bitcast(F32), 1.0)
            dve.memset(ones[:, :], 1.0)

            def x_lo(c, gain=gain_t, banks=acc[1]):
                dve.wait_ge(ht_hi, c + 1)
                for k in range(2):
                    kk = (2 * c + k) % KT_IN
                    last = dve.scalar_tensor_tensor(
                        lhs_lo[:, kk, :], banks[c % 2][:, k * T:(k + 1) * T],
                        gain[:, kk:kk + 1], lhs_hi[:, kk, :].bitcast(F32), ALU.mult, ALU.subtract)
                last.then_inc(ht_lo, 1)

            x_lo(0)
            lo(0, 0)
            x_lo(1)
            lo(1, 1)
            lo(2, 2)
            for c in range(PAIRS):
                if c + 2 < PAIRS:
                    x_lo(c + 2)
                slot(0, c)
                if c == 7:
                    dve.wait_ge(pre_pe, 3)
                    dve.tensor_tensor(toe_row[:, :], by[0:HEADS_A, 0:TOE], toe_mask[:, :], ALU.add
                                      ).then_inc(pre_dve, 1)
                if c == 10:
                    dve.wait_ge(pre_pe, 5)
                    for t in range(TT):
                        last = dve.tensor_tensor(
                            bias_c[:, t], (bz, bv)[t][:, 0:N_CMP * HEADS_A].rearrange(
                                "p (n h) -> p n h", h=HEADS_A),
                            cmp_neg[:, t, :].unsqueeze(2).broadcast_to([P, N_CMP, HEADS_A]),
                            ALU.add)
                    last.then_inc(pre_dve, 1)
            dve.wait_ge(pre_act, 3)
            dve.tensor_reduce(ss[:, :], ss8[:, :, :], AX, ALU.add).then_inc(pre_dve, 1)
            dve.wait_ge(pre_pool, 1)
            take(0, 0, stage[:, 1, :])

            def positions_lo():
                dve.wait_ge(pre_act, 4)
                for j in range(2):
                    last = dve.tensor_tensor(cin[j][1][:, 4, 0:CMP_L],
                                             pos_t[:, j * CMP_L:(j + 1) * CMP_L],
                                             cin[j][0][:, 4, 0:CMP_L].bitcast(F32), ALU.subtract)
                last.then_inc(pre_dve, 1)

            stream(1, {2: [lambda: transposed(T_CK, *two(cin[0], lambda m: m))],
                       6: [positions_lo]})
            dve.wait_ge(tr_done, T_CK + 1)
            take(1, 1, stage[:, 1, :])

            def small_columns():
                dve.wait_ge(pe_used, MIXED * PAIRS + 2 * EXTRA)
                for j, bk in enumerate((bx, bv)):
                    last = dve.tensor_copy(hid_b[:, j:j + 1], bk[:, 64:65])
                link(last)
                for j, bk in enumerate((bx, bv)):
                    last = dve.tensor_scalar(hid[:, j * 64:(j + 1) * 64], bk[:, 0:64],
                                             hid_b[:, j:j + 1], None, ALU.add)
                last.then_inc(pre_dve, 1)
                for t in range(TT):
                    last = dve.tensor_scalar(small[:, t, :], (by, bz)[t][:, 0:N_SMALL],
                                             rstd[:, t:t + 1], None, ALU.mult)
                link(last)
                for t in range(TT):
                    last = dve.tensor_tensor(small[:, t, 0:N_IF], small[:, t, 0:N_IF], b_if[:, :],
                                             ALU.add)
                link(last)
                dve.scalar_tensor_tensor(f_abs[:, :, :], small[:, :, HEADS_M:N_IF], -1.0,
                                         small[:, :, HEADS_M:N_IF], ALU.mult, ALU.max
                                         ).then_inc(pre_dve, 1)

            def sigmoids():
                dve.wait_ge(pre_act, 5)
                link(dve.tensor_scalar(hid_e[:, :], hid_e[:, :], 1.0, None, ALU.add))
                dve.reciprocal(hid_e[:, :], hid_e[:, :]).then_inc(pre_dve, 1)
                dve.wait_ge(pre_act, 7)
                dve.scalar_tensor_tensor(log_f[:, :, :], small[:, :, HEADS_M:N_IF], 0.0,
                                         log_f[:, :, :], ALU.min, ALU.subtract
                                         ).then_inc(pre_dve, 1)
                link(dve.tensor_scalar(g_sig[:, :, :], g_sig[:, :, :], 1.0, None, ALU.add))
                link(dve.reciprocal(g_sig[:, :, :], g_sig[:, :, :]))

            def decay_columns():
                dve.wait_ge(pre_pe, 7)
                link(dve.tensor_copy(f_cum[:, :, :], bx[:, 0:8].rearrange("p (a h) -> p a h", a=TT)))
                dve.tensor_tensor(a_col[:, :, :], small[:, :, 0:HEADS_M], f_cum[:, :, :],
                                  ALU.subtract).then_inc(pre_dve, 1)
                dve.wait_ge(pre_act, 8)
                dve.tensor_tensor(kc_lo[:, :], by[:, 0:GROUPS * NP16], kc_hi[:, :].bitcast(F32),
                                  ALU.subtract)
                link(dve.tensor_tensor(vc_lo[0:N_CMP, :], bz[0:N_CMP, :],
                                       vc_hi[0:N_CMP, :].bitcast(F32), ALU.subtract))

            def running_maximum():
                dve.wait_ge(pre_pe, 8)
                link(dve.tensor_copy(a_row[:, :], bx[0:4, 128:128 + T]))
                dve.tensor_tensor_scan(m_row[:, :], a_row[:, :], a_row[:, :], 0.0, ALU.max,
                                       ALU.max).then_inc(pre_dve, 1)

            def stabiliser():
                dve.wait_ge(pre_pe, 9)
                m = bx[:, 8:16].rearrange("p (a h) -> p a h", a=TT)
                dve.tensor_scalar(m_neg.rearrange("p h a -> p a h"), m, -1.0, None, ALU.mult)
                dve.tensor_tensor(e_neg_m[:, :, :], f_cum[:, :, :], m, ALU.add
                                  ).then_inc(pre_dve, 1)

            for j, (q, _, _) in enumerate(mixed_block()):
                q += LOOKAHEAD
                lo(q, q % RING)
                if j == 1:
                    transposed(T_CV, *two(cin[1], lambda m: m))
                if j == 2 * EXTRA + 1:
                    small_columns()
                if j == 2 * EXTRA + 3:
                    sigmoids()
            extra = EXTRA
            dve.wait_ge(tr_done, T_CV + 1)
            take(2, 0, stage[:, 1, :])
            stream(3, {2: [lambda: transposed(T_SK, *two((k_hi, k_lo), lambda m: m[:, 0]))],
                       6: [decay_columns], 9: [running_maximum], 12: [stabiliser]})
            dve.wait_ge(tr_done, T_SK + 1)
            take(3, 1, stage[:, 1, :])
            stream(4, {1: [lambda: staged_values(0, v_hi[:, 0], v_lo[:, 0])]})
            dve.wait_ge(v_split_lo, 1)
            take(4, 0, stage[:, 1, :])
            stream(5, {2: [lambda: transposed(T_WK, *two((k_hi, k_lo), lambda m: m[:, 1]))]})
            dve.wait_ge(tr_done, T_WK + 1)
            take(5, 1, stage[:, 1, :])
            stream(B_Q0, {1: [lambda: staged_values(1, v_hi[:, 1], v_lo[:, 1])]})
            dve.wait_ge(v_split_lo, 2)
            take(B_Q0, 0, stage[:, 1, :])

            def group_pieces(g):
                def logits(u):
                    hh, t = divmod(u, TT)
                    n = P * (t + 1)
                    lg = lgs[u % 2]
                    if u == 0:
                        dve.wait_ge(toe_in, g * 16 + 16)
                    dve.wait_ge(s_ready, g * UNITS + u + 1)
                    dve.scalar_tensor_tensor(
                        halves(lg)[:, :, 0:n], halves(bx)[:, :, 0:n], DH ** -0.5,
                        toe[:, (hh + 1) * T - n:(hh + 1) * T].unsqueeze(1)
                        .broadcast_to([P, 2, n]), ALU.mult, ALU.add)
                    link(dve.scalar_tensor_tensor(
                        lg[:, 512:512 + N_CMP], by[:, 0:N_CMP], DH ** -0.5,
                        bias_c[:, t, :, bass.ds(g * HPG + hh, 1)].rearrange("p n o -> p (n o)"),
                        ALU.mult, ALU.add))
                    dve.tensor_reduce(nmax[:, 1:3], halves(lg)[:, :, 0:n], AX, ALU.max, negate=True)
                    dve.tensor_reduce(nmax[:, 0:1], lg[:, 512:512 + N_CMP], AX, ALU.max,
                                      negate=True).then_inc(l_done, 1)

                def weights(u):
                    hh, t = divmod(u, TT)
                    n = P * (t + 1)
                    lg = lgs[u % 2]
                    dve.wait_ge(e_done, g * UNITS + u + 1)
                    link(dve.reciprocal(coef[:, :], rsum[:, :]))
                    link(dve.tensor_tensor(coef[:, :], coef[:, :], flat(g_sig)[
                        :, bass.ds(3 * (g * HPG + hh) + t * N_GATE, 3)], ALU.mult))
                    for b in range(2):
                        dve.tensor_scalar(halves(lg)[:, b, 0:n], halves(lg)[:, b, 0:n],
                                          coef[:, 1 + b:2 + b], None, ALU.mult)
                    dve.scalar_tensor_tensor(lg[:, 512:512 + N_CMP], lg[:, 512:512 + N_CMP],
                                             coef[:, 0:1], cmp_01[:, t, :], ALU.mult, ALU.mult
                                             ).then_inc(p_done, 1)

                def weights_lo(u):
                    n = P * (u % TT + 1)
                    dve.wait_ge(pt_hi_done, g * UNITS + u + 1)
                    dve.tensor_tensor(halves(pt_lo)[:, :, 0:n], halves(bz)[:, :, 0:n],
                                      halves(pt_hi)[:, :, 0:n].bitcast(F32), ALU.subtract)
                    dve.tensor_tensor(pct_lo[0:N_CMP, :], bv[0:N_CMP, P:2 * P],
                                      pct_hi[0:N_CMP, :].bitcast(F32), ALU.subtract
                                      ).then_inc(pt_lo_done, 1)

                def take_gate():
                    dve.wait_ge(az_free, g + 1)
                    take(2 * g + B_NSA, 1, gate_buf[:, 1, :])

                entries = [(2, lambda: transposed(g + T_AQ, *two((q_hi, q_lo), lambda m: m))),
                           (16, take_gate)]
                gate = sigmoid((az_e, g + 1), ebuf, az_r, (19, 22, 25, 28))
                for u in range(UNITS):
                    s = UNIT0 + UNIT_STEP * u
                    entries += [(s + 2, lambda u=u: weights(u)),
                                (s + 3, lambda u=u: weights_lo(u))]
                entries += [(UNIT0 + UNIT_STEP * u, lambda u=u: logits(u)) for u in range(UNITS)]
                return piece_map(*entries, *gate)

            def group(g):
                b, pieces = 2 * g + B_NSA, group_pieces(g)
                for n in range(2):
                    stream(b + n, {s - n * PAIRS: f for s, f in pieces.items()
                                   if n * PAIRS <= s < (n + 1) * PAIRS}, first=True)
                dve.wait_ge(tr_done, g + (T_AQ + 1))
                take(b + 1, 0, stage[:, 1, :])

            with dve.Fori(0, GROUPS - 1) as g:
                chain.enter(g, GROUP_LINKS)
                group(g)
            chain.leave(GROUPS - 1)
            group(GROUPS - 1)

            dve.tensor_copy(m_wide, flat(m_neg).unsqueeze(2)
                            .broadcast_to([P, HEADS_M * TT, P])).then_inc(m_spread, 1)
            link(dve.memset(conv_in[:, :, 0:3], 0.0))

            def stabilisers():
                dve.wait_ge(nm_ready, 1)
                for i, bk in enumerate((by, bz)):
                    v = tiles(bk[:, :])
                    dve.tensor_copy(neg_m[:, 2 * i:2 * i + 2, :], v)
                    for hh in range(2):
                        last = dve.tensor_tensor(
                            neg_m_diag[:, 2 * i + hh, :].rearrange("p (a t) -> p a t", a=TT),
                            v[:, hh, :].rearrange("p (a t) -> p a t", a=TT),
                            diag_mask.unsqueeze(1).broadcast_to([P, TT, P]), ALU.add)
                last.then_inc(nm_done, 1)

            stabilisers()

            def head_pieces(h):
                b = 4 * h + B_MLSTM

                def conv_inputs():
                    dve.wait_ge(tr_hi, h + (T_MQK + 1))
                    link(dve.tensor_copy(conv_in[:, 2:4, 3:PADT], tiles(bx[:, :])))
                    dve.memset(spare[:, 2:3], 0.0).then_inc(tr_lo, 1)

                def conv(j):
                    for c in range(4):
                        w = conv_w[:, bass.ds(h * 8 + ((c // 2) * 8 + c % 2) * 4 + j, 1)]
                        if j == 0:
                            last = dve.tensor_scalar(qk[:, c, :], conv_in[:, c, 0:T], w, None,
                                                     ALU.mult)
                        else:
                            last = dve.scalar_tensor_tensor(
                                qk[:, c, :], conv_in[:, c, j:j + T], w, qk[:, c, :], ALU.mult,
                                ALU.add)
                    if j < 3:
                        link(last)
                    else:
                        last.then_inc(conv_done, 1)

                def qk_lo_part():
                    dve.wait_ge(qk_hi_done, h + 1)
                    dve.tensor_tensor(qk_lo[:, :, :], qk[:, :, :], qk_hi[:, :, :].bitcast(F32),
                                      ALU.subtract).then_inc(qk_lo_done, 1)

                def scores():
                    dve.wait_ge(st_ready, h + 1)
                    dve.wait_ge(wexp_done, h + 1)
                    dve.scalar_tensor_tensor(sw[:, :], bx[:, 0:384], QK_M ** -0.5, wexp[:, :],
                                             ALU.mult, ALU.mult).then_inc(sw_done, 1)

                def scores_lo():
                    dve.wait_ge(sw_hi_done, h + 1)
                    dve.tensor_tensor(sw_lo[:, :], sw[:, :], sw_hi[:, :].bitcast(F32),
                                      ALU.subtract).then_inc(sw_lo_done, 1)

                def normalise(t):
                    if t == 0:
                        dve.wait_ge(num_ready, h + 1)
                        link(dve.tensor_copy(den[:, :], bv[:, 0:2 * TT:2]))
                        link(dve.scalar_tensor_tensor(den[:, :], den[:, :], -1.0, den[:, :],
                                                      ALU.mult, ALU.max))
                        link(dve.tensor_tensor(den[:, :], den[:, :], e_neg_m[
                            :, :, bass.ds(h, 1)].rearrange("p a o -> p (a o)"), ALU.max))
                        link(dve.reciprocal(den[:, :], den[:, :]))
                    last = dve.tensor_scalar(hm[:, t, :], (by, bz)[t][:, :], den[:, t:t + 1], None,
                                             ALU.mult)
                    if t == 1:
                        last.then_inc(hm_done, 1)

                def output_gate():
                    dve.wait_ge(hm_done, h + 1)
                    dve.wait_ge(mo_r, h + 1)
                    dve.tensor_tensor(hm[:, :, :], hm[:, :, :], ebuf[:, :, :],
                                      ALU.mult).then_inc(ho_done, 1)

                return {0: piece_map((2, conv_inputs), *[(3 + j, lambda j=j: conv(j))
                                                         for j in range(4)],
                                     *sigmoid((conv_e, h + 1), qk_sig, conv_r, (8, 9, 10, 11)),
                                     (14, qk_lo_part)),
                        1: piece_map((0, scores),
                                     (1, lambda: staged_values(h + 2, mv_hi[:, :, :],
                                                               mv_lo[:, :, :])),
                                     (2, scores_lo),
                                     (5, lambda: normalise(0)), (6, lambda: normalise(1))),
                        2: piece_map(*sigmoid((mo_e, h + 1), ebuf, mo_r, (2, 3, 4, 5)),
                                     (6, output_gate))}

            def silu_gate(h):
                return sigmoid((mz_e, h + 1), ebuf, mz_r, (2, 3, 4, 5))

            def head_output(h):
                dve.wait_ge(mz_done, h + 1)
                for t in range(TT):
                    last = dve.scalar_tensor_tensor(mix_m[:, t, bass.ds(h * BW, BW)], hm[:, t, :],
                                                    hr[:, t:t + 1], gate_buf[:, t, :],
                                                    ALU.mult, ALU.mult)
                last.then_inc(ym_done, 1)

            def mix_lo(c):
                x_lo(PAIRS + c, gain_mix, (by, bz))

            def head(h, blocks, last={}):
                b, pieces = 4 * h + B_MLSTM, head_pieces(h)
                for c, late in last.items():
                    pieces[2].setdefault(c, []).extend(late)
                pieces[3] = piece_map(*silu_gate(h), (8, lambda: head_output(h)))
                stage_free = ((tr_done, h + (T_MQK + 1)), (v_split_lo, h + 3), (mo_e, h + 1),
                              (mz_done, h + 1))
                for n in range(blocks):
                    stream(b + n, pieces.get(n))
                    dve.wait_ge(*stage_free[n])
                    take(b + n, 1 - n % 2, stage[:, 1, :])

            with dve.Fori(0, HEADS_M - 1) as h:
                chain.enter(h, HEAD_LINKS)
                head(h, 4)
            chain.leave(HEADS_M - 1)
            head(HEADS_M - 1, 3, {c + 2: [lambda c=c: mix_lo(c)] for c in range(MIX_EARLY)})

            def add_residual(n, i, parity, turn):
                cols = bass.ds(n * BW, BW)
                dve.wait_ge(acc0_full, n + (B_OUT + 1))
                dve.wait_ge(xr_in[i], turn)
                dve.tensor_tensor(res[:, 0, cols], acc[parity][0][:, :], xres[:, i, 0, :],
                                  ALU.add).then_inc(out0_free, 1)
                dve.wait_ge(pe_used, n * PAIRS + ((B_OUT + 1) * PAIRS + EXTRA))
                dve.tensor_tensor(res[:, 1, cols], acc[parity][1][:, :], xres[:, i, 1, :],
                                  ALU.add).then_inc(out1_free, 1)

            late = piece_map(*silu_gate(HEADS_M - 1), (8, lambda: head_output(HEADS_M - 1)))
            for c in range(PAIRS):
                if MIX_LATE <= c < MIX_LATE + PAIRS - MIX_EARLY:
                    mix_lo(MIX_EARLY + c - MIX_LATE)
                slot(B_OUT, c)
                for piece in late.get(c, ()):
                    piece()
            add_residual(0, 0, 0, 16)
            stream(B_OUT + 1)
            add_residual(1, 1, 1, 16)
            with dve.Fori(1, 3) as i:
                stream(2 * i + B_OUT)
                add_residual(2 * i, 0, 0, i * 16 + 16)
                stream(2 * i + (B_OUT + 1))
                add_residual(2 * i + 1, 1, 1, i * 16 + 16)
            stream(B_OUT + 6)
            add_residual(6, 0, 0, 64)
            for c in range(PAIRS - LOOKAHEAD):
                slot(B_OUT + 7, c)
            add_residual(7, 1, 1, 64)
            dve.wait_ge(sq_done, N_OUT)
            dve.tensor_reduce(ss[:, :], ssf[:, :, :], AX, ALU.add).then_inc(ssf_sum, 1)
            dve.wait_ge(fr_done, 1)
            dve.wait_ge(gained, N_OUT)
            for i in range(4):
                cols = slice(i * 1024, (i + 1) * 1024)
                dve.tensor_scalar(res[:, 1, cols], res[:, 1, cols], fr[:, 1:2], None,
                                  ALU.mult).then_inc(y1_done, 1)

        @block.gpsimd
        def _(pool):
            chain = Count()

            def link(ins):
                chain.n += 1
                ins.then_inc(pool_chain, 1)
                pool.wait_ge(pool_chain, chain.value())

            def rsqrt_mean(dst, src, n):
                link(pool.tensor_scalar(dst[:, :], src[:, :], 1.0 / n, EPS, ALU.mult, ALU.add))
                return pool.tensor_tensor(dst[:, :], dst[:, :], m_half[:, :], ALU.pow)

            pool.wait_ge(pre_dve, 3)
            rsqrt_mean(rstd, ss, D).then_inc(pre_pool, 1)
            pool.memset(gate_buf[:, 0, 0:1], 0.0).then_inc(az_free, 1)
            pool.wait_ge(ht_lo, PAIRS)
            for j in range(2):
                for m in cin[j]:
                    pool.memset(m[:, 0:GROUPS, T:CPAD].bitcast(F32), 0.0)
                    last = pool.memset(m[:, 4, :].bitcast(F32), 0.0)
            last.then_inc(pre_pool, 1)
            pool.wait_ge(pre_dve, 7)
            pool.tensor_tensor(hid[:, :], hid[:, :], hid_e[:, :], ALU.mult
                               ).then_inc(pre_pool, 1)

            def group(g):
                pool.wait_ge(az_r, g + 1)
                pool.tensor_tensor(gate_buf[:, :, :], gate_buf[:, :, :], ebuf[:, :, :], ALU.mult
                                   ).then_inc(az_mul, 1)
                pool.wait_ge(az_mul, g + 1)
                pool.wait_ge(o_done, g * UNITS + UNITS)
                dst = mix_a[:, :, bass.ds(g * BW, BW)]
                pool.tensor_tensor(dst, dst, gate_buf[:, :, :], ALU.mult).then_inc(az_free, 1)

            with pool.Fori(0, GROUPS - 1) as g:
                group(g)
            group(GROUPS - 1)

            def head(h):
                pool.wait_ge(conv_r, h + 1)
                pool.tensor_tensor(qk[:, :, :], qk[:, :, :], qk_sig, ALU.mult
                                   ).then_inc(qk_done, 1)
                pool.wait_ge(ssm_done, h + 1)
                link(pool.tensor_tensor(hr[:, :], ssm[:, :], eps_m[:, :], ALU.add))
                link(pool.tensor_tensor(hr[:, :], hr[:, :], inv_m[:, :], ALU.mult))
                pool.tensor_tensor(hr[:, :], hr[:, :], m_half[:, :], ALU.pow).then_inc(hr_done, 1)
                pool.wait_ge(mz_r, h + 1)
                pool.tensor_tensor(gate_buf[:, :, :], stage[:, :, :], ebuf[:, :, :], ALU.mult
                                   ).then_inc(mz_done, 1)

            with pool.Fori(0, HEADS_M - 1) as h:
                chain.enter(h, 2)
                head(h)
            chain.leave(HEADS_M - 1)
            head(HEADS_M - 1)

            pool.wait_ge(gf_in, 16)
            with pool.Fori(0, N_OUT) as n:
                pool.wait_ge(sq_done, n + 1)
                for t in range(TT):
                    dst = res[:, t, bass.ds(n * BW, BW)]
                    last = pool.tensor_tensor(dst, dst, gain_f[:, bass.ds(n * BW, BW)], ALU.mult)
                last.then_inc(gained, 1)
            pool.wait_ge(ssf_sum, 1)
            rsqrt_mean(fr, ss, D).then_inc(fr_done, 1)


GROUP_LINKS = 3 * UNITS + 1
HEAD_LINKS = 1 + 3 + 1 + 4 + 1 + 1


def shape_constants():
    s, t = np.arange(P)[:, None], np.arange(P)[None, :]
    tri = (s <= t).astype(np.float32)
    end = np.arange(N_CMP) * CMP_S + CMP_L - 1
    seen = (np.arange(T)[:, None] >= end[None, :]).astype(np.float32)
    seen = seen.reshape(TT, P, N_CMP).transpose(1, 0, 2).reshape(P, TT * N_CMP)
    const128 = np.concatenate([np.eye(P, dtype=np.float32), tri,
                               np.where(tri > 0, np.float32(0), np.float32(NEG)),
                               np.where(seen > 0, np.float32(0), np.float32(NEG)), seen], axis=1)
    n = np.arange(T)
    exact = BUCKETS // 2
    nf = np.maximum(n, exact).astype(np.float32)
    large = exact + (np.log(nf / np.float32(exact)) / np.float32(math.log(1024 / exact))
                     * np.float32(BUCKETS - exact)).astype(np.int32)
    bucket = np.where(n < exact, n, np.minimum(large, BUCKETS - 1))
    const32 = np.zeros((BUCKETS, 1024), np.float32)
    const32[bucket, 255 + n] = 1
    const32[bucket, 512 + 255 - n] = 1
    const16 = np.zeros((HEADS_A, TOE), np.float32)
    const16[:, T:] = NEG
    return const128.astype(np.float32), const32, const16


def kernel(x, norm_gain, w_in, w_conv, b_igate, b_fgate, mlstm_norm_gain,
           cmp_k_pos, cmp_k_w1, cmp_k_w2, cmp_v_pos, cmp_v_w1, cmp_v_w2,
           rel_bias, w_out, final_norm_gain):
    import concourse.bacc as bacc
    from concourse.bass_utils import run_bass_kernel_spmd

    const128, const32, const16 = shape_constants()
    arrays = dict(x=x, norm_gain=norm_gain, w_in=w_in, w_conv=w_conv, b_igate=b_igate,
                  b_fgate=b_fgate, mlstm_norm_gain=mlstm_norm_gain, cmp_k_pos=cmp_k_pos,
                  cmp_k_w1=cmp_k_w1, cmp_k_w2=cmp_k_w2, cmp_v_pos=cmp_v_pos, cmp_v_w1=cmp_v_w1,
                  cmp_v_w2=cmp_v_w2, rel_bias=rel_bias, w_out=w_out,
                  final_norm_gain=final_norm_gain, const128=const128, const32=const32,
                  const16=const16)
    nc = bacc.Bacc("TRN2", target_bir_lowering=False, num_devices=1)
    feed, args = {}, []
    for name, a in arrays.items():
        a = np.ascontiguousarray(a)
        feed[f"in_{name}"] = a
        args.append(nc.dram_tensor(f"in_{name}", a.shape, mybir.dt.from_np(a.dtype),
                                   kind="ExternalInput").ap())
    out = nc.dram_tensor("out_y", (1, T, D), F32, kind="ExternalOutput").ap()
    hybrid_layer(nc, *args, out)
    r = run_bass_kernel_spmd(nc, [feed], core_ids=[0])
    return r.results[0]["out_y"]
```

```python
import math
from contextlib import ExitStack

import numpy as np
import concourse.bass as bass
from concourse import mybir

F32 = mybir.dt.float32
F32R = mybir.dt.float32r
ALU = mybir.AluOpType
ACT = mybir.ActivationFunctionType
AX = mybir.AxisListType.X

P = 128
T = 256
TT = T // P
D = 4096
KT_IN = D // P
BW = 512
PAIRS = KT_IN // 2
RING = 4
LOADED = 32
LOOKAHEAD = 3
HEADS_M, QK_M, V_M = 4, 256, 512
GROUPS, HPG, DH = 4, 4, 128
HEADS_A = GROUPS * HPG
N_CMP, CMP_L, CMP_S = 15, 32, 16
BUCKETS = 32
EPS = 1e-6
NEG = -1e30

C_MQ, C_MK, C_MV, C_MO, C_MZ = 0, 1024, 2048, 4096, 6144
C_IF = 8192
C_AQ = 8200
C_KV = 10248
C_GATE = 13320
C_AZ = 13368
N_IF, N_GATE = 2 * HEADS_M, 3 * HEADS_A
N_SMALL = N_IF + N_GATE

B_KV, B_Q0, B_NSA, B_MLSTM, B_OUT = 0, 6, 7, 15, 30
N_OUT = D // BW
SMALL_PAIRS, CMP_PAIRS = 4, 4
EXTRA = SMALL_PAIRS + 2 * CMP_PAIRS
SMALL_K = KT_IN // SMALL_PAIRS
CMP_PL = CMP_S // CMP_PAIRS
MIXED = 2


def mixed_block():
    steps, extras = [], list(range(EXTRA))
    for c in range(PAIRS):
        if c % 2 == 1 or c >= 2 * SMALL_PAIRS:
            steps.append((extras.pop(0), None))
        steps.append((None, c))
    assert not extras
    return [(MIXED * PAIRS + j, *step) for j, step in enumerate(steps)]


UNIT0, UNIT_STEP, UNITS = 3, 3, HPG * TT
TOE = 383
NP16 = 16
CHUNKS = T // CMP_S
CIN = GROUPS * T + CMP_L
ROWS = CIN // CMP_S


MIX_EARLY, MIX_LATE = PAIRS - 2, 11


class Count:

    def __init__(self):
        self.base, self.n, self.i, self.per = 0, 0, None, 0

    def enter(self, i, per):
        self.base, self.n, self.i, self.per = self.base + self.n, 0, i, per

    def leave(self, turns):
        assert self.n == self.per, (self.n, self.per)
        self.base, self.n, self.i = self.base + self.per * turns, 0, None

    def value(self):
        v = self.base + self.n
        return v if self.i is None else self.i * self.per + v


def flat(ap):
    return ap.rearrange("p a b -> p (a b)")


def hybrid_layer(nc, x, norm_gain, w_in, w_conv, b_igate, b_fgate, mlstm_norm_gain,
                 cmp_k_pos, cmp_k_w1, cmp_k_w2, cmp_v_pos, cmp_v_w1, cmp_v_w2,
                 rel_bias, w_out, final_norm_gain, const128, const32, const16, out):
    ctx = ExitStack()
    with ctx:
        def sb(name, cols, dt=F32, parts=P):
            return ctx.enter_context(nc.sbuf_tensor(name, [parts, cols], dt))

        def sem(name):
            return ctx.enter_context(nc.semaphore(name))

        def bank(name):
            return ctx.enter_context(nc.psum_tensor(name, [P, 512], F32))

        lhs_hi = sb("lhs_hi", KT_IN * T, F32R)[:, :].rearrange("p (k t) -> p k t", t=T)
        lhs_lo = sb("lhs_lo", KT_IN * T, F32R)[:, :].rearrange("p (k t) -> p k t", t=T)
        w_raw = sb("w_raw", RING * 2 * BW)
        w_split = sb("w_split", 2 * RING * 2 * BW, F32R)[:, :].rearrange("p (s c) -> p s c", s=2)
        w_hi, w_lo = w_split[:, 0], w_split[:, 1]

        KIB = 1024
        arena_start = (nc.sbuf_base + 31) // 32 * 32
        sb("arena", (32 * KIB + 55552) // 4)

        def at(name, kib, cols, dt=F32, parts=P):
            return nc.alloc_sbuf_tensor_at(name, [parts, cols], dt,
                                           offset=arena_start + int(kib * KIB))

        wide = at("wide", 0, TT * D)
        x_nat = wide[:, :].rearrange("p (a d) -> p a d", a=TT)
        mix_a = wide[:, 0:D].rearrange("p (a c) -> p a c", a=TT)
        mix_m = wide[:, D:2 * D].rearrange("p (a c) -> p a c", a=TT)
        res = x_nat
        cin = [[at(f"cmp_{kind}_{part}", (2 * i + j) * 5.5, CIN, F32R)[:, :]
                for j, part in enumerate(("hi", "lo"))] for i, kind in enumerate("kv")]

        def by_group(m):
            return m[:, 0:GROUPS * T].rearrange("p (g t) -> p g t", t=T)

        k_hi, k_lo = [at(n, 16 + 8 * i, 2 * GROUPS * T, F32R)[:, :].rearrange(
            "p (j g t) -> p j g t", j=2, g=GROUPS) for i, n in enumerate(("k_hi", "k_lo"))]

        Z = 32
        stage = at("stage", Z, TT * BW)[:, :].rearrange("p (a c) -> p a c", a=TT)
        ebuf = at("ebuf", Z + 4, TT * BW)[:, :].rearrange("p (a c) -> p a c", a=TT)
        gate_buf = at("gate_buf", Z + 8, TT * BW)[:, :].rearrange("p (a c) -> p a c", a=TT)
        toe = at("toe", Z + 12, HPG * T)
        v_split = at("v_split", Z + 16, 2 * 2 * TT * BW, F32R)[:, :].rearrange(
            "p (s j a c) -> p s j a c", s=2, j=2, a=TT)
        v_hi, v_lo = v_split[:, 0], v_split[:, 1]
        q_hi, q_lo = [at(n, Z + 32 + 4 * i, HPG * T, F32R)[:, :].rearrange(
            "p (h t) -> p h t", t=T) for i, n in enumerate(("q_hi", "q_lo"))]
        lgs = [at(f"lg{i}", Z + 40 + 2.0625 * i, 512 + NP16) for i in range(2)]
        pt_hi, pt_lo = [at(n, Z + 44.25 + 2 * i, 512, F32R) for i, n in enumerate(("pt_hi", "pt_lo"))]
        pct_hi, pct_lo = [at(n, Z + 48.25 + 0.5 * i, P, F32R)
                          for i, n in enumerate(("pct_hi", "pct_lo"))]
        vc_split = at("vc_split", Z + 49.25, 2 * GROUPS * P, F32R)[:, :].rearrange(
            "p (s c) -> p s c", s=2)
        vc_hi, vc_lo = vc_split[:, 0], vc_split[:, 1]
        hm = at("hm", Z + 12, TT * BW)[:, :].rearrange("p (a c) -> p a c", a=TT)
        m_wide = at("m_wide", Z + 12, 8 * P)[:, :].rearrange("p (i m) -> p i m", m=P)
        PADT = T + 3
        conv_in = at("conv_in", Z + 16, 4 * PADT)[:, :].rearrange("p (c t) -> p c t", t=PADT)
        qk = at("qk", Z + 20.25, 4 * T)[:, :].rearrange("p (c t) -> p c t", t=T)
        qk_sig = flat(ebuf).rearrange("p (c t) -> p c t", t=T)
        qk_hi, qk_lo = [at(n, Z + 24.25 + 4 * i, 4 * T, F32R)[:, :].rearrange(
            "p (c t) -> p c t", t=T) for i, n in enumerate(("qk_hi", "qk_lo"))]
        mv_hi, mv_lo = [at(n, Z + 32.25 + 4 * i, TT * BW, F32R)[:, :].rearrange(
            "p (a c) -> p a c", a=TT) for i, n in enumerate(("mv_hi", "mv_lo"))]
        neg_m = at("neg_m", Z + 40.25, HEADS_M * T)[:, :].rearrange("p (h t) -> p h t", t=T)
        neg_m_diag = at("neg_m_diag", Z + 44.25, HEADS_M * T)[:, :].rearrange(
            "p (h t) -> p h t", t=T)
        wexp = at("wexp", Z + 48.25, 384)
        sw = at("sw", Z + 49.75, 384)
        sw_hi, sw_lo = [at(n, Z + 51.25 + 1.5 * i, 384, F32R) for i, n in enumerate(("sw_hi", "sw_lo"))]
        gain_f = at("gain_f", Z + 16, D)
        xres = at("xres", Z + 32, 2 * TT * BW)[:, :].rearrange("p (n a c) -> p n a c", n=2, a=TT)
        hot = at("hot", Z + 16, 1024, parts=BUCKETS)
        hot_up, hot_down = hot[:, 0:511], hot[:, 512:512 + TOE]
        hot_r = at("hot_r", Z + 43, 511, F32R, parts=BUCKETS)
        toe_mask = at("toe_mask", Z + 20, TOE, parts=HEADS_A)
        toe_row = at("toe_row", Z + 22, TOE, parts=HEADS_A)
        conv_rows = at("conv_rows", Z + 24, 16 * P, parts=4)
        gain_rows = at("gain_rows", Z + 32, P, parts=KT_IN)
        pos_rows = at("pos_rows", Z + 32.5, 2 * P, parts=CMP_L)
        gain_m_rows = at("gain_m_rows", Z + 33.5, P, parts=KT_IN // 2)
        junk = at("junk", Z + 36, 1024)
        hid_n = at("hid_n", Z + 43, 2 * 2 * P, parts=ROWS)
        hid = at("hid", Z + 40, 2 * 64)
        hid_e = at("hid_e", Z + 40.5, 2 * 64)
        a_row = at("a_row", Z + 41, T, parts=4)
        m_row = at("m_row", Z + 42, T, parts=4)

        c128 = sb("c128", const128.shape[1])
        ident = c128[:, 0:P]
        tri = c128[:, P:2 * P]
        diag_mask = c128[:, 2 * P:3 * P]
        o = 3 * P
        cmp_neg = c128[:, o:o + TT * N_CMP].rearrange("p (a n) -> p a n", a=TT)
        cmp_01 = c128[:, o + TT * N_CMP:o + 2 * TT * N_CMP].rearrange("p (a n) -> p a n", a=TT)
        rb = sb("rb", HEADS_A, parts=BUCKETS)
        rb_split = sb("rb_split", 2 * HEADS_A, F32R, parts=BUCKETS)
        ones = sb("ones", P)
        ones_r = sb("ones_r", 2, F32R)
        gain_t = sb("gain_t", KT_IN)
        gain_mix = sb("gain_mix", KT_IN)
        pos_t = sb("pos_t", 2 * CMP_L)
        conv_w = sb("conv_w", 16 * 4)
        w2 = sb("w2", 2 * P)
        b_if = sb("b_if", N_IF)
        ss8 = sb("ss8", TT * 4)[:, :].rearrange("p (a n) -> p a n", a=TT)
        ss = sb("ss", TT)
        rstd = sb("rstd", TT)
        m_half = sb("m_half", TT)
        eps_m = sb("eps_m", TT)
        inv_m = sb("inv_m", TT)

        def by_head(name, n=HEADS_M):
            return sb(name, TT * n)[:, :].rearrange("p (a n) -> p a n", a=TT)

        small = by_head("small", N_SMALL)
        g_sig = by_head("g_sig", N_GATE)
        f_abs, log_f, f_cum = by_head("f_abs"), by_head("log_f"), by_head("f_cum")
        a_col, e_neg_m = by_head("a_col"), by_head("e_neg_m")
        m_neg = sb("m_neg", TT * HEADS_M)[:, :].rearrange("p (h a) -> p h a", a=TT)
        hid_b = sb("hid_b", 2)
        kc_split = sb("kc_split", 2 * GROUPS * NP16, F32R)[:, :].rearrange("p (s c) -> p s c", s=2)
        kc_hi, kc_lo = kc_split[:, 0], kc_split[:, 1]
        bias_c = sb("bias_c", TT * N_CMP * HEADS_A)[:, :].rearrange(
            "p (a n h) -> p a n h", a=TT, h=HEADS_A)
        nmax = sb("nmax", 3)
        rsum = sb("rsum", 3)
        coef = sb("coef", 3)
        den = sb("den", TT)
        ssm = sb("ssm", TT)
        hr = sb("hr", TT)
        ssf = by_head("ssf", N_OUT)
        fr = sb("fr", TT)
        spare = sb("spare", 3)

        acc = [[bank("acc_a0"), bank("acc_a1")], [bank("acc_b0"), bank("acc_b1")]]
        bx, by, bz, bv = bank("bank_x"), bank("bank_y"), bank("bank_z"), bank("bank_v")

        def halves(t):
            return t[:, 0:512].rearrange("p (b s) -> p b s", b=2)

        toe_dram = nc.dram_tensor("toe_dram", (HEADS_A, P, TOE), F32, kind="Internal")

        x_in = [sem(f"x_in{i}") for i in range(8)]
        first_in = sem("first_in")
        consts_in = sem("consts_in")
        w_loaded = [sem(f"w_loaded{i}") for i in range(RING)]
        hi_done = sem("hi_done")
        lo_done = sem("lo_done")
        pe_used = sem("pe_used")
        acc0_full = sem("acc0_full")
        acc0_free = sem("acc0_free")
        acc1_free = sem("acc1_free")
        act_chain = sem("act_chain")
        dve_chain = sem("dve_chain")
        pool_chain = sem("pool_chain")
        pre_pe, pre_dve, pre_act, pre_pool = [sem(f"pre_{e}") for e in ("pe", "dve", "act", "pool")]
        ht_ready = sem("ht_ready")
        ht_hi = sem("ht_hi")
        ht_lo = sem("ht_lo")
        toe_out = sem("toe_out")
        toe_in = sem("toe_in")
        tr_done = sem("tr_done")
        tr_hi = sem("tr_hi")
        tr_lo = sem("tr_lo")
        v_split_hi = sem("v_split_hi")
        v_split_lo = sem("v_split_lo")
        s_ready = sem("s_ready")
        l_done = sem("l_done")
        e_done = sem("e_done")
        p_done = sem("p_done")
        pt_ready = sem("pt_ready")
        pt_hi_done = sem("pt_hi_done")
        pt_lo_done = sem("pt_lo_done")
        o_ready = sem("o_ready")
        o_done = sem("o_done")
        az_e = sem("az_e")
        az_r = sem("az_r")
        az_mul = sem("az_mul")
        az_free = sem("az_free")
        m_spread = sem("m_spread")
        nm_ready = sem("nm_ready")
        rb_hi_done = sem("rb_hi_done")
        rb_lo_done = sem("rb_lo_done")
        nm_done = sem("nm_done")
        conv_done = sem("conv_done")
        conv_e = sem("conv_e")
        conv_r = sem("conv_r")
        qk_done = sem("qk_done")
        qk_hi_done = sem("qk_hi_done")
        qk_lo_done = sem("qk_lo_done")
        wexp_done = sem("wexp_done")
        st_ready = sem("st_ready")
        sw_done = sem("sw_done")
        sw_hi_done = sem("sw_hi_done")
        sw_lo_done = sem("sw_lo_done")
        num_ready = sem("num_ready")
        hm_done = sem("hm_done")
        mo_e = sem("mo_e")
        mo_r = sem("mo_r")
        ho_done = sem("ho_done")
        ssm_done = sem("ssm_done")
        hr_done = sem("hr_done")
        mz_e = sem("mz_e")
        mz_r = sem("mz_r")
        mz_done = sem("mz_done")
        ym_done = sem("ym_done")
        xr_in = [sem("xr_in0"), sem("xr_in1")]
        out0_free = sem("out0_free")
        out1_free = sem("out1_free")
        sq_done = sem("sq_done")
        sq_last = sem("sq_last")
        gained = sem("gained")
        gf_in = sem("gf_in")
        ssf_sum = sem("ssf_sum")
        fr_done = sem("fr_done")
        y0_done = sem("y0_done")
        y1_done = sem("y1_done")
        y0_last = sem("y0_last")
        stored = sem("stored")

        block = ctx.enter_context(nc.Block())

        N_CONST = 11
        Y_COLS = D // 4
        LAST = (N_OUT - 1) * BW
        XC = 512
        T_CK, T_CV, T_SK, T_WK, T_AQ, T_MQK = 0, 1, 2, 3, 4, 8

        def piece_map(*entries):
            found = {}
            for slot, piece in entries:
                found.setdefault(slot, []).append(piece)
            return found

        @block.sync
        def _(sp):
            extra = 0

            def fetch(q, s, parts):
                if not isinstance(q, int) or q >= RING:
                    sp.wait_ge(lo_done, q - RING + 1)
                for dst, src in parts:
                    sp.dma_start(dst, src).then_inc(w_loaded[s], LOADED // len(parts))

            def slot_of(s, k=0, n=2):
                return w_raw[:, (2 * s + k) * BW:(2 * s + k + n) * BW]

            def rows(w, c):
                return w[c * 2 * P:(c + 1) * 2 * P, :].rearrange("(k p) n -> p k n", p=P)

            def columns(b, col, pairs=range(PAIRS)):
                for c in pairs:
                    fetch(b * PAIRS + (c + extra), c % RING,
                          [(slot_of(c % RING), rows(w_in, c)[:, :, bass.ds(col, BW)])])

            def mlstm_qk(b, h):
                for c in range(PAIRS):
                    fetch(b * PAIRS + (c + extra), c % RING,
                          [(slot_of(c % RING, k, 1), w_in[
                              (2 * c + k) * P:(2 * c + k + 1) * P, C_MQ:C_MV].rearrange(
                              "p (s n) -> p s n", s=2)[:, :, bass.ds(h * QK_M, QK_M)])
                           for k in range(2)])

            def fetch_x(i):
                sp.dma_start(x_nat[:, :, i * XC:(i + 1) * XC],
                             x[0, :, i * XC:(i + 1) * XC].rearrange("(a p) d -> p a d", p=P)
                             ).then_inc(x_in[i], 16)

            fetch_x(0)
            columns(0, C_KV, [0])
            fetch_x(1)
            columns(0, C_KV, [1])
            fetch_x(2)
            columns(0, C_KV, [2])
            fetch_x(3)
            columns(0, C_KV, [3])
            for i in range(4, 8):
                fetch_x(i)
            loads = [
                (hot[:, :], const32), (toe_mask[:, :], const16), (rb[:, :], rel_bias),
                (gain_m_rows[:, :], mlstm_norm_gain.rearrange("(k p) -> k p", p=P)),
                (pos_rows[:, 0:P], cmp_k_pos), (pos_rows[:, P:2 * P], cmp_v_pos),
                (conv_rows[:, :], w_conv), (w2[:, 0:P], cmp_k_w2), (w2[:, P:2 * P], cmp_v_w2),
            ] + [(b_if[:, i * HEADS_M:(i + 1) * HEADS_M],
                  src.rearrange("(o n) -> o n", o=1).broadcast_to([P, HEADS_M]))
                 for i, src in enumerate((b_igate, b_fgate))]
            assert len(loads) == N_CONST
            for c in range(RING, PAIRS):
                columns(0, C_KV, [c])
                for dst, src in loads[2 * (c - RING):2 * (c - RING) + 2]:
                    sp.dma_start(dst, src).then_inc(consts_in, 16)
            columns(1, C_KV + BW)

            def extra_pair(q, i):
                s = q % RING
                if i < SMALL_PAIRS:
                    dst = slot_of(s)[:, 0:SMALL_K * N_SMALL].rearrange(
                        "p (k n) -> p k n", n=N_SMALL)
                    src = w_in[i * SMALL_K * P:(i + 1) * SMALL_K * P, :].rearrange(
                        "(k p) n -> p k n", p=P)
                    fetch(q, s, [(dst[:, :, 0:N_IF], src[:, :, C_IF:C_IF + N_IF]),
                                 (dst[:, :, N_IF:], src[:, :, C_GATE:C_GATE + N_GATE])])
                else:
                    j, i = divmod(i - SMALL_PAIRS, CMP_PAIRS)
                    fetch(q, s, [(slot_of(s, half, 1).rearrange("p (l e) -> p l e", e=P),
                                  (cmp_k_w1, cmp_v_w1)[j][
                                      half * CMP_S + i * CMP_PL:half * CMP_S + (i + 1) * CMP_PL]
                                  .rearrange("l d e -> d l e")) for half in range(2)])

            for q, i, c in mixed_block():
                if i is not None:
                    extra_pair(q, i)
                else:
                    fetch(q, q % RING, [(slot_of(q % RING), rows(w_in, c)[
                        :, :, C_KV + MIXED * BW:C_KV + (MIXED + 1) * BW])])
            extra = EXTRA
            for b in range(MIXED + 1, 6):
                columns(b, C_KV + b * BW)
            columns(B_Q0, C_AQ)
            with sp.Fori(0, GROUPS - 1) as g:
                columns(2 * g + B_NSA, g * BW + C_AZ)
                columns(2 * g + B_NSA + 1, g * BW + C_AQ + BW)
            columns(B_MLSTM - 2, C_AZ + 3 * BW)
            mlstm_qk(B_MLSTM - 1, 0)
            with sp.Fori(1, HEADS_M) as h:
                columns(4 * h + B_MLSTM - 4, h * BW + C_MV - BW)
                columns(4 * h + B_MLSTM - 3, h * BW + C_MO - BW)
                columns(4 * h + B_MLSTM - 2, h * BW + C_MZ - BW)
                mlstm_qk(4 * h + B_MLSTM - 1, h)
            for n, col in enumerate((C_MV, C_MO, C_MZ)):
                columns(B_OUT - 3 + n, col + 3 * BW)
            with sp.Fori(1, N_OUT + 1) as n:
                for c in range(PAIRS):
                    fetch((n + B_OUT - 1) * PAIRS + (c + extra), c % RING,
                          [(slot_of(c % RING), rows(w_out, (c + PAIRS // 2) % PAIRS)[
                              :, :, bass.ds(n * BW - BW, BW)])])
            y_dram = out[0].rearrange("(a p) d -> p a d", p=P)
            for t, done in enumerate((y0_done, y1_done)):
                for i in range(4):
                    cols = slice(i * Y_COLS, (i + 1) * Y_COLS)
                    sp.wait_ge(done, i + 1)
                    if (t, i) == (0, 3):
                        sp.wait_ge(y0_last, 1)
                    sp.dma_start(y_dram[:, t, cols], res[:, t, cols]).then_inc(stored, 16)
            sp.wait_ge(stored, 2 * 4 * 16)

        @block.tensor
        def _(pe):
            extra = 0

            def passes(dst, a, b, start, stop):
                pe.matmul(dst, a[0], b[0], start=start, stop=False)
                pe.matmul(dst, a[0], b[1], start=False, stop=False)
                return pe.matmul(dst, a[1], b[0], start=False, stop=stop)

            def two_products(dst, n, a, both, start, stop):
                pe.matmul(dst[:, 0:2 * n], a[0], both, start=start, stop=False)
                return pe.matmul(dst[:, 0:n], a[1], both[:, 0], start=False, stop=stop)

            def wide(parity, t, kk, s, k):
                cols = slice((2 * s + k) * BW, (2 * s + k + 1) * BW)
                toks = slice(t * P, (t + 1) * P)
                return passes(acc[parity][t][:, :], (lhs_hi[:, kk, toks], lhs_lo[:, kk, toks]),
                              (w_hi[:, cols], w_lo[:, cols]), kk == 0, kk == KT_IN - 1)

            def pair(b, c, parity, free=None):
                s = c % RING
                pe.wait_ge(lo_done, b * PAIRS + (c + extra + 1))
                for t in range(TT):
                    if c == 0 and free is not None:
                        pe.wait_ge(*free[t])
                    for k in range(2):
                        last = wide(parity, t, 2 * c + k, s, k)
                    if c == PAIRS - 1 and t == 0:
                        last.then_inc(acc0_full, 1)
                last.then_inc(pe_used, 1)

            def stream(b, parity, pieces=None):
                free = None
                if not isinstance(b, int) or b >= 2:
                    free = ((acc0_free, b - 1), (acc1_free, b - 1))
                for c in range(PAIRS):
                    for piece in (pieces or {}).get(c, ()):
                        piece()
                    pair(b, c, parity, free)

            def transpose_stage(event, b):
                pe.wait_ge(acc0_free, b + 1)
                pe.wait_ge(acc1_free, b + 1)
                if not isinstance(event, int) or event > 0:
                    pe.wait_ge(tr_lo, event)
                for cc in range(4):
                    for t in range(TT):
                        o = (cc % 2) * T + t * P
                        last = pe.transpose((bv, bx)[cc // 2][:, o:o + P],
                                            stage[:, t, cc * P:(cc + 1) * P], ident)
                last.then_inc(tr_done, 1)

            def x_t(c):
                if c % 2 == 0:
                    pe.wait_ge(x_in[c // 2], 16)
                if c >= 2:
                    pe.wait_ge(ht_lo, c - 1)
                for k in range(2):
                    for t in range(TT):
                        last = pe.transpose(acc[1][c % 2][:, k * T + t * P:k * T + (t + 1) * P],
                                            x_nat[:, t, (2 * c + k) * P:(2 * c + k + 1) * P], ident)
                last.then_inc(ht_ready, 1)

            def prepare_rows():
                pe.wait_ge(consts_in, 16 * N_CONST)
                for i in range(2):
                    pe.transpose(bx[:, i * CMP_L:(i + 1) * CMP_L], pos_rows[:, i * P:(i + 1) * P],
                                 ident[0:CMP_L, 0:CMP_L])
                pe.transpose(bx[:, 192:192 + KT_IN // 2], gain_m_rows[:, :],
                             ident[0:KT_IN // 2, 0:KT_IN // 2])
                for c in range(16):
                    last = pe.transpose(bx[:, 128 + 4 * c:132 + 4 * c],
                                        conv_rows[:, c * P:(c + 1) * P], ident[0:4, 0:4])
                last.then_inc(pre_pe, 1)
                pe.matmul(by[0:HEADS_A, 0:TOE], rb[:, :], hot_down, start=True,
                          stop=True).then_inc(pre_pe, 1)

            def prepare_bias(t):
                pe.wait_ge(rb_lo_done, 1)
                for n in range(N_CMP):
                    start = 255 + t * P - (CMP_S * n + CMP_L - 1)
                    last = pe.matmul((bz, bv)[t][:, 2 * n * HEADS_A:2 * (n + 1) * HEADS_A],
                                     hot_r[:, start:start + P], rb_split[:, :],
                                     start=True, stop=True)
                last.then_inc(pre_pe, 1)

            pe.wait_ge(first_in, 32)
            pe.transpose(bx[:, 0:KT_IN], gain_rows[:, :], ident[0:KT_IN, 0:KT_IN]
                         ).then_inc(pre_pe, 1)
            x_t(0)
            x_t(1)
            pe.wait_ge(pre_act, 1)
            for c in range(PAIRS):
                pe.wait_ge(ht_lo, c + 1)
                pair(0, c, 0)
                if c + 2 < PAIRS:
                    x_t(c + 2)
                if c == 6:
                    prepare_rows()
                if c in (8, 9):
                    prepare_bias(c - 8)
            pe.wait_ge(pre_dve, 2)
            pe.wait_ge(pre_act, 2)
            stream(1, 1, {1: [lambda: transpose_stage(T_CK, 0)]})

            def small_pair(q, i):
                for t in range(TT):
                    for k in range(SMALL_K):
                        kk = i * SMALL_K + k
                        col = (q % RING) * 2 * BW + k * N_SMALL
                        toks = slice(t * P, (t + 1) * P)
                        yield two_products((by, bz)[t][:, :], N_SMALL,
                                           (lhs_hi[:, kk, toks], lhs_lo[:, kk, toks]),
                                           w_split[:, :, col:col + N_SMALL],
                                           kk == 0, kk == KT_IN - 1)

            def compressor_pair(q, j, i):
                for m in range(CMP_PL):
                    at_ = i * CMP_PL + m
                    cols = slice((q % RING) * 2 * BW, (q % RING + 1) * 2 * BW)
                    yield passes((bx, bv)[j][0:ROWS, 0:2 * P].rearrange("p (h e) -> p h e", h=2),
                                 [part[:, at_:at_ + (ROWS - 1) * CMP_S + 1:CMP_S]
                                  for part in cin[j]],
                                 [w[:, cols].rearrange("p (h c) -> p h c", h=2)[
                                     :, :, m * P:(m + 1) * P] for w in (w_hi, w_lo)],
                                 at_ == 0, at_ == CMP_S - 1)

            transpose_stage(T_CV, 1)
            def narrow_products(q, i):
                if i == SMALL_PAIRS:
                    pe.wait_ge(tr_lo, T_CV + 1)
                    pe.wait_ge(pre_dve, 4)
                pe.wait_ge(lo_done, q + 1)
                return (small_pair(q, i) if i < SMALL_PAIRS
                        else compressor_pair(q, *divmod(i - SMALL_PAIRS, CMP_PAIRS)))

            steps = mixed_block()
            for n, (q, i, c) in enumerate(steps):
                if i is not None:
                    if i >= SMALL_PAIRS:
                        narrow = narrow_products(q, i)
                    continue
                if c < 2 * SMALL_PAIRS and c % 2 == 0:
                    narrow = narrow_products(*steps[n + 1][:2])
                total = TT * SMALL_K if c < 2 * SMALL_PAIRS else CMP_PL
                share = total // (2 if c < 2 * SMALL_PAIRS else 1) // (2 * TT)
                closes = c >= 2 * SMALL_PAIRS or c % 2 == 1
                pe.wait_ge(lo_done, q + 1)
                for t in range(TT):
                    if c == 0:
                        pe.wait_ge((acc0_free, acc1_free)[t], MIXED - 1)
                    for k in range(2):
                        for _ in range(share):
                            last = next(narrow)
                        if closes and (t, k) == (TT - 1, 1):
                            last.then_inc(pe_used, 1)
                        last = wide(MIXED % 2, t, 2 * c + k, q % RING, k)
                    if c == PAIRS - 1 and t == 0:
                        last.then_inc(acc0_full, 1)
                last.then_inc(pe_used, 1)
            extra = EXTRA

            def hidden_t():
                pe.wait_ge(pre_dve, 6)
                for i in range(4):
                    last = pe.transpose(by[:, i * ROWS:(i + 1) * ROWS],
                                        hid_n[:, i * P:(i + 1) * P], ident[0:ROWS, 0:ROWS])
                last.then_inc(pre_pe, 1)

            def compressed():
                pe.wait_ge(pre_pool, 2)
                pe.wait_ge(tr_lo, T_SK + 1)
                pe.matmul(by[:, 0:GROUPS * NP16], w2[:, 0:P], hid[:, 0:GROUPS * NP16],
                          start=True, stop=True)
                for g in range(GROUPS):
                    last = pe.matmul(bz[0:N_CMP, g * P:(g + 1) * P],
                                     hid[:, 64 + g * NP16:64 + g * NP16 + N_CMP], w2[:, P:2 * P],
                                     start=True, stop=True)
                last.then_inc(pre_pe, 1)

            def running_sum():
                pe.wait_ge(pre_dve, 9)
                pe.matmul(bx[:, 0:4], tri, log_f[:, 0, :], start=True, stop=True)
                pe.matmul(bx[:, 4:8], ones[:, :], log_f[:, 0, :], start=True, stop=False)
                pe.matmul(bx[:, 4:8], tri, log_f[:, 1, :], start=False,
                          stop=True).then_inc(pre_pe, 1)

            def a_rows():
                pe.wait_ge(pre_dve, 10)
                for t in range(TT):
                    last = pe.transpose(bx[0:4, 128 + t * P:128 + (t + 1) * P], a_col[:, t, :],
                                        ident)
                last.then_inc(pre_pe, 1)

            def m_columns():
                pe.wait_ge(pre_dve, 11)
                for t in range(TT):
                    last = pe.transpose(bx[:, 8 + 4 * t:12 + 4 * t], m_row[:, t * P:(t + 1) * P],
                                        ident[0:4, 0:4])
                last.then_inc(pre_pe, 1)

            def key_block():
                pe.wait_ge(pre_dve, 5)
                transpose_stage(T_SK, 2)

            def window_key_block():
                pe.wait_ge(pre_dve, 12)
                transpose_stage(T_WK, 4)

            stream(3, 1, {1: [key_block], 2: [hidden_t], 7: [compressed, running_sum],
                          10: [a_rows], 13: [m_columns]})
            stream(4, 0)
            stream(5, 1, {1: [window_key_block]})
            stream(B_Q0, 0)

            def group_pieces(g):
                def logits(u):
                    hh, t = divmod(u, TT)
                    n = P * (t + 1)
                    q = [m[:, hh, t * P:(t + 1) * P] for m in (q_hi, q_lo)]
                    if u == 0:
                        pe.wait_ge(tr_lo, g + (T_AQ + 1))
                    else:
                        pe.wait_ge(l_done, g * UNITS + u)
                    keys = [m.rearrange("p j g t -> p j (g t)")[:, :, bass.ds(g * T, n)]
                            for m in (k_hi, k_lo)]
                    passes(halves(bx)[:, :, 0:n], q, keys, True, True)
                    two_products(by[:, :], NP16, q, kc_split[:, :, bass.ds(g * NP16, NP16)],
                                 True, True).then_inc(s_ready, 1)

                def weights_t(u):
                    t = u % TT
                    lg = lgs[u % 2]
                    pe.wait_ge(p_done, g * UNITS + u + 1)
                    for b in range(2):
                        for s in range(t + 1):
                            pe.transpose(bz[:, (2 * b + s) * P:(2 * b + s + 1) * P],
                                         halves(lg)[:, b, s * P:(s + 1) * P], ident)
                    if u:
                        pe.wait_ge(o_done, g * UNITS + u)
                    pe.transpose(bv[0:N_CMP, 2 * P:3 * P], lg[:, 512:512 + N_CMP],
                                 ident).then_inc(pt_ready, 1)

                def values(u):
                    t = u % TT
                    pe.wait_ge(pt_lo_done, g * UNITS + u + 1)
                    for b in range(2):
                        for s in range(t + 1):
                            cols = slice((2 * b + s) * P, (2 * b + s + 1) * P)
                            two_products(bv[:, :], P, (pt_hi[:, cols], pt_lo[:, cols]),
                                         v_split[:, :, b, s, bass.ds(g * P, P)],
                                         b == 0 and s == 0, False)
                    two_products(bv[:, :], P, (pct_hi[0:N_CMP, :], pct_lo[0:N_CMP, :]),
                                 vc_split[0:N_CMP, :, bass.ds(g * P, P)],
                                 False, True).then_inc(o_ready, 1)

                entries = [(1, lambda: transpose_stage(g + T_AQ, 2 * g + B_Q0))]
                for u in range(UNITS):
                    s = UNIT0 + UNIT_STEP * u
                    entries += [(s + 3, lambda u=u: weights_t(u)), (s + 4, lambda u=u: values(u))]
                entries += [(UNIT0 + UNIT_STEP * u, lambda u=u: logits(u)) for u in range(UNITS)]
                return piece_map(*entries)

            def group(g):
                b, pieces = 2 * g + B_NSA, group_pieces(g)
                for n in range(2):
                    stream(b + n, 1 - n, {s - n * PAIRS: f for s, f in pieces.items()
                                          if n * PAIRS <= s < (n + 1) * PAIRS})

            with pe.Fori(0, GROUPS - 1) as g:
                group(g)
            group(GROUPS - 1)

            def spread_m():
                pe.wait_ge(m_spread, 1)
                for i in range(HEADS_M * TT):
                    last = pe.matmul((by, bz)[i // 4][:, (i % 4) * P:(i % 4 + 1) * P],
                                     m_wide[:, i, :], ident, start=True, stop=True)
                last.then_inc(nm_ready, 1)

            def head_pieces(h):
                def scores():
                    pe.wait_ge(qk_lo_done, h + 1)
                    for s in range(TT):
                        o0 = 2 * P * s
                        for d in range(2):
                            last = passes(bx[:, o0:o0 + T - s * P],
                                          [m[:, 2 + d, s * P:(s + 1) * P] for m in (qk_hi, qk_lo)],
                                          [m[:, d, s * P:T] for m in (qk_hi, qk_lo)],
                                          d == 0, d == 1)
                    last.then_inc(st_ready, 1)

                def numerator():
                    pe.wait_ge(sw_lo_done, h + 1)
                    pe.wait_ge(v_split_lo, h + 3)
                    parts = ((0, 0, 0), (1, 0, 1), (1, 1, 2))
                    for t, s, i in parts:
                        cols = slice(i * P, (i + 1) * P)
                        passes((by, bz)[t][:, :], (sw_hi[:, cols], sw_lo[:, cols]),
                               (mv_hi[:, s, :], mv_lo[:, s, :]), s == 0, s == t)
                    for t, s, i in parts:
                        for m in (sw_hi, sw_lo):
                            last = pe.matmul(bv[:, 2 * t:2 * t + 2], m[:, i * P:(i + 1) * P],
                                             ones_r[:, :], start=(s == 0 and m is sw_hi),
                                             stop=(s == t and m is sw_lo))
                    last.then_inc(num_ready, 1)

                return {0: {1: [lambda: transpose_stage(h + T_MQK, 4 * h + B_MLSTM - 1)],
                            },
                        1: {0: [scores], 3: [numerator]}}

            def head(h, blocks, last={}):
                pieces = head_pieces(h)
                pieces[2] = last
                for n in range(blocks):
                    stream(4 * h + B_MLSTM + n, 1 - n % 2, pieces.get(n))

            def mix_t(c):
                if c == 0:
                    pe.wait_ge(hm_done, HEADS_M)
                if c < PAIRS // 2:
                    src, col = mix_a, c * 2 * P
                    pe.wait_ge(az_free, GROUPS + 1)
                else:
                    src, col = mix_m, (c - PAIRS // 2) * 2 * P
                    pe.wait_ge(ym_done, (c - PAIRS // 2) // 2 + 1)
                if c >= 2:
                    pe.wait_ge(ht_lo, PAIRS + c - 1)
                for k in range(2):
                    for t in range(TT):
                        last = pe.transpose((by, bz)[c % 2][:, k * T + t * P:k * T + (t + 1) * P],
                                            src[:, t, col + k * P:col + (k + 1) * P], ident)
                last.then_inc(ht_ready, 1)

            spread_m()
            with pe.Fori(0, HEADS_M - 1) as h:
                head(h, 4)
            head(HEADS_M - 1, 3, {c + 2: [lambda c=c: mix_t(c)] for c in range(MIX_EARLY)})

            for c in range(PAIRS):
                if MIX_LATE <= c < MIX_LATE + PAIRS - MIX_EARLY:
                    mix_t(MIX_EARLY + c - MIX_LATE)
                pe.wait_ge(ht_lo, PAIRS + c + 1)
                pair(B_OUT, c, 0, ((acc0_free, B_OUT - 1), (acc1_free, B_OUT - 1)))
            for c in range(PAIRS):
                pair(B_OUT + 1, c, 1, ((acc0_free, B_OUT), (acc1_free, B_OUT)))

            def out_pairs(n, parity, pairs):
                for c in pairs:
                    pair(n + B_OUT, c, parity, ((out0_free, n - 1), (out1_free, n - 1)))

            with pe.Fori(1, 3) as i:
                for n in range(2):
                    out_pairs(2 * i + n, n, range(PAIRS))
            out_pairs(N_OUT - 2, 0, range(PAIRS))
            out_pairs(N_OUT - 1, 1, range(PAIRS - RING))
            for t in range(TT):
                for c in range(PAIRS - RING, PAIRS):
                    if t == 0:
                        pe.wait_ge(lo_done, (N_OUT - 1 + B_OUT) * PAIRS + (c + extra + 1))
                    for k in range(2):
                        last = wide(1, t, 2 * c + k, c % RING, k)
                    if t == 1:
                        last.then_inc(pe_used, 1)
                if t == 0:
                    last.then_inc(acc0_full, 1)

        @block.scalar
        def _(act):
            chain = Count()
            extra = 0

            def link(ins):
                chain.n += 1
                ins.then_inc(act_chain, 1)
                act.wait_ge(act_chain, chain.value())

            def split(q, s, turn):
                if not isinstance(q, int) or q >= RING:
                    act.wait_ge(pe_used, q - RING + 1)
                act.wait_ge(w_loaded[s], turn)
                cols = slice(s * 2 * BW, (s + 1) * 2 * BW)
                act.activation(w_hi[:, cols], w_raw[:, cols], ACT.Copy).then_inc(hi_done, 1)

            def slot(b, c):
                n = c + LOOKAHEAD + extra
                split(b * PAIRS + n, n % RING,
                      b * (PAIRS // RING * LOADED) + LOADED * (n // RING + 1))

            def take(b, parity, dst):
                act.wait_ge(acc0_full, b + 1)
                act.activation(dst, acc[parity][0][:, :], ACT.Copy,
                               scale=rstd[:, 0:1]).then_inc(acc0_free, 1)

            def stream(b, pieces=None, first=False):
                for c in range(PAIRS):
                    if not first:
                        slot(b, c)
                    for piece in (pieces or {}).get(c, ()):
                        piece()
                    if first:
                        slot(b, c)

            def tiles(t):
                return t.rearrange("p (g t) -> p g t", t=T)

            def transposed(event, dst):
                act.wait_ge(tr_done, event + 1)
                act.activation(dst(0), tiles(bv[:, :]), ACT.Copy)
                act.activation(dst(1), tiles(bx[:, :]), ACT.Copy).then_inc(tr_hi, 1)

            def staged_values(b, dst):
                act.wait_ge(acc1_free, b + 1)
                act.wait_ge(acc0_free, b + 1)
                act.activation(dst, stage[:, :, :], ACT.Copy).then_inc(v_split_hi, 1)

            act.dma_start(c128[:, :], const128).then_inc(first_in, 16)
            act.dma_start(gain_rows[:, :], norm_gain.rearrange("(k p) -> k p", p=P)
                          ).then_inc(first_in, 16)

            def x_hi(c, gain=gain_t, banks=acc[1]):
                act.wait_ge(ht_ready, c + 1)
                if c >= PAIRS:
                    act.wait_ge(pe_used, (B_OUT - 1) * PAIRS + (EXTRA + 1) + c - PAIRS)
                for k in range(2):
                    kk = (2 * c + k) % KT_IN
                    last = act.activation(lhs_hi[:, kk, :], banks[c % 2][:, k * T:(k + 1) * T],
                                          ACT.Copy, scale=gain[:, kk:kk + 1])
                last.then_inc(ht_hi, 1)

            act.wait_ge(pre_pe, 1)
            link(act.activation(gain_t[:, :], bx[:, 0:KT_IN], ACT.Copy))
            act.activation(spare[:, 0:1], gain_t[:, 0:1], ACT.Copy).then_inc(pre_act, 1)
            split(0, 0, LOADED)
            x_hi(0)
            x_hi(1)
            split(1, 1, LOADED)
            split(2, 2, LOADED)
            for c in range(PAIRS):
                if c + 2 < PAIRS:
                    x_hi(c + 2)
                slot(0, c)
                if c == 6:
                    act.wait_ge(consts_in, 16 * N_CONST)
                    act.activation(hot_r[:, :], hot_up, ACT.Copy)
                    act.activation(rb_split[:, 0:HEADS_A], rb[:, :], ACT.Copy
                                   ).then_inc(rb_hi_done, 1)
                if c == 8:
                    act.wait_ge(pre_pe, 2)
                    act.activation(gain_mix[:, KT_IN // 2:KT_IN], bx[:, 192:192 + KT_IN // 2],
                                   ACT.Copy)
                    act.activation(pos_t[:, :], bx[:, 0:2 * CMP_L], ACT.Copy)
                    act.activation(conv_w[:, :], bx[:, 128:192], ACT.Copy).then_inc(pre_act, 1)
                if c % 2 == 1:
                    t, i = divmod(c // 2, 4)
                    act.wait_ge(x_in[2 * i], 16)
                    act.wait_ge(x_in[2 * i + 1], 16)
                    link(act.activation(junk[:, :], x_nat[:, t, i * 1024:(i + 1) * 1024],
                                        ACT.Square, accum_out=ss8[:, t, i:i + 1]))
            act.activation(spare[:, 1:2], gain_t[:, 0:1], ACT.Copy).then_inc(pre_act, 1)
            act.wait_ge(pre_pool, 1)
            take(0, 0, stage[:, 0, :])

            def copies_out(i):
                act.wait_ge(pre_dve, 1)
                act.dma_start(toe_dram.ap()[:, i * 32:(i + 1) * 32], toe_row[:, :].unsqueeze(1)
                              .broadcast_to([HEADS_A, 32, TOE])).then_inc(toe_out, 16)

            def first_bias():
                act.wait_ge(toe_out, 4 * 16)
                act.dma_start(toe[:, :].rearrange("p (h s) -> p h s", s=T), toe_rows[:, 0:HPG, :]
                              ).then_inc(toe_in, 16)

            toe_rows = bass.AP(toe_dram, P - 1, [[TOE - 1, P], [P * TOE, HEADS_A], [1, T]])

            def positions_hi():
                act.activation(cin[0][0][:, GROUPS * T:], pos_t[:, 0:CMP_L], ACT.Copy)
                act.activation(cin[1][0][:, GROUPS * T:], pos_t[:, CMP_L:2 * CMP_L], ACT.Copy
                               ).then_inc(pre_act, 1)

            stream(1, {2: [lambda: transposed(T_CK, lambda i: by_group(cin[0][0])[:, 2 * i:2 * i + 2, :])],
                       3: [lambda: copies_out(0)], 5: [positions_hi], 6: [lambda: copies_out(1)],
                       9: [lambda: copies_out(2)], 12: [lambda: copies_out(3)],
                       15: [first_bias]})
            act.wait_ge(tr_done, T_CK + 1)
            take(1, 1, stage[:, 0, :])

            def small_exponentials():
                act.wait_ge(pre_dve, 6)
                act.activation(g_sig[:, :, :], small[:, :, N_IF:], ACT.Exp, scale=-1.0
                               ).then_inc(pre_act, 1)
                link(act.activation(log_f[:, :, :], f_abs[:, :, :], ACT.Exp, scale=-1.0))
                act.activation(log_f[:, :, :], log_f[:, :, :], ACT.Ln, bias=1.0
                               ).then_inc(pre_act, 1)

            def hidden_exponentials():
                act.wait_ge(pre_dve, 7)
                act.activation(hid_e[:, :], hid[:, :], ACT.Exp, scale=-1.0).then_inc(pre_act, 1)

            def compressed_hi():
                act.wait_ge(pre_pe, 7)
                act.activation(kc_hi[:, :], by[:, 0:GROUPS * NP16], ACT.Copy)
                act.activation(vc_hi[0:N_CMP, :], bz[0:N_CMP, :], ACT.Copy).then_inc(pre_act, 1)

            def e_neg_m_exp():
                act.wait_ge(pre_dve, 12)
                act.activation(e_neg_m[:, :, :], e_neg_m[:, :, :], ACT.Exp, scale=-1.0
                               ).then_inc(pre_act, 1)

            for j, (q, _, _) in enumerate(mixed_block()):
                q += LOOKAHEAD
                split(q, q % RING, LOADED * (q // RING + 1))
                if j == 1:
                    transposed(T_CV, lambda i: by_group(cin[1][0])[:, 2 * i:2 * i + 2, :])
            extra = EXTRA
            act.wait_ge(tr_done, T_CV + 1)
            take(2, 0, stage[:, 0, :])
            stream(3, {2: [lambda: transposed(T_SK, lambda i: k_hi[:, 0, 2 * i:2 * i + 2, :])],
                       1: [small_exponentials], 4: [hidden_exponentials], 8: [compressed_hi],
                       15: [e_neg_m_exp]})
            act.wait_ge(tr_done, T_SK + 1)
            take(3, 1, stage[:, 0, :])
            stream(4, {1: [lambda: staged_values(3, v_hi[:, 0])]})
            act.wait_ge(v_split_lo, 1)
            take(4, 0, stage[:, 0, :])
            stream(5, {2: [lambda: transposed(T_WK, lambda i: k_hi[:, 1, 2 * i:2 * i + 2, :])]})
            act.wait_ge(tr_done, T_WK + 1)
            take(5, 1, stage[:, 0, :])
            stream(B_Q0, {1: [lambda: staged_values(5, v_hi[:, 1])]})
            act.wait_ge(v_split_lo, 2)
            take(B_Q0, 0, stage[:, 0, :])

            def group_pieces(g, last):
                def exponentials(u):
                    n = P * (u % TT + 1)
                    lg = lgs[u % 2]
                    act.wait_ge(l_done, g * UNITS + u + 1)
                    for b in range(2):
                        act.activation(halves(lg)[:, b, 0:n], halves(lg)[:, b, 0:n], ACT.Exp,
                                       bias=nmax[:, 1 + b:2 + b], accum_out=rsum[:, 1 + b:2 + b])
                    act.activation(lg[:, 512:512 + N_CMP], lg[:, 512:512 + N_CMP], ACT.Exp,
                                   bias=nmax[:, 0:1], accum_out=rsum[:, 0:1]).then_inc(e_done, 1)

                def weights_hi(u):
                    n = P * (u % TT + 1)
                    act.wait_ge(pt_ready, g * UNITS + u + 1)
                    act.activation(halves(pt_hi)[:, :, 0:n], halves(bz)[:, :, 0:n], ACT.Copy)
                    act.activation(pct_hi[0:N_CMP, :], bv[0:N_CMP, 2 * P:3 * P],
                                   ACT.Copy).then_inc(pt_hi_done, 1)

                def take_gate():
                    act.wait_ge(az_free, g + 1)
                    take(2 * g + B_NSA, 1, gate_buf[:, 0, :])

                def gate_exp():
                    act.wait_ge(acc1_free, 2 * g + (B_NSA + 1))
                    act.wait_ge(acc0_free, 2 * g + (B_NSA + 1))
                    act.activation(ebuf[:, :, :], gate_buf[:, :, :], ACT.Exp, scale=-1.0
                                   ).then_inc(az_e, 1)

                def next_bias():
                    act.wait_ge(l_done, g * UNITS + UNITS)
                    act.dma_start(toe[:, :].rearrange("p (h s) -> p h s", s=T),
                                  toe_rows[:, bass.ds(g * HPG + HPG, HPG), :]).then_inc(toe_in, 16)

                entries = [(2, lambda: transposed(g + T_AQ, lambda i: q_hi[:, 2 * i:2 * i + 2, :])),
                           (16, take_gate), (17, gate_exp)]
                for u in range(UNITS):
                    s = UNIT0 + UNIT_STEP * u
                    entries += [(s + 1, lambda u=u: exponentials(u)),
                                (s + 3, lambda u=u: weights_hi(u))]
                if not last:
                    entries.append((28, next_bias))
                return piece_map(*entries)

            def group(g, last=False):
                b, pieces = 2 * g + B_NSA, group_pieces(g, last)
                for n in range(2):
                    stream(b + n, {s - n * PAIRS: f for s, f in pieces.items()
                                   if n * PAIRS <= s < (n + 1) * PAIRS}, first=True)
                act.wait_ge(tr_done, g + (T_AQ + 1))
                take(b + 1, 0, stage[:, 0, :])

            with act.Fori(0, GROUPS - 1) as g:
                group(g)
            group(GROUPS - 1, last=True)

            def head_pieces(h):
                b = 4 * h + B_MLSTM

                def conv_inputs():
                    act.wait_ge(tr_done, h + (T_MQK + 1))
                    act.activation(conv_in[:, 0:2, 3:PADT], tiles(bv[:, :]),
                                   ACT.Copy).then_inc(tr_hi, 1)

                def conv_exp():
                    act.wait_ge(conv_done, h + 1)
                    act.wait_ge(az_free, GROUPS + 1)
                    act.activation(qk_sig, qk[:, :, :], ACT.Exp, scale=-1.0).then_inc(conv_e, 1)

                def decay():
                    act.wait_ge(nm_done, 1)
                    for i, (s, src) in enumerate(((0, neg_m_diag), (0, neg_m), (1, neg_m_diag))):
                        t = (0, 1, 1)[i]
                        last = act.activation(
                            wexp[:, i * P:(i + 1) * P], flat(src)[:, bass.ds(h * T + t * P, P)],
                            ACT.Exp, bias=flat(a_col)[:, bass.ds(h + s * HEADS_M, 1)])
                    last.then_inc(wexp_done, 1)

                def qk_hi_part():
                    act.wait_ge(qk_done, h + 1)
                    act.activation(qk_hi[:, :, :], qk[:, :, :], ACT.Copy).then_inc(qk_hi_done, 1)

                def sw_hi_part():
                    act.wait_ge(sw_done, h + 1)
                    act.activation(sw_hi[:, :], sw[:, :], ACT.Copy).then_inc(sw_hi_done, 1)

                def output_gate():
                    act.wait_ge(acc1_free, b + 2)
                    act.wait_ge(acc0_free, b + 2)
                    act.activation(ebuf[:, :, :], stage[:, :, :], ACT.Exp, scale=-1.0
                                   ).then_inc(mo_e, 1)

                def squares():
                    act.wait_ge(ho_done, h + 1)
                    for t in range(TT):
                        last = act.activation(ebuf[:, t, :], hm[:, t, :], ACT.Square,
                                              accum_out=ssm[:, t:t + 1])
                    last.then_inc(ssm_done, 1)

                return {0: piece_map((2, conv_inputs), (7, conv_exp), (9, decay),
                                     (13, qk_hi_part)),
                        1: piece_map((1, sw_hi_part),
                                     (1, lambda: staged_values(b, mv_hi[:, :, :]))),
                        2: piece_map((1, output_gate), (7, squares))}

            def silu_gate(h):
                act.wait_ge(hr_done, h + 1)
                act.wait_ge(acc1_free, 4 * h + (B_MLSTM + 3))
                act.wait_ge(acc0_free, 4 * h + (B_MLSTM + 3))
                act.activation(ebuf[:, :, :], stage[:, :, :], ACT.Exp, scale=-1.0
                               ).then_inc(mz_e, 1)

            def head(h, blocks, last={}):
                b, pieces = 4 * h + B_MLSTM, head_pieces(h)
                pieces[3] = {1: [lambda: silu_gate(h)]}
                for c, late in last.items():
                    pieces[2].setdefault(c, []).extend(late)
                stage_free = ((tr_done, h + (T_MQK + 1)), (v_split_lo, h + 3), None,
                              (mz_done, h + 1))
                for n in range(blocks):
                    stream(b + n, pieces.get(n))
                    if stage_free[n] is not None:
                        act.wait_ge(*stage_free[n])
                    take(b + n, 1 - n % 2, stage[:, 0, :])

            def mix_hi(c):
                x_hi(PAIRS + c, gain_mix, (by, bz))

            with act.Fori(0, HEADS_M - 1) as h:
                head(h, 4)
            head(HEADS_M - 1, 3, {c + 2: [lambda c=c: mix_hi(c)] for c in range(MIX_EARLY)})

            x_cols = x[0].rearrange("(a p) d -> p a d", p=P)

            def fetch_residual(n, i):
                act.dma_start(xres[:, i], x_cols[:, :, bass.ds(n * BW, BW)]).then_inc(xr_in[i], 16)

            def square(t, n):
                return act.activation(ebuf[:, t, :], res[:, t, bass.ds(n * BW, BW)], ACT.Square,
                                      accum_out=ssf[:, t, bass.ds(n, 1)])

            def squares(n):
                act.wait_ge(out1_free, n + 1)
                for t in range(TT):
                    last = square(t, n)
                last.then_inc(sq_done, 1)

            for c in range(PAIRS):
                if MIX_LATE <= c < MIX_LATE + PAIRS - MIX_EARLY:
                    mix_hi(MIX_EARLY + c - MIX_LATE)
                slot(B_OUT, c)
                if c == 1:
                    silu_gate(HEADS_M - 1)
                if c == 9:
                    act.wait_ge(ym_done, HEADS_M)
                    fetch_residual(0, 0)
                    fetch_residual(1, 1)
                    act.dma_start(gain_f[:, :], final_norm_gain.rearrange("(o n) -> o n", o=1)
                                  .broadcast_to([P, D])).then_inc(gf_in, 16)

            def out_block(n, i, last=False):
                for c in range(PAIRS - LOOKAHEAD if last else PAIRS):
                    slot(n + B_OUT, c)
                    if c == 2:
                        squares(n - 1)
                    if c == 4 and not last:
                        fetch_residual(n + 1, i)

            out_block(1, 0)
            with act.Fori(1, 3) as i:
                out_block(2 * i, 1)
                out_block(2 * i + 1, 0)
            out_block(6, 1)
            out_block(7, 0, last=True)
            act.wait_ge(out0_free, N_OUT)
            square(0, N_OUT - 1).then_inc(sq_last, 1)
            act.wait_ge(gained, N_OUT - 1)
            act.wait_ge(fr_done, 1)
            for i in range(4):
                cols = slice(i * Y_COLS, min((i + 1) * Y_COLS, LAST))
                act.activation(res[:, 0, cols], res[:, 0, cols], ACT.Copy,
                               scale=fr[:, 0:1]).then_inc(y0_done, 1)
            act.wait_ge(out1_free, N_OUT)
            square(1, N_OUT - 1).then_inc(sq_last, 1)

        @block.vector
        def _(dve):
            chain = Count()
            extra = 0

            def link(ins):
                chain.n += 1
                ins.then_inc(dve_chain, 1)
                dve.wait_ge(dve_chain, chain.value())

            def lo(q, s):
                dve.wait_ge(hi_done, q + 1)
                cols = slice(s * 2 * BW, (s + 1) * 2 * BW)
                dve.tensor_tensor(w_lo[:, cols], w_raw[:, cols], w_hi[:, cols].bitcast(F32),
                                  ALU.subtract).then_inc(lo_done, 1)

            def slot(b, c):
                n = c + LOOKAHEAD + extra
                lo(b * PAIRS + n, n % RING)

            def take(b, parity, dst):
                dve.wait_ge(pe_used, b * PAIRS + (PAIRS + extra))
                dve.tensor_scalar(dst, acc[parity][1][:, :], rstd[:, 1:2], None,
                                  ALU.mult).then_inc(acc1_free, 1)

            def stream(b, pieces=None, first=False):
                for c in range(PAIRS):
                    if not first:
                        slot(b, c)
                    for piece in (pieces or {}).get(c, ()):
                        piece()
                    if first:
                        slot(b, c)

            def tiles(t):
                return t.rearrange("p (g t) -> p g t", t=T)

            def transposed(event, hi, dst):
                dve.wait_ge(tr_hi, event + 1)
                for i, bk in enumerate((bv, bx)):
                    last = dve.tensor_tensor(dst(i), tiles(bk[:, :]), hi(i).bitcast(F32),
                                             ALU.subtract)
                last.then_inc(tr_lo, 1)

            def two(m, lead):
                return (lambda i: lead(m[0])[:, 2 * i:2 * i + 2, 0:T],
                        lambda i: lead(m[1])[:, 2 * i:2 * i + 2, 0:T])

            def staged_values(event, hi, dst):
                dve.wait_ge(v_split_hi, event + 1)
                dve.tensor_tensor(dst, stage[:, :, :], hi.bitcast(F32), ALU.subtract
                                  ).then_inc(v_split_lo, 1)

            def sigmoid(ready, buf, done, slots):
                flat_buf = flat(buf)

                def piece(i):
                    if i == 0:
                        dve.wait_ge(*ready)
                        link(dve.tensor_scalar(flat_buf, flat_buf, 1.0, None, ALU.add))
                    part = flat_buf[:, i * 256:(i + 1) * 256]
                    last = dve.reciprocal(part, part)
                    if i == 3:
                        last.then_inc(done, 1)
                return [(n, lambda i=i: piece(i)) for i, n in enumerate(slots)]

            dve.memset(m_half[:, :], -0.5)
            dve.memset(gain_mix[:, 0:KT_IN // 2], 1.0)
            dve.memset(eps_m[:, :], V_M * EPS)
            dve.memset(inv_m[:, :], 1.0 / V_M)
            dve.memset(ones_r[:, :].bitcast(F32), 1.0)
            dve.memset(ones[:, :], 1.0)

            def x_lo(c, gain=gain_t, banks=acc[1]):
                dve.wait_ge(ht_hi, c + 1)
                for k in range(2):
                    kk = (2 * c + k) % KT_IN
                    last = dve.scalar_tensor_tensor(
                        lhs_lo[:, kk, :], banks[c % 2][:, k * T:(k + 1) * T],
                        gain[:, kk:kk + 1], lhs_hi[:, kk, :].bitcast(F32), ALU.mult, ALU.subtract)
                last.then_inc(ht_lo, 1)

            lo(0, 0)
            x_lo(0)
            x_lo(1)
            lo(1, 1)
            lo(2, 2)
            for c in range(PAIRS):
                if c + 2 < PAIRS:
                    x_lo(c + 2)
                slot(0, c)
                if c == 7:
                    dve.wait_ge(rb_hi_done, 1)
                    dve.tensor_tensor(rb_split[:, HEADS_A:], rb[:, :],
                                      rb_split[:, 0:HEADS_A].bitcast(F32), ALU.subtract
                                      ).then_inc(rb_lo_done, 1)
                if c == 8:
                    dve.wait_ge(pre_pe, 3)
                    dve.tensor_tensor(toe_row[:, :], by[0:HEADS_A, 0:TOE], toe_mask[:, :], ALU.add
                                      ).then_inc(pre_dve, 1)
                if c == 10:
                    dve.wait_ge(pre_pe, 5)
                    parts = [bk[:, 0:N_CMP * 2 * HEADS_A].rearrange(
                        "p (n s h) -> p n s h", s=2, h=HEADS_A) for bk in (bz, bv)]
                    for t in range(TT):
                        last = dve.tensor_tensor(
                            bias_c[:, t], parts[t][:, :, 0],
                            cmp_neg[:, t, :].unsqueeze(2).broadcast_to([P, N_CMP, HEADS_A]),
                            ALU.add)
                    link(last)
                    for t in range(TT):
                        last = dve.tensor_tensor(bias_c[:, t], bias_c[:, t], parts[t][:, :, 1],
                                                 ALU.add)
                    last.then_inc(pre_dve, 1)
            dve.wait_ge(pre_act, 3)
            dve.tensor_reduce(ss[:, :], ss8[:, :, :], AX, ALU.add).then_inc(pre_dve, 1)
            dve.wait_ge(pre_pool, 1)
            take(0, 0, stage[:, 1, :])

            def positions_lo():
                dve.wait_ge(pre_act, 4)
                for j in range(2):
                    last = dve.tensor_tensor(cin[j][1][:, GROUPS * T:],
                                             pos_t[:, j * CMP_L:(j + 1) * CMP_L],
                                             cin[j][0][:, GROUPS * T:].bitcast(F32), ALU.subtract)
                last.then_inc(pre_dve, 1)

            stream(1, {2: [lambda: transposed(T_CK, *two(cin[0], by_group))],
                       6: [positions_lo]})
            dve.wait_ge(tr_done, T_CK + 1)
            take(1, 1, stage[:, 1, :])

            def small_columns():
                dve.wait_ge(pe_used, (MIXED + 1) * PAIRS + EXTRA)
                for j, bk in enumerate((bx, bv)):
                    last = dve.tensor_copy(hid_n[:, j * 2 * P:(j + 1) * 2 * P],
                                           bk[0:ROWS, 0:2 * P])
                last.then_inc(pre_dve, 1)
                for t in range(TT):
                    last = dve.tensor_scalar(small[:, t, :], (by, bz)[t][:, 0:N_SMALL],
                                             rstd[:, t:t + 1], None, ALU.mult)
                link(last)
                for t in range(TT):
                    last = dve.scalar_tensor_tensor(
                        small[:, t, :], (by, bz)[t][:, N_SMALL:2 * N_SMALL], rstd[:, t:t + 1],
                        small[:, t, :], ALU.mult, ALU.add)
                link(last)
                for t in range(TT):
                    last = dve.tensor_tensor(small[:, t, 0:N_IF], small[:, t, 0:N_IF], b_if[:, :],
                                             ALU.add)
                link(last)
                dve.scalar_tensor_tensor(f_abs[:, :, :], small[:, :, HEADS_M:N_IF], -1.0,
                                         small[:, :, HEADS_M:N_IF], ALU.mult, ALU.max
                                         ).then_inc(pre_dve, 1)

            def hidden():
                dve.wait_ge(pre_pe, 6)
                parts = by[:, 0:4 * ROWS].rearrange("p (j h r) -> p j h r", j=2, h=2)
                windows = hid[:, :].rearrange("p (j g n) -> p j g n", j=2, g=GROUPS)

                def chunks(j, h):
                    return parts[:, j, h, 0:ROWS - 2].rearrange("p (g n) -> p g n", g=GROUPS)

                dve.tensor_copy(hid_b[:, :], parts[:, :, 0, ROWS - 2])
                for j in range(2):
                    last = dve.tensor_copy(windows[:, j], chunks(j, 0))
                link(last)
                dve.tensor_tensor(hid_b[:, :], hid_b[:, :], parts[:, :, 1, ROWS - 1], ALU.add)
                for j in range(2):
                    last = dve.tensor_tensor(windows[:, j, :, 0:N_CMP], windows[:, j, :, 0:N_CMP],
                                             chunks(j, 1)[:, :, 1:CHUNKS], ALU.add)
                link(last)
                for j in range(2):
                    last = dve.tensor_scalar(hid[:, j * 64:(j + 1) * 64],
                                             hid[:, j * 64:(j + 1) * 64], hid_b[:, j:j + 1], None,
                                             ALU.add)
                last.then_inc(pre_dve, 1)

            def sigmoids():
                dve.wait_ge(pre_act, 7)
                link(dve.tensor_scalar(hid_e[:, :], hid_e[:, :], 1.0, None, ALU.add))
                dve.reciprocal(hid_e[:, :], hid_e[:, :]).then_inc(pre_dve, 1)
                dve.scalar_tensor_tensor(log_f[:, :, :], small[:, :, HEADS_M:N_IF], 0.0,
                                         log_f[:, :, :], ALU.min, ALU.subtract
                                         ).then_inc(pre_dve, 1)
                link(dve.tensor_scalar(g_sig[:, :, :], g_sig[:, :, :], 1.0, None, ALU.add))
                link(dve.reciprocal(g_sig[:, :, :], g_sig[:, :, :]))

            def decay_columns():
                dve.wait_ge(pre_pe, 8)
                link(dve.tensor_copy(f_cum[:, :, :], bx[:, 0:8].rearrange("p (a h) -> p a h", a=TT)))
                dve.tensor_tensor(a_col[:, :, :], small[:, :, 0:HEADS_M], f_cum[:, :, :],
                                  ALU.subtract).then_inc(pre_dve, 1)
                dve.wait_ge(pre_act, 8)
                dve.tensor_tensor(kc_lo[:, :], by[:, 0:GROUPS * NP16], kc_hi[:, :].bitcast(F32),
                                  ALU.subtract)
                link(dve.tensor_tensor(vc_lo[0:N_CMP, :], bz[0:N_CMP, :],
                                       vc_hi[0:N_CMP, :].bitcast(F32), ALU.subtract))

            def running_maximum():
                dve.wait_ge(pre_pe, 9)
                link(dve.tensor_copy(a_row[:, :], bx[0:4, 128:128 + T]))
                dve.tensor_tensor_scan(m_row[:, :], a_row[:, :], a_row[:, :], 0.0, ALU.max,
                                       ALU.max).then_inc(pre_dve, 1)

            def stabiliser():
                dve.wait_ge(pre_pe, 10)
                m = bx[:, 8:16].rearrange("p (a h) -> p a h", a=TT)
                dve.tensor_scalar(m_neg.rearrange("p h a -> p a h"), m, -1.0, None, ALU.mult)
                dve.tensor_tensor(e_neg_m[:, :, :], f_cum[:, :, :], m, ALU.add
                                  ).then_inc(pre_dve, 1)

            for j, (q, _, _) in enumerate(mixed_block()):
                q += LOOKAHEAD
                lo(q, q % RING)
                if j == 1:
                    transposed(T_CV, *two(cin[1], by_group))
            extra = EXTRA
            dve.wait_ge(tr_done, T_CV + 1)
            take(2, 0, stage[:, 1, :])
            stream(3, {2: [lambda: transposed(T_SK, *two((k_hi, k_lo), lambda m: m[:, 0]))],
                       0: [small_columns], 3: [hidden], 5: [sigmoids], 8: [decay_columns],
                       11: [running_maximum], 14: [stabiliser]})
            dve.wait_ge(tr_done, T_SK + 1)
            take(3, 1, stage[:, 1, :])
            stream(4, {1: [lambda: staged_values(0, v_hi[:, 0], v_lo[:, 0])]})
            dve.wait_ge(v_split_lo, 1)
            take(4, 0, stage[:, 1, :])
            stream(5, {2: [lambda: transposed(T_WK, *two((k_hi, k_lo), lambda m: m[:, 1]))]})
            dve.wait_ge(tr_done, T_WK + 1)
            take(5, 1, stage[:, 1, :])
            stream(B_Q0, {1: [lambda: staged_values(1, v_hi[:, 1], v_lo[:, 1])]})
            dve.wait_ge(v_split_lo, 2)
            take(B_Q0, 0, stage[:, 1, :])

            def group_pieces(g):
                def logits(u):
                    hh, t = divmod(u, TT)
                    n = P * (t + 1)
                    lg = lgs[u % 2]
                    if u == 0:
                        dve.wait_ge(toe_in, g * 16 + 16)
                    dve.wait_ge(s_ready, g * UNITS + u + 1)
                    lg_c = lg[:, 512:512 + N_CMP]
                    dve.scalar_tensor_tensor(
                        lg_c, by[:, 0:N_CMP], DH ** -0.5,
                        bias_c[:, t, :, bass.ds(g * HPG + hh, 1)].rearrange("p n o -> p (n o)"),
                        ALU.mult, ALU.add)
                    link(dve.scalar_tensor_tensor(
                        halves(lg)[:, :, 0:n], halves(bx)[:, :, 0:n], DH ** -0.5,
                        toe[:, (hh + 1) * T - n:(hh + 1) * T].unsqueeze(1)
                        .broadcast_to([P, 2, n]), ALU.mult, ALU.add))
                    link(dve.scalar_tensor_tensor(lg_c, by[:, NP16:NP16 + N_CMP], DH ** -0.5, lg_c,
                                                  ALU.mult, ALU.add))
                    dve.tensor_reduce(nmax[:, 1:3], halves(lg)[:, :, 0:n], AX, ALU.max, negate=True)
                    dve.tensor_reduce(nmax[:, 0:1], lg[:, 512:512 + N_CMP], AX, ALU.max,
                                      negate=True).then_inc(l_done, 1)

                def outputs(u):
                    hh, t = divmod(u, TT)
                    dve.wait_ge(o_ready, g * UNITS + u + 1)
                    out_ = mix_a[:, t, bass.ds(g * BW + hh * P, P)]
                    link(dve.tensor_copy(out_, bv[:, 0:P]))
                    dve.tensor_tensor(out_, out_, bv[:, P:2 * P], ALU.add).then_inc(o_done, 1)

                def weights(u):
                    hh, t = divmod(u, TT)
                    n = P * (t + 1)
                    lg = lgs[u % 2]
                    dve.wait_ge(e_done, g * UNITS + u + 1)
                    link(dve.reciprocal(coef[:, :], rsum[:, :]))
                    link(dve.tensor_tensor(coef[:, :], coef[:, :], flat(g_sig)[
                        :, bass.ds(3 * (g * HPG + hh) + t * N_GATE, 3)], ALU.mult))
                    for b in range(2):
                        dve.tensor_scalar(halves(lg)[:, b, 0:n], halves(lg)[:, b, 0:n],
                                          coef[:, 1 + b:2 + b], None, ALU.mult)
                    dve.scalar_tensor_tensor(lg[:, 512:512 + N_CMP], lg[:, 512:512 + N_CMP],
                                             coef[:, 0:1], cmp_01[:, t, :], ALU.mult, ALU.mult
                                             ).then_inc(p_done, 1)

                def weights_lo(u):
                    n = P * (u % TT + 1)
                    dve.wait_ge(pt_hi_done, g * UNITS + u + 1)
                    dve.tensor_tensor(halves(pt_lo)[:, :, 0:n], halves(bz)[:, :, 0:n],
                                      halves(pt_hi)[:, :, 0:n].bitcast(F32), ALU.subtract)
                    dve.tensor_tensor(pct_lo[0:N_CMP, :], bv[0:N_CMP, 2 * P:3 * P],
                                      pct_hi[0:N_CMP, :].bitcast(F32), ALU.subtract
                                      ).then_inc(pt_lo_done, 1)

                def take_gate():
                    dve.wait_ge(az_free, g + 1)
                    take(2 * g + B_NSA, 1, gate_buf[:, 1, :])

                entries = [(2, lambda: transposed(g + T_AQ, *two((q_hi, q_lo), lambda m: m))),
                           (16, take_gate)]
                gate = sigmoid((az_e, g + 1), ebuf, az_r, (19, 22, 25, 28))
                for u in range(UNITS):
                    s = UNIT0 + UNIT_STEP * u
                    entries += [(s + 5, lambda u=u: outputs(u)), (s + 2, lambda u=u: weights(u)),
                                (s + 3, lambda u=u: weights_lo(u))]
                entries += [(UNIT0 + UNIT_STEP * u, lambda u=u: logits(u)) for u in range(UNITS)]
                return piece_map(*entries, *gate)

            def group(g):
                b, pieces = 2 * g + B_NSA, group_pieces(g)
                for n in range(2):
                    stream(b + n, {s - n * PAIRS: f for s, f in pieces.items()
                                   if n * PAIRS <= s < (n + 1) * PAIRS}, first=True)
                dve.wait_ge(tr_done, g + (T_AQ + 1))
                take(b + 1, 0, stage[:, 1, :])

            with dve.Fori(0, GROUPS - 1) as g:
                chain.enter(g, GROUP_LINKS)
                group(g)
            chain.leave(GROUPS - 1)
            group(GROUPS - 1)

            dve.tensor_copy(m_wide, flat(m_neg).unsqueeze(2)
                            .broadcast_to([P, HEADS_M * TT, P])).then_inc(m_spread, 1)
            link(dve.memset(conv_in[:, :, 0:3], 0.0))

            def stabilisers():
                dve.wait_ge(nm_ready, 1)
                for i, bk in enumerate((by, bz)):
                    v = tiles(bk[:, :])
                    dve.tensor_copy(neg_m[:, 2 * i:2 * i + 2, :], v)
                    for hh in range(2):
                        last = dve.tensor_tensor(
                            neg_m_diag[:, 2 * i + hh, :].rearrange("p (a t) -> p a t", a=TT),
                            v[:, hh, :].rearrange("p (a t) -> p a t", a=TT),
                            diag_mask.unsqueeze(1).broadcast_to([P, TT, P]), ALU.add)
                last.then_inc(nm_done, 1)

            stabilisers()

            def head_pieces(h):
                b = 4 * h + B_MLSTM

                def conv_inputs():
                    dve.wait_ge(tr_hi, h + (T_MQK + 1))
                    link(dve.tensor_copy(conv_in[:, 2:4, 3:PADT], tiles(bx[:, :])))
                    dve.memset(spare[:, 2:3], 0.0).then_inc(tr_lo, 1)

                def conv(j):
                    for c in range(4):
                        w = conv_w[:, bass.ds(h * 8 + ((c // 2) * 8 + c % 2) * 4 + j, 1)]
                        if j == 0:
                            last = dve.tensor_scalar(qk[:, c, :], conv_in[:, c, 0:T], w, None,
                                                     ALU.mult)
                        else:
                            last = dve.scalar_tensor_tensor(
                                qk[:, c, :], conv_in[:, c, j:j + T], w, qk[:, c, :], ALU.mult,
                                ALU.add)
                    if j < 3:
                        link(last)
                    else:
                        last.then_inc(conv_done, 1)

                def qk_lo_part():
                    dve.wait_ge(qk_hi_done, h + 1)
                    dve.tensor_tensor(qk_lo[:, :, :], qk[:, :, :], qk_hi[:, :, :].bitcast(F32),
                                      ALU.subtract).then_inc(qk_lo_done, 1)

                def scores():
                    dve.wait_ge(st_ready, h + 1)
                    dve.wait_ge(wexp_done, h + 1)
                    dve.scalar_tensor_tensor(sw[:, :], bx[:, 0:384], QK_M ** -0.5, wexp[:, :],
                                             ALU.mult, ALU.mult).then_inc(sw_done, 1)

                def scores_lo():
                    dve.wait_ge(sw_hi_done, h + 1)
                    dve.tensor_tensor(sw_lo[:, :], sw[:, :], sw_hi[:, :].bitcast(F32),
                                      ALU.subtract).then_inc(sw_lo_done, 1)

                def normalise(t):
                    if t == 0:
                        dve.wait_ge(num_ready, h + 1)
                        link(dve.tensor_copy(den[:, :], bv[:, 0:2 * TT:2]))
                        link(dve.scalar_tensor_tensor(den[:, :], den[:, :], -1.0, den[:, :],
                                                      ALU.mult, ALU.max))
                        link(dve.tensor_tensor(den[:, :], den[:, :], e_neg_m[
                            :, :, bass.ds(h, 1)].rearrange("p a o -> p (a o)"), ALU.max))
                        link(dve.reciprocal(den[:, :], den[:, :]))
                    last = dve.tensor_scalar(hm[:, t, :], (by, bz)[t][:, :], den[:, t:t + 1], None,
                                             ALU.mult)
                    if t == 1:
                        last.then_inc(hm_done, 1)

                def output_gate():
                    dve.wait_ge(hm_done, h + 1)
                    dve.wait_ge(mo_r, h + 1)
                    dve.tensor_tensor(hm[:, :, :], hm[:, :, :], ebuf[:, :, :],
                                      ALU.mult).then_inc(ho_done, 1)

                return {0: piece_map((2, conv_inputs), *[(3 + j, lambda j=j: conv(j))
                                                         for j in range(4)],
                                     *sigmoid((conv_e, h + 1), qk_sig, conv_r, (8, 9, 10, 11)),
                                     (14, qk_lo_part)),
                        1: piece_map((0, scores),
                                     (1, lambda: staged_values(h + 2, mv_hi[:, :, :],
                                                               mv_lo[:, :, :])),
                                     (2, scores_lo),
                                     (5, lambda: normalise(0)), (6, lambda: normalise(1))),
                        2: piece_map(*sigmoid((mo_e, h + 1), ebuf, mo_r, (2, 3, 4, 5)),
                                     (6, output_gate))}

            def silu_gate(h):
                return sigmoid((mz_e, h + 1), ebuf, mz_r, (2, 3, 4, 5))

            def head_output(h):
                dve.wait_ge(mz_done, h + 1)
                for t in range(TT):
                    last = dve.scalar_tensor_tensor(mix_m[:, t, bass.ds(h * BW, BW)], hm[:, t, :],
                                                    hr[:, t:t + 1], gate_buf[:, t, :],
                                                    ALU.mult, ALU.mult)
                last.then_inc(ym_done, 1)

            def mix_lo(c):
                x_lo(PAIRS + c, gain_mix, (by, bz))

            def head(h, blocks, last={}):
                b, pieces = 4 * h + B_MLSTM, head_pieces(h)
                for c, late in last.items():
                    pieces[2].setdefault(c, []).extend(late)
                pieces[3] = piece_map(*silu_gate(h), (8, lambda: head_output(h)))
                stage_free = ((tr_done, h + (T_MQK + 1)), (v_split_lo, h + 3), (mo_e, h + 1),
                              (mz_done, h + 1))
                for n in range(blocks):
                    stream(b + n, pieces.get(n))
                    dve.wait_ge(*stage_free[n])
                    take(b + n, 1 - n % 2, stage[:, 1, :])

            with dve.Fori(0, HEADS_M - 1) as h:
                chain.enter(h, HEAD_LINKS)
                head(h, 4)
            chain.leave(HEADS_M - 1)
            head(HEADS_M - 1, 3, {c + 2: [lambda c=c: mix_lo(c)] for c in range(MIX_EARLY)})

            def add_residual(n, i, parity, turn, tiles=range(TT)):
                cols = bass.ds(n * BW, BW)
                for t in tiles:
                    if t == 0:
                        dve.wait_ge(acc0_full, n + (B_OUT + 1))
                        dve.wait_ge(xr_in[i], turn)
                    else:
                        dve.wait_ge(pe_used, n * PAIRS + ((B_OUT + 1) * PAIRS + EXTRA))
                    dve.tensor_tensor(res[:, t, cols], acc[parity][t][:, :], xres[:, i, t, :],
                                      ALU.add).then_inc((out0_free, out1_free)[t], 1)

            late = piece_map(*silu_gate(HEADS_M - 1), (8, lambda: head_output(HEADS_M - 1)))
            for c in range(PAIRS):
                if MIX_LATE <= c < MIX_LATE + PAIRS - MIX_EARLY:
                    mix_lo(MIX_EARLY + c - MIX_LATE)
                slot(B_OUT, c)
                for piece in late.get(c, ()):
                    piece()
            add_residual(0, 0, 0, 16)
            stream(B_OUT + 1)
            add_residual(1, 1, 1, 16)
            with dve.Fori(1, 3) as i:
                stream(2 * i + B_OUT)
                add_residual(2 * i, 0, 0, i * 16 + 16)
                stream(2 * i + (B_OUT + 1))
                add_residual(2 * i + 1, 1, 1, i * 16 + 16)
            stream(B_OUT + 6)
            add_residual(6, 0, 0, 64)
            for c in range(PAIRS - LOOKAHEAD):
                slot(B_OUT + 7, c)

            def final_sum(t):
                dve.wait_ge(sq_last, t + 1)
                dve.tensor_reduce(ss[:, t:t + 1], ssf[:, t, :], AX, ALU.add).then_inc(ssf_sum, 1)

            def last_columns(t):
                return dve.scalar_tensor_tensor(res[:, t, LAST:], res[:, t, LAST:], fr[:, t:t + 1],
                                                gain_f[:, LAST:], ALU.mult, ALU.mult)

            add_residual(N_OUT - 1, 1, 1, 64, [0])
            final_sum(0)
            dve.wait_ge(fr_done, 1)
            last_columns(0).then_inc(y0_last, 1)
            add_residual(N_OUT - 1, 1, 1, 64, [1])
            final_sum(1)
            dve.wait_ge(fr_done, 2)
            for i in range(4):
                cols = slice(i * Y_COLS, min((i + 1) * Y_COLS, LAST))
                last = dve.tensor_scalar(res[:, 1, cols], res[:, 1, cols], fr[:, 1:2], None,
                                         ALU.mult)
                if i == 3:
                    last = last_columns(1)
                last.then_inc(y1_done, 1)

        @block.gpsimd
        def _(pool):
            chain = Count()

            def link(ins):
                chain.n += 1
                ins.then_inc(pool_chain, 1)
                pool.wait_ge(pool_chain, chain.value())

            def rsqrt_mean(dst, src, n, power):
                link(pool.tensor_scalar(dst, src, 1.0 / n, EPS, ALU.mult, ALU.add))
                return pool.tensor_tensor(dst, dst, power, ALU.pow)

            pool.wait_ge(pre_dve, 3)
            rsqrt_mean(rstd[:, :], ss[:, :], D, m_half[:, :]).then_inc(pre_pool, 1)
            pool.memset(gate_buf[:, 0, 0:1], 0.0).then_inc(az_free, 1)
            pool.wait_ge(pre_dve, 8)
            pool.tensor_tensor(hid[:, :], hid[:, :], hid_e[:, :], ALU.mult
                               ).then_inc(pre_pool, 1)

            def group(g):
                pool.wait_ge(az_r, g + 1)
                pool.tensor_tensor(gate_buf[:, :, :], gate_buf[:, :, :], ebuf[:, :, :], ALU.mult
                                   ).then_inc(az_mul, 1)
                pool.wait_ge(az_mul, g + 1)
                pool.wait_ge(o_done, g * UNITS + UNITS)
                dst = mix_a[:, :, bass.ds(g * BW, BW)]
                pool.tensor_tensor(dst, dst, gate_buf[:, :, :], ALU.mult).then_inc(az_free, 1)

            with pool.Fori(0, GROUPS - 1) as g:
                group(g)
            group(GROUPS - 1)

            def head(h):
                pool.wait_ge(conv_r, h + 1)
                pool.tensor_tensor(qk[:, :, :], qk[:, :, :], qk_sig, ALU.mult
                                   ).then_inc(qk_done, 1)
                pool.wait_ge(ssm_done, h + 1)
                link(pool.tensor_tensor(hr[:, :], ssm[:, :], eps_m[:, :], ALU.add))
                link(pool.tensor_tensor(hr[:, :], hr[:, :], inv_m[:, :], ALU.mult))
                pool.tensor_tensor(hr[:, :], hr[:, :], m_half[:, :], ALU.pow).then_inc(hr_done, 1)
                pool.wait_ge(mz_r, h + 1)
                pool.tensor_tensor(gate_buf[:, :, :], stage[:, :, :], ebuf[:, :, :], ALU.mult
                                   ).then_inc(mz_done, 1)

            with pool.Fori(0, HEADS_M - 1) as h:
                chain.enter(h, 2)
                head(h)
            chain.leave(HEADS_M - 1)
            head(HEADS_M - 1)

            pool.wait_ge(gf_in, 16)
            with pool.Fori(0, N_OUT - 1) as n:
                pool.wait_ge(sq_done, n + 1)
                for t in range(TT):
                    dst = res[:, t, bass.ds(n * BW, BW)]
                    last = pool.tensor_tensor(dst, dst, gain_f[:, bass.ds(n * BW, BW)], ALU.mult)
                last.then_inc(gained, 1)
            for t in range(TT):
                pool.wait_ge(ssf_sum, t + 1)
                rsqrt_mean(fr[:, t:t + 1], ss[:, t:t + 1], D, m_half[:, t:t + 1]
                           ).then_inc(fr_done, 1)


GROUP_LINKS = 5 * UNITS + 1
HEAD_LINKS = 1 + 3 + 1 + 4 + 1 + 1


def shape_constants():
    s, t = np.arange(P)[:, None], np.arange(P)[None, :]
    tri = (s <= t).astype(np.float32)
    end = np.arange(N_CMP) * CMP_S + CMP_L - 1
    seen = (np.arange(T)[:, None] >= end[None, :]).astype(np.float32)
    seen = seen.reshape(TT, P, N_CMP).transpose(1, 0, 2).reshape(P, TT * N_CMP)
    const128 = np.concatenate([np.eye(P, dtype=np.float32), tri,
                               np.where(tri > 0, np.float32(0), np.float32(NEG)),
                               np.where(seen > 0, np.float32(0), np.float32(NEG)), seen], axis=1)
    n = np.arange(T)
    exact = BUCKETS // 2
    nf = np.maximum(n, exact).astype(np.float32)
    large = exact + (np.log(nf / np.float32(exact)) / np.float32(math.log(1024 / exact))
                     * np.float32(BUCKETS - exact)).astype(np.int32)
    bucket = np.where(n < exact, n, np.minimum(large, BUCKETS - 1))
    const32 = np.zeros((BUCKETS, 1024), np.float32)
    const32[bucket, 255 + n] = 1
    const32[bucket, 512 + 255 - n] = 1
    const16 = np.zeros((HEADS_A, TOE), np.float32)
    const16[:, T:] = NEG
    return const128.astype(np.float32), const32, const16


def kernel(x, norm_gain, w_in, w_conv, b_igate, b_fgate, mlstm_norm_gain,
           cmp_k_pos, cmp_k_w1, cmp_k_w2, cmp_v_pos, cmp_v_w1, cmp_v_w2,
           rel_bias, w_out, final_norm_gain):
    import concourse.bacc as bacc
    from concourse.bass_utils import run_bass_kernel_spmd

    const128, const32, const16 = shape_constants()
    arrays = dict(x=x, norm_gain=norm_gain, w_in=w_in, w_conv=w_conv, b_igate=b_igate,
                  b_fgate=b_fgate, mlstm_norm_gain=mlstm_norm_gain, cmp_k_pos=cmp_k_pos,
                  cmp_k_w1=cmp_k_w1, cmp_k_w2=cmp_k_w2, cmp_v_pos=cmp_v_pos, cmp_v_w1=cmp_v_w1,
                  cmp_v_w2=cmp_v_w2, rel_bias=rel_bias, w_out=w_out,
                  final_norm_gain=final_norm_gain, const128=const128, const32=const32,
                  const16=const16)
    nc = bacc.Bacc("TRN2", target_bir_lowering=False, num_devices=1)
    feed, args = {}, []
    for name, a in arrays.items():
        a = np.ascontiguousarray(a)
        feed[f"in_{name}"] = a
        args.append(nc.dram_tensor(f"in_{name}", a.shape, mybir.dt.from_np(a.dtype),
                                   kind="ExternalInput").ap())
    out = nc.dram_tensor("out_y", (1, T, D), F32, kind="ExternalOutput").ap()
    hybrid_layer(nc, *args, out)
    r = run_bass_kernel_spmd(nc, [feed], core_ids=[0])
    return r.results[0]["out_y"]
```
